# Optimizing a Trainium2 kernel written in Bass

```python
import jax, jax.numpy as jnp
from jax import lax
import numpy as np
import jax
import jax.numpy as jnp

D_MODEL = 1024
BATCH = 1
SEQ = 512
DEPTH = 1

N_MEM = 256
CONV_CH = D_MODEL
CONV_WIDTH = 31
N_HEADS = 8
HEAD_DIM = D_MODEL // N_HEADS
ATTN_W = N_HEADS * HEAD_DIM
IDX_HEADS = 8
IDX_DIM = 64
TOPK_MAX = 256
Q_BLOCK = 128
X_HEADS = 4
X_HEAD_DIM = 128
X_W = X_HEADS * X_HEAD_DIM
D_FF = 4 * D_MODEL
EPS = 1e-6

IN_SIZES = (CONV_CH, CONV_CH, ATTN_W, ATTN_W, ATTN_W, IDX_HEADS * IDX_DIM, IDX_DIM, IDX_HEADS, D_MODEL, D_MODEL)
IN_WIDTH = sum(IN_SIZES)


def _rmsnorm(x, g):
    x32 = x.astype(jnp.float32)
    y = x32 * lax.rsqrt(jnp.mean(x32 * x32, axis=-1, keepdims=True) + EPS)
    return y.astype(x.dtype) * g

def _layernorm(x, g, b):
    x32 = x.astype(jnp.float32)
    mu = jnp.mean(x32, axis=-1, keepdims=True)
    xc = x32 - mu
    var = jnp.mean(xc * xc, axis=-1, keepdims=True)
    return (xc * lax.rsqrt(var + EPS)).astype(x.dtype) * g + b

def _split_cols(z, sizes):
    offs = []
    acc = 0
    for s in sizes[:-1]:
        acc += s
        offs.append(acc)
    return jnp.split(z, offs, axis=-1)

def _conformer_conv(a, gate, conv_w, conv_b, ln_g, ln_b, w_out):
    u = a * jax.nn.sigmoid(gate)
    u = lax.conv_general_dilated(
        u, conv_w[:, None, :].astype(u.dtype), window_strides=(1,),
        padding=[(CONV_WIDTH - 1, 0)], dimension_numbers=('NWC', 'WIO', 'NWC'),
        feature_group_count=CONV_CH) + conv_b
    u = jax.nn.silu(_layernorm(u, ln_g, ln_b))
    return u @ w_out

def _dsa_attention(q, k, v, qi, ki, wi):
    B, L = q.shape[0], q.shape[1]
    k_top = min(TOPK_MAX, L // 4)
    nb = L // Q_BLOCK
    key_pos = jnp.arange(L)
    ki32 = ki.astype(jnp.float32)

    def to_blocks(a):
        return a.reshape((B, nb, Q_BLOCK) + a.shape[2:]).swapaxes(0, 1)

    def block(args):
        qb, qib, wb, bi = args
        q_pos = bi * Q_BLOCK + jnp.arange(Q_BLOCK)
        causal = key_pos[None, :] <= q_pos[:, None]
        logits = jnp.einsum('bqhd,bsd->bqhs', qib.astype(jnp.float32), ki32) * (IDX_DIM ** -0.5)
        score = jnp.einsum('bqh,bqhs->bqs', wb.astype(jnp.float32), jax.nn.relu(logits))
        score = jnp.where(causal[None], score, -jnp.inf)
        _, idx = lax.top_k(score, k_top)
        valid = idx <= q_pos[None, :, None]
        k_sel = jax.vmap(lambda kb, ib: kb[ib])(k, idx)
        v_sel = jax.vmap(lambda vb, ib: vb[ib])(v, idx)
        s = jnp.einsum('bqhd,bqkhd->bhqk', qb.astype(jnp.float32), k_sel.astype(jnp.float32)) * (HEAD_DIM ** -0.5)
        s = jnp.where(valid[:, None], s, -jnp.inf)
        p = jax.nn.softmax(s, axis=-1)
        return jnp.einsum('bhqk,bqkhd->bqhd', p.astype(v.dtype), v_sel)

    out = lax.map(block, (to_blocks(q), to_blocks(qi), to_blocks(wi), jnp.arange(nb)))
    return out.swapaxes(0, 1).reshape(B, L, ATTN_W)

def _cross_attention(hn, memn, wq, wkv, wo):
    B, L, _ = hn.shape
    q = (hn @ wq).reshape(B, L, X_HEADS, X_HEAD_DIM)
    kv = memn @ wkv
    k, v = jnp.split(kv, 2, axis=-1)
    k = k.reshape(B, N_MEM, X_HEADS, X_HEAD_DIM)
    v = v.reshape(B, N_MEM, X_HEADS, X_HEAD_DIM)
    s = jnp.einsum('bshd,bmhd->bhsm', q.astype(jnp.float32), k.astype(jnp.float32)) * (X_HEAD_DIM ** -0.5)
    p = jax.nn.softmax(s, axis=-1)
    o = jnp.einsum('bhsm,bmhd->bshd', p.astype(v.dtype), v).reshape(B, L, X_W)
    return o @ wo

def first_inputs(seed: int = 0) -> dict:
    key = jax.random.key(seed)
    ks = jax.random.split(key, 24)
    f32 = jnp.float32

    def w(k, shape, fan_in):
        return jax.random.normal(k, shape, f32) * (fan_in ** -0.5)

    def gain(k, shape):
        return 1.0 + 0.02 * jax.random.normal(k, shape, f32)

    def bias(k, shape):
        return 0.02 * jax.random.normal(k, shape, f32)

    return {
        "x": jax.random.normal(ks[0], (BATCH, SEQ, D_MODEL), f32),
        "mem": jax.random.normal(ks[1], (BATCH, N_MEM, D_MODEL), f32),
        "norm_mix_g": gain(ks[2], (DEPTH, D_MODEL)),
        "w_in": w(ks[3], (DEPTH, D_MODEL, IN_WIDTH), D_MODEL),
        "b_gate": bias(ks[4], (DEPTH, 2 * D_MODEL)),
        "conv_w": w(ks[5], (DEPTH, CONV_WIDTH, CONV_CH), CONV_WIDTH),
        "conv_b": bias(ks[6], (DEPTH, CONV_CH)),
        "conv_ln_g": gain(ks[7], (DEPTH, CONV_CH)),
        "conv_ln_b": bias(ks[8], (DEPTH, CONV_CH)),
        "w_conv_out": w(ks[9], (DEPTH, CONV_CH, D_MODEL), CONV_CH),
        "w_attn_out": w(ks[10], (DEPTH, ATTN_W, D_MODEL), ATTN_W),
        "w_mix_out": w(ks[11], (DEPTH, D_MODEL, D_MODEL), D_MODEL),
        "norm_x_g": gain(ks[12], (DEPTH, D_MODEL)),
        "norm_mem_g": gain(ks[13], (DEPTH, D_MODEL)),
        "wx_q": w(ks[14], (DEPTH, D_MODEL, X_W), D_MODEL),
        "wx_kv": w(ks[15], (DEPTH, D_MODEL, 2 * X_W), D_MODEL),
        "wx_o": w(ks[16], (DEPTH, X_W, D_MODEL), X_W),
        "norm_ffn_g": gain(ks[17], (DEPTH, D_MODEL)),
        "w_ff1": w(ks[18], (DEPTH, D_MODEL, D_FF), D_MODEL),
        "w_ff2": w(ks[19], (DEPTH, D_FF, D_MODEL), D_FF),
        "norm_final_g": gain(ks[20], (D_MODEL,)),
    }

def first_block(x, mem, norm_mix_g, w_in, b_gate, conv_w, conv_b, conv_ln_g, conv_ln_b,
              w_conv_out, w_attn_out, w_mix_out, norm_x_g, norm_mem_g, wx_q, wx_kv, wx_o,
              norm_ffn_g, w_ff1, w_ff2, norm_final_g):
    B, L, _ = x.shape
    h = x
    for l in range(DEPTH):
        n = _rmsnorm(h, norm_mix_g[l])
        z = n @ w_in[l]
        c_a, c_g, q, k, v, qi, ki, wi, gc_logit, ga_logit = _split_cols(z, IN_SIZES)
        bg_conv, bg_attn = jnp.split(b_gate[l], 2)
        g_conv = jax.nn.sigmoid(gc_logit + bg_conv)
        g_attn = jax.nn.sigmoid(ga_logit + bg_attn)
        y_conv = _conformer_conv(c_a, c_g, conv_w[l], conv_b[l], conv_ln_g[l], conv_ln_b[l], w_conv_out[l])
        qh = q.reshape(B, L, N_HEADS, HEAD_DIM)
        kh = k.reshape(B, L, N_HEADS, HEAD_DIM)
        vh = v.reshape(B, L, N_HEADS, HEAD_DIM)
        qih = qi.reshape(B, L, IDX_HEADS, IDX_DIM)
        wih = wi * (IDX_HEADS ** -0.5)
        y_attn = _dsa_attention(qh, kh, vh, qih, ki, wih) @ w_attn_out[l]
        h = h + (g_conv * y_conv + g_attn * y_attn) @ w_mix_out[l]
        h = h + _cross_attention(_rmsnorm(h, norm_x_g[l]), _rmsnorm(mem, norm_mem_g[l]),
                                 wx_q[l], wx_kv[l], wx_o[l])
        hf = _rmsnorm(h, norm_ffn_g[l]) @ w_ff1[l]
        h = h + jnp.square(jax.nn.relu(hf)) @ w_ff2[l]
    return _rmsnorm(h, norm_final_g)


ML_HEADS = 4
ML_QK = 64
ML_V = 128
ML_CONV = 4
ML_CHUNK = 64
MLA_HEADS = 8
MLA_NOPE = 64
MLA_ROPE = 32
MLA_V = 64
MLA_Q_RANK = 256
MLA_KV_RANK = 128
ROPE_THETA = 10000.0
D_FF_2 = 4 * D_MODEL

ML_WIDTH = ML_HEADS * ML_V
MLA_WIDTH = MLA_HEADS * MLA_V
MIX_WIDTH = ML_WIDTH + MLA_WIDTH
QK_COLS = 2 * ML_HEADS * ML_QK
GATE_COLS = 2 * ML_HEADS
IN_WIDTH_2 = QK_COLS + 2 * ML_WIDTH + GATE_COLS + MLA_Q_RANK + MLA_KV_RANK + MLA_ROPE


def rmsnorm(x, g):
    xf = x.astype(jnp.float32)
    y = xf * lax.rsqrt(jnp.mean(xf * xf, axis=-1, keepdims=True) + EPS)
    return (y * g.astype(jnp.float32)).astype(x.dtype)

def rope_tables(positions):
    inv = 1.0 / (ROPE_THETA ** (jnp.arange(0, MLA_ROPE, 2, dtype=jnp.float32) / MLA_ROPE))
    ang = positions.astype(jnp.float32)[..., None] * inv
    return jnp.cos(ang), jnp.sin(ang)

def apply_rope(x, cos, sin):
    xf = x.astype(jnp.float32)
    x1, x2 = jnp.split(xf, 2, axis=-1)
    return jnp.concatenate([x1 * cos - x2 * sin, x1 * sin + x2 * cos], axis=-1).astype(x.dtype)

def causal_conv(x, w, b):
    K = w.shape[0]
    S = x.shape[1]
    xp = jnp.pad(x, ((0, 0), (K - 1, 0), (0, 0)))
    return sum(xp[:, k:k + S] * w[k] for k in range(K)) + b

def mlstm_chunkwise(q, k, v, i_pre, f_pre):
    B, S, H, dk = q.shape
    dv = v.shape[-1]
    L = ML_CHUNK
    NC = S // L
    f32 = jnp.float32

    def chunk(t):
        t = t.reshape((B, NC, L, H) + t.shape[3:])
        return jnp.moveaxis(t, 3, 1)

    qc = chunk(q).astype(f32)
    kc = chunk(k).astype(f32) * (dk ** -0.5)
    vc = chunk(v).astype(f32)
    ig = chunk(i_pre).astype(f32)
    logf = jax.nn.log_sigmoid(chunk(f_pre).astype(f32))
    b = jnp.cumsum(logf, axis=-1)
    b_end = b[..., -1]

    a = b_end[..., None] - b + ig
    m_loc = jnp.max(a, axis=-1)
    w_loc = jnp.exp(a - m_loc[..., None])
    C_loc = jnp.einsum('bhcl,bhcld,bhcle->bhcde', w_loc, kc, vc)
    n_loc = jnp.einsum('bhcl,bhcld->bhcd', w_loc, kc)

    def step(carry, xs):
        C, n, m = carry
        Cl, nl, ml, bl = xs
        m_new = jnp.maximum(bl + m, ml)
        s_prev = jnp.exp(bl + m - m_new)
        s_loc = jnp.exp(ml - m_new)
        C_new = s_prev[..., None, None] * C + s_loc[..., None, None] * Cl
        n_new = s_prev[..., None] * n + s_loc[..., None] * nl
        return (C_new, n_new, m_new), (C, n, m)

    init = (jnp.zeros((B, H, dk, dv), f32), jnp.zeros((B, H, dk), f32), jnp.zeros((B, H), f32))
    xs = (jnp.moveaxis(C_loc, 2, 0), jnp.moveaxis(n_loc, 2, 0),
          jnp.moveaxis(m_loc, 2, 0), jnp.moveaxis(b_end, 2, 0))
    _, (C_prev, n_prev, m_prev) = lax.scan(step, init, xs)
    C_prev = jnp.moveaxis(C_prev, 0, 2)
    n_prev = jnp.moveaxis(n_prev, 0, 2)
    m_prev = jnp.moveaxis(m_prev, 0, 2)

    causal = jnp.tril(jnp.ones((L, L), dtype=bool))
    D = b[..., :, None] - b[..., None, :] + ig[..., None, :]
    D = jnp.where(causal, D, -jnp.inf)
    m_inter = b + m_prev[..., None]
    m_comb = jnp.maximum(jnp.max(D, axis=-1), m_inter)
    Dw = jnp.exp(D - m_comb[..., None])
    inter_w = jnp.exp(m_inter - m_comb)
    s = jnp.einsum('bhcid,bhcjd->bhcij', qc, kc) * Dw
    num = jnp.einsum('bhcij,bhcje->bhcie', s, vc) + inter_w[..., None] * jnp.einsum('bhcid,bhcde->bhcie', qc, C_prev)
    den = jnp.sum(s, axis=-1) + inter_w * jnp.einsum('bhcid,bhcd->bhci', qc, n_prev)
    h = num / jnp.maximum(jnp.abs(den), jnp.exp(-m_comb))[..., None]
    return jnp.moveaxis(h, 1, 3).reshape(B, S, H, dv)

def causal_block_attention(q, k, v):
    B, S, H, dq = q.shape
    dv = v.shape[-1]
    nb = S // Q_BLOCK
    scale = dq ** -0.5
    kf = k.astype(jnp.float32)
    vf = v.astype(jnp.float32)
    qb = jnp.transpose(q.reshape(B, nb, Q_BLOCK, H, dq), (1, 0, 3, 2, 4))
    kpos = jnp.arange(S)

    def one_block(args):
        qblk, bi = args
        sc = jnp.einsum('bhqd,bkhd->bhqk', qblk.astype(jnp.float32), kf) * scale
        qpos = bi * Q_BLOCK + jnp.arange(Q_BLOCK)
        sc = jnp.where(kpos[None, :] <= qpos[:, None], sc, -jnp.inf)
        p = jax.nn.softmax(sc, axis=-1)
        return jnp.einsum('bhqk,bkhd->bqhd', p, vf)

    out = lax.map(one_block, (qb, jnp.arange(nb)))
    return jnp.transpose(out, (1, 0, 2, 3, 4)).reshape(B, S, H * dv)

def token_mixer(a, cos, sin, w_in, b_gates, conv_w, conv_b, ml_head_norm,
                q_norm, w_uq, kv_norm, w_ukv, w_out):
    B, S, _ = a.shape
    proj = a @ w_in
    o0 = QK_COLS
    o1 = o0 + ML_WIDTH
    o2 = o1 + ML_WIDTH
    o3 = o2 + GATE_COLS
    o4 = o3 + MLA_Q_RANK
    o5 = o4 + MLA_KV_RANK
    qk_ml = proj[..., :o0]
    v_ml = proj[..., o0:o1]
    o_ml = proj[..., o1:o2]
    gates = proj[..., o2:o3] + b_gates
    c_q = proj[..., o3:o4]
    c_kv = proj[..., o4:o5]
    k_r = proj[..., o5:]

    qk_ml = jax.nn.silu(causal_conv(qk_ml, conv_w, conv_b))
    q_ml = qk_ml[..., :QK_COLS // 2].reshape(B, S, ML_HEADS, ML_QK)
    k_ml = qk_ml[..., QK_COLS // 2:].reshape(B, S, ML_HEADS, ML_QK)
    h_ml = mlstm_chunkwise(q_ml, k_ml, v_ml.reshape(B, S, ML_HEADS, ML_V),
                           gates[..., :ML_HEADS], gates[..., ML_HEADS:])
    h_ml = rmsnorm(h_ml, ml_head_norm.reshape(ML_HEADS, ML_V))
    h_ml = h_ml * jax.nn.sigmoid(o_ml.astype(jnp.float32)).reshape(B, S, ML_HEADS, ML_V)
    h_ml = h_ml.reshape(B, S, ML_WIDTH).astype(a.dtype)

    q = (rmsnorm(c_q, q_norm) @ w_uq).reshape(B, S, MLA_HEADS, MLA_NOPE + MLA_ROPE)
    q = jnp.concatenate([q[..., :MLA_NOPE],
                         apply_rope(q[..., MLA_NOPE:], cos[:, :, None, :], sin[:, :, None, :])], axis=-1)
    kv = (rmsnorm(c_kv, kv_norm) @ w_ukv).reshape(B, S, MLA_HEADS, MLA_NOPE + MLA_V)
    k_rope = apply_rope(k_r, cos, sin)[:, :, None, :]
    k = jnp.concatenate([kv[..., :MLA_NOPE],
                         jnp.broadcast_to(k_rope, (B, S, MLA_HEADS, MLA_ROPE))], axis=-1)
    h_mla = causal_block_attention(q, k, kv[..., MLA_NOPE:]).astype(a.dtype)

    return jnp.concatenate([h_ml, h_mla], axis=-1) @ w_out

def second_inputs(seed: int = 0) -> dict:
    key = jax.random.key(seed)
    ks = jax.random.split(key, 20)

    def nrm(k, shape, scale):
        return jax.random.normal(k, shape, jnp.float32) * scale

    def gain(k, shape):
        return 1.0 + 0.05 * jax.random.normal(k, shape, jnp.float32)

    x = nrm(ks[0], (BATCH, SEQ, D_MODEL), 1.0)
    positions = jnp.broadcast_to(jnp.arange(SEQ, dtype=jnp.int32), (BATCH, SEQ))
    b_gates = jnp.concatenate([nrm(ks[3], (DEPTH, ML_HEADS), 0.1),
                               3.0 + nrm(ks[4], (DEPTH, ML_HEADS), 0.1)], axis=-1)
    return {
        'x': x,
        'positions': positions,
        'norm_pre_mix': gain(ks[1], (DEPTH, D_MODEL)),
        'w_in': nrm(ks[2], (DEPTH, D_MODEL, IN_WIDTH_2), D_MODEL ** -0.5),
        'b_gates': b_gates,
        'conv_w': nrm(ks[5], (DEPTH, ML_CONV, QK_COLS), ML_CONV ** -0.5),
        'conv_b': nrm(ks[6], (DEPTH, QK_COLS), 0.02),
        'ml_head_norm': gain(ks[7], (DEPTH, ML_WIDTH)),
        'q_norm': gain(ks[8], (DEPTH, MLA_Q_RANK)),
        'w_uq': nrm(ks[9], (DEPTH, MLA_Q_RANK, MLA_HEADS * (MLA_NOPE + MLA_ROPE)), MLA_Q_RANK ** -0.5),
        'kv_norm': gain(ks[10], (DEPTH, MLA_KV_RANK)),
        'w_ukv': nrm(ks[11], (DEPTH, MLA_KV_RANK, MLA_HEADS * (MLA_NOPE + MLA_V)), MLA_KV_RANK ** -0.5),
        'w_out': nrm(ks[12], (DEPTH, MIX_WIDTH, D_MODEL), MIX_WIDTH ** -0.5),
        'norm_post_mix': gain(ks[13], (DEPTH, D_MODEL)),
        'norm_pre_mlp': gain(ks[14], (DEPTH, D_MODEL)),
        'w_up': nrm(ks[15], (DEPTH, D_MODEL, D_FF_2), D_MODEL ** -0.5),
        'w_down': nrm(ks[16], (DEPTH, D_FF_2, D_MODEL), D_FF_2 ** -0.5),
        'norm_post_mlp': gain(ks[17], (DEPTH, D_MODEL)),
    }

def second_block(x, positions, norm_pre_mix, w_in, b_gates, conv_w, conv_b, ml_head_norm,
              q_norm, w_uq, kv_norm, w_ukv, w_out, norm_post_mix, norm_pre_mlp,
              w_up, w_down, norm_post_mlp):
    cos, sin = rope_tables(positions)
    for l in range(DEPTH):
        a = rmsnorm(x, norm_pre_mix[l])
        mix = token_mixer(a, cos, sin, w_in[l], b_gates[l], conv_w[l], conv_b[l], ml_head_norm[l],
                          q_norm[l], w_uq[l], kv_norm[l], w_ukv[l], w_out[l])
        x = x + rmsnorm(mix, norm_post_mix[l])
        m = rmsnorm(x, norm_pre_mlp[l])
        y = jnp.square(jax.nn.relu(m @ w_up[l])) @ w_down[l]
        x = x + rmsnorm(y, norm_post_mlp[l])
    return x


def setup_inputs(seed=0):
    out = dict(first_inputs(seed))
    for name, value in second_inputs(seed + 1).items():
        if name != "x":
            out[name + "_2"] = value
    return out


def reference(
    x, mem, norm_mix_g, w_in, b_gate, conv_w, conv_b, conv_ln_g, conv_ln_b, w_conv_out,
    w_attn_out, w_mix_out, norm_x_g, norm_mem_g, wx_q, wx_kv, wx_o, norm_ffn_g, w_ff1, w_ff2,
    norm_final_g, positions_2, norm_pre_mix_2, w_in_2, b_gates_2, conv_w_2, conv_b_2,
    ml_head_norm_2, q_norm_2, w_uq_2, kv_norm_2, w_ukv_2, w_out_2, norm_post_mix_2,
    norm_pre_mlp_2, w_up_2, w_down_2, norm_post_mlp_2,
):
    x = first_block(
        x, mem, norm_mix_g, w_in, b_gate, conv_w, conv_b, conv_ln_g, conv_ln_b, w_conv_out,
        w_attn_out, w_mix_out, norm_x_g, norm_mem_g, wx_q, wx_kv, wx_o, norm_ffn_g, w_ff1,
        w_ff2, norm_final_g,
    )
    return second_block(
        x, positions_2, norm_pre_mix_2, w_in_2, b_gates_2, conv_w_2, conv_b_2, ml_head_norm_2,
        q_norm_2, w_uq_2, kv_norm_2, w_ukv_2, w_out_2, norm_post_mix_2, norm_pre_mlp_2, w_up_2,
        w_down_2, norm_post_mlp_2,
    )


_drawn_inputs = setup_inputs


def setup_inputs(seed=0):
    import zlib

    import numpy as np

    out = dict(_drawn_inputs(seed))
    spreads = {}
    factors = {'norm_mix_g': 3.359,
     'b_gate': 8.0,
     'conv_ln_g': 5.128,
     'conv_ln_b': 5.342,
     'norm_x_g': 8.0,
     'norm_mem_g': 8.0,
     'conv_b_2': 15.195,
     'q_norm_2': 7.379,
     'kv_norm_2': 2.695,
     'norm_ffn_g': 4.187,
     'ml_head_norm_2': 7.511}
    for name, (base, spread) in spreads.items():
        noise = np.random.default_rng([zlib.crc32(name.encode()), seed]).standard_normal(out[name].shape)
        drawn = base * np.exp(spread * noise) if base else spread * noise
        out[name] = jnp.asarray(drawn.astype(out[name].dtype))
    for name, factor in factors.items():
        out[name] = (out[name] * factor).astype(out[name].dtype)
    return out
```

```python
from contextlib import ExitStack

import numpy as np

import concourse.bass as bass
from concourse import mybir

ALU = mybir.AluOpType
ACT = mybir.ActivationFunctionType
AX = mybir.AxisListType
F32 = mybir.dt.float32
F32R = mybir.dt.float32r
I32 = mybir.dt.int32

P = 128
D = 1024
KB = D // P
T = 512
TB = T // P
M = 256
MB = M // P
EPS = 1e-6
TAPS = 31
PAD = TAPS - 1
HEADS = 8
IDX_HEADS = 8
IDX_DIM = 64
TOPK = 128
XH = 4
ML_HEADS = 4
ML_QK = 64
ML_V = 128
ML_TAPS = 4
MLA_HEADS = 8
NOPE = 64
ROPE = 32
MLA_V = 64
FF_GROUPS = 4
RING = 4
AHEAD = 3
MASKED = -3.0e38
TAKEN = -3.4e38
TAKEN_BELOW = -3.2e38

STAGES = [("MK", 4), ("MV", 4), ("QI", 4), ("KI", 1), ("C", 16), ("G", 16), ("V", 8), ("ATT", 16),
          ("CO", 8), ("AO", 8), ("MX", 8), ("QX", 4), ("OX", 4), ("FF1", 64), ("CQ", 2), ("CKV", 1),
          ("KR", 1), ("QK", 4), ("VM", 4), ("OM", 4), ("UQ", 2), ("UKV", 1), ("WO", 8), ("FF2", 64)]
CH = {}
_n = 0
for _name, _count in STAGES:
    CH[_name] = _n
    _n += _count
CHUNKS = _n
OUTS = [("MK", 4), ("MV", 2), ("QI", 4), ("KI", 1), ("C", 16), ("G", 16), ("V", 8), ("ATT", 16),
        ("CO", 8), ("AO", 8), ("MX", 8), ("QX", 4), ("OX", 8), ("FF1", 64), ("CQ", 2), ("CKV", 1),
        ("KR", 1), ("QK", 4), ("VM", 4), ("OM", 4), ("UQ", 8), ("UKV", 8), ("WO", 8), ("FF2", 64)]
O = {}
_n = 0
for _name, _count in OUTS:
    O[_name] = _n
    _n += _count
DVE_FROM = O["CO"]

COLS = [("norm_mix_g", 8), ("b_gate", 16), ("conv_w", KB * TAPS), ("conv_b", 8), ("conv_ln_g", 8),
        ("conv_ln_b", 8), ("norm_x_g", 8), ("norm_mem_g", 8), ("norm_ffn_g", 8), ("norm_final_g", 8),
        ("norm_pre_mix_2", 8), ("conv_w_2", 4 * ML_TAPS), ("conv_b_2", 4), ("ml_head_norm_2", 4),
        ("q_norm_2", 2), ("kv_norm_2", 1), ("norm_post_mix_2", 8), ("norm_pre_mlp_2", 8),
        ("norm_post_mlp_2", 8), ("b_gates_2", 2)]
COL = {}
_n = 0
for _name, _count in COLS:
    COL[_name] = _n
    _n += _count
NCOLS = _n
CONSTS = [("ident", P), ("ones", P), ("bias", T), ("maskT", P), ("misc", 8)]
CON = {}
_n = 0
for _name, _count in CONSTS:
    CON[_name] = _n
    _n += _count
NCONST = _n
EPS_COL, INV_COL, SIGN_COL, ONE_COL = 0, 1, 2, 3
TWO_PI = float(2 * np.pi)
PI_SAFE = float(np.nextafter(np.float32(np.pi), np.float32(0)))
PI_HI = 6.28125
PI_MID = float(np.float32(np.floor((TWO_PI - PI_HI) * 2.0 ** 21) / 2.0 ** 21))
PI_LO = float(np.float32(TWO_PI - PI_HI - PI_MID))
ROUND = 12582912.0


SEMAPHORES = """
angles centred cn_hi_done cn_ready cn_scaled conv_done convact_ready cq_squared f_hi f_ready f_sq
gains_ready gate_step gated gates_done gates_turned gcols_done hg_hi hg_ready kr_moved kv_keys_done
late_landed ln_hi ln_inv ln_root ln_scaled ln_silu ln_squared ln_sum logits_ready mean2 mix_added
mix_hi mix_ready ml_abs ml_conv ml_decay ml_diag ml_fl ml_floor ml_gated ml_hi ml_inv ml_normed
ml_num ml_out ml_ready ml_root ml_rows ml_s ml_sT ml_sq ml_sum norm2 o_gated o_hi o_ready ox_first
pT_copied pT_ready p_inv p_ready p_scaled pad_zeroed post_added post_scaled pv_done q_moved qk_pad
qk_silu relu_ready res_sq res_sqg rope_done rope_half rope_q row_step rstd_ready rt_cols rt_done
rt_turned s_masked s_negmax s_ready score_added score_masked sines squares ssq_added ssqg_added
start_hi start_ready start_scaled stat_ready stat_root tap_done topk_done topk_step wi_copied
wi_turned x2_done y_scaled y_written y_zeroed
"""
LN_SQ_AT, LN_VAR_AT, LN_SILU_AT = 5, 10, 17


def program(nc, stream, xT, memT, cols_in, consts_in, sel_in, pos_in, out):
    with ExitStack() as ctx:
        def sem(name):
            return ctx.enter_context(nc.semaphore(name))

        def at(name, shape, offset, dt=F32):
            return nc.alloc_sbuf_tensor_at(name, shape, dt, offset=offset)

        W0, A0, B0, C0 = 2048, 34816, 67584, 101376
        G0, H0, QK0, BIAS0, KX0, TMP0, CON0 = 134144, 166912, 183296, 191488, 199680, 207872, 220160
        w_hi = at("w_hi", [P, RING, 1024], W0, F32R)
        w_raw = at("w_raw", [P, RING, 1024], W0 + 16384)
        w_lo = at("w_lo", [P, RING, 1024], W0 + 16384, F32R)
        a_hi = at("a_hi", [P, KB, T], A0, F32R)
        a_lo = at("a_lo", [P, KB, T], A0 + 16384, F32R)
        b_hi = at("b_hi", [P, KB, T], B0, F32R)
        b_lo = at("b_lo", [P, KB, T], B0 + 17408, F32R)
        c_hi = at("c_hi", [P, KB, T], C0, F32R)
        c_lo = at("c_lo", [P, KB, T], C0 + 16384, F32R)
        conv_in = at("conv_in", [P, KB, PAD + T], B0)
        conv_io = at("conv_io", [P, KB, T], B0 + 17408)
        gate_c = at("gate_c", [P, KB, T], G0)
        gate_a = at("gate_a", [P, KB, T], G0 + 16384)
        res = at("res", [P, KB, T], H0)
        values = at("values", [P, TB, D], H0)
        qT = at("qT", [P, 2, T], QK0)
        kT = at("kT", [P, 2, T], QK0 + 4096)
        rstd = at("rstd", [P, T], QK0)
        ssq = at("ssq", [P, T], QK0 + 2048)
        sq = at("sq", [P, 2, T], QK0 + 4096)
        bias = at("bias", [P, TB, T], BIAS0)
        kxT = at("kxT", [P, XH, M], KX0)
        vx = at("vx", [P, MB, XH * P], KX0 + 4096)
        masked = at("masked", [P, 2, T], TMP0)
        probs = at("probs", [P, 2, T], TMP0 + 4096)
        probsT = at("probsT", [P, 2, T], TMP0 + 8192)
        cols = at("cols", [P, NCOLS], CON0)
        consts = at("consts", [P, NCONST], CON0 + 1792)
        small0 = CON0 + 1792 + NCONST * 4
        top8 = at("top8", [P, 3, 8], small0)
        wiT = at("wiT", [P, TB, IDX_HEADS], small0 + 96)
        rowmax = at("rowmax", [P, 2], small0 + 224)
        negmax = at("negmax", [P, 2], small0 + 256)
        rowsum = at("rowsum", [P, 2], small0 + 288)
        rowinv = at("rowinv", [P, 2], small0 + 320)
        g2g = at("g2g", [P, KB], small0 + 352)
        gcols = at("gcols", [P, TB, ML_HEADS], small0 + 384)
        rtcol = at("rtcol", [P, TB], small0 + 448)
        mem_raw = at("mem_raw", [P, KB, M], G0)
        mem_sq = at("mem_sq", [P, KB, M], G0 + 8192)
        mem_hi = at("mem_hi", [P, KB, M], G0 + 16384, F32R)
        mem_lo = at("mem_lo", [P, KB, M], G0 + 24576, F32R)
        mem_rstd = at("mem_rstd", [P, M], C0 + 28672)
        x_sq = at("x_sq", [P, KB, T], C0)
        x_rstd = at("x_rstd", [P, T], QK0)
        qiT = at("qiT", [P, IDX_HEADS // 2, T], C0 + 16384)
        kiT = at("kiT", [P, T], C0 + 24576)
        wi_rows = at("wi_rows", [P, T], C0 + 26624)
        relu = at("relu", [P, 2, T], TMP0)
        score = bias
        ln_rstd = at("ln_rstd", [P, T], small0 + 480)
        ln_sq = at("ln_sq", [P, KB, T], B0)
        qxT = at("qxT", [P, XH, T], G0)
        xo_hi = at("xo_hi", [P, XH, T], C0, F32R)
        xo_lo = at("xo_lo", [P, XH, T], C0 + 16384, F32R)
        ff_t = at("ff_t", [P, 2, T], TMP0)
        ff_f = at("ff_f", [P, 2, T], TMP0 + 4096)
        ssq_g = at("ssq_g", [P, T], TMP0 + 8192)
        sq_g = at("sq_g", [P, T], TMP0 + 10240)
        cq_sq = at("cq_sq", [P, 3, T], TMP0)
        cq_rstd = at("cq_rstd", [P, 2, T], TMP0 + 6144)
        cq = at("cq", [P, 3, T], C0)
        cn_hi = at("cn_hi", [P, 3, T], TMP0, F32R)
        cn_lo = at("cn_lo", [P, 3, T], C0 + 24576, F32R)
        ogate = at("ogate", [P, ML_HEADS, T], C0 + 16384)
        qk_in = at("qk_in", [P, 4, ML_TAPS - 1 + T], G0)
        qk_ml = at("qk_ml", [P, 4, T], G0 + 8256)
        v_ml = at("v_ml", [P, TB, ML_HEADS * ML_V], G0 + 16448)
        v_mla = at("v_mla", [P, TB, MLA_HEADS * MLA_V], G0)
        qh = at("qh", [P, MLA_HEADS, T], BIAS0)
        kh = at("kh", [P, MLA_HEADS, T], C0)
        gt = at("gt", [P, 6, T], B0)
        ropet = at("ropet", [P, 5, T], B0 + 12288)
        rot = at("rot", [P, 2, T], B0 + 22528)
        krT = at("krT", [P, T], B0 + 26624)
        sel = at("sel", [P, ML_HEADS * P], B0 + 28672)
        posi = at("posi", [P, T], B0 + 30720, I32)
        ml_square = at("ml_square", [P, T], TMP0)
        negm_diag = at("negm_diag", [P, TB, P], TMP0 + 2048)
        decay = at("decay", [P, 2, T], TMP0 + 4096)
        sT = at("sT", [P, 2, T], TMP0 + 8192)
        den = at("den", [P, T], QK0)
        floor_ = at("floor_", [P, T], QK0 + 2048)
        hml = at("hml", [P, 2, T], QK0 + 4096)
        mixed = at("mixed", [P, KB, T], C0)
        ffy = at("ffy", [P, KB, T], C0 + 16384)
        y_out = at("y_out", [P, KB, T], G0)

        def col(name, i=0, n=1, p0=0, p1=P):
            return cols[p0:p1, COL[name] + i:COL[name] + i + n]

        def con(name, n, i=0, p0=0, p1=P):
            return consts[p0:p1, CON[name] + i:CON[name] + i + n]

        ident = con("ident", P)
        ones = con("ones", P)
        eps = con("misc", 1, EPS_COL)

        ps = [ctx.enter_context(nc.psum_tensor(f"bank{i}", [P, 512], F32)) for i in range(8)]
        STAT = 4

        raw_landed = [sem(f"raw_landed{i}") for i in range(RING)]
        w_hi_done = sem("w_hi_done")
        w_lo_done = sem("w_lo_done")
        chunk_done = sem("chunk_done")
        evac_act = sem("evac_act")
        evac_dve = sem("evac_dve")
        consts_landed = sem("consts_landed")
        mem_landed = sem("mem_landed")
        x_landed = sem("x_landed")
        x_again = sem("x_landed_again")
        out_landed = sem("out_landed")
        sems = {n: sem(n) for n in SEMAPHORES.split()}
        block = ctx.enter_context(nc.Block())

        def w_slot(t, slot, k, n=P):
            return t[:, slot, k * n:(k + 1) * n]

        DSA_G, X_G, MLA_G = 0, HEADS, HEADS + XH

        def keys_of(G, qb):
            return M if X_G <= G < MLA_G else (qb + 1) * P

        def scale_of(G):
            if G < MLA_G:
                return float(P) ** -0.5
            return float(NOPE + ROPE) ** -0.5

        def bias_of(G, qb):
            n = keys_of(G, qb)
            if G < X_G and qb > 0:
                return bias[:, qb, 0:n]
            if G < X_G or G >= MLA_G:
                return con("bias", n, T - n)
            return con("bias", n, 0)

        def out_of(G):
            if G < X_G:
                return ps[2][:, :], c_hi[:, G, :], c_lo[:, G, :]
            if G < MLA_G:
                return ps[2][:, :], xo_hi[:, G - X_G, :], xo_lo[:, G - X_G, :]
            h = G - MLA_G
            r = slice(MLA_V * (h % 2), MLA_V * (h % 2) + MLA_V)
            return ps[2][r, :], a_hi[r, ML_HEADS + h // 2, :], a_lo[r, ML_HEADS + h // 2, :]

        @block.sync
        def _(sp):
            sp.dma_start(mem_raw[:, :, :], memT).then_inc(mem_landed, 16)
            for j in range(RING):
                sp.dma_start(w_raw[:, j, :], stream[j]).then_inc(raw_landed[j], 16)
            with sp.Fori(1, CHUNKS // RING) as i:
                for j in range(RING):
                    sp.wait_ge(chunk_done, RING * i + j - (RING - 1))
                    sp.dma_start(w_raw[:, j, :],
                                 stream[bass.ds(RING * i + j, 1), :, :].rearrange("o p n -> (o p) n")
                                 ).then_inc(raw_landed[j], 16)
            for i in range(KB):
                sp.wait_ge(sems["y_written"], i + 1)
                sp.dma_start(out[:, i, :], y_out[:, i, :]).then_inc(out_landed, 16)
            sp.wait_ge(out_landed, 16 * KB)

        @block.gpsimd
        def _(pool):
            nc.gpsimd.memset(conv_in[:, :, 0:PAD], 0.0).then_inc(sems["pad_zeroed"], 1)
            with pool.Fori(0, CHUNKS // RING) as i:
                for j in range(RING):
                    pool.wait_ge(w_hi_done, RING * i + j + 1)
                    nc.gpsimd.tensor_tensor(w_lo[:, j, :], w_raw[:, j, :], w_hi[:, j, :].bitcast(F32),
                                            ALU.subtract).then_inc(w_lo_done, 1)

        @block.tensor
        def _(pe):
            def mm(o, l, r, start=True, stop=True):
                return nc.tensor.matmul(o, l, r, start=start, stop=stop)

            def three(o, wh, wl, xh, xl, start, stop):
                mm(o, wh, xh, start, False)
                mm(o, wh, xl, False, False)
                return mm(o, wl, xh, False, stop)

            def bank_free(o, first=None):
                if (o if first is None else first) >= DVE_FROM + RING:
                    pe.wait_ge(evac_dve, o - RING + 1 - DVE_FROM)
                elif first is not None or RING <= o <= DVE_FROM:
                    pe.wait_ge(evac_act, o - RING + 1)

            def chunk(c, slot, o, bank, hi, lo, width=T, ready=None, base=0, first=None):
                pe.wait_ge(w_lo_done, c + 1)
                if o is not None:
                    bank_free(o, first)
                for k in range(KB):
                    if ready is not None:
                        pe.wait_ge(ready, base + k + 1)
                    m = three(ps[bank][:, 0:width], w_slot(w_hi, slot, k), w_slot(w_lo, slot, k),
                              hi[:, k, 0:width], lo[:, k, 0:width], k == 0, k == KB - 1)
                m.then_inc(chunk_done, 1)

            def stage(name, n, hi, lo, width=T, ready=None, base=0):
                c0, o0 = CH[name], O[name]
                if n <= RING:
                    for j in range(n):
                        chunk(c0 + j, (c0 + j) % RING, o0 + j, (o0 + j) % RING, hi, lo, width,
                              ready if j == 0 else None, base)
                    return
                with pe.Fori(0, n // RING) as i:
                    for j in range(RING):
                        chunk(RING * i + c0 + j, (c0 + j) % RING, RING * i + (o0 + j), (o0 + j) % RING,
                              hi, lo, width, ready if j == 0 else None, base, first=o0 + j)

            def token_major(c0, o0, blocks, hi, lo, ready=None, base=0):
                for t in range(RING):
                    slot = (c0 + t) % RING
                    pe.wait_ge(w_lo_done, c0 + t + 1)
                    for b in range(blocks):
                        if t == 0:
                            bank_free(o0 + b)
                        for kk in range(2):
                            k = 2 * t + kk
                            if ready is not None and b == 0:
                                pe.wait_ge(ready, base + k + 1)
                            o = ps[(o0 + b) % RING][:, :]
                            xh, xl = hi[:, k, b * P:(b + 1) * P], lo[:, k, b * P:(b + 1) * P]
                            wh, wl = w_slot(w_hi, slot, kk, T), w_slot(w_lo, slot, kk, T)
                            mm(o, xh, wh, k == 0, False)
                            mm(o, xh, wl, False, False)
                            m = mm(o, xl, wh, False, k == KB - 1)
                    m.then_inc(chunk_done, 1)

            def stat(n, bank, parts, width=T):
                for k, (s, v, part) in enumerate(parts):
                    if s is not None:
                        pe.wait_ge(s, v)
                    m = mm(ps[bank][:, 0:width], ones, part, k == 0, k == len(parts) - 1)
                m.then_inc(sems["stat_ready"], 1)

            def attend(G0, n_heads, score, value, hook=None):
                n_units = 4 * n_heads

                def scores(n):
                    U, G, qb = 4 * G0 + n, G0 + n // 4, n % 4
                    if U >= 2:
                        pe.wait_ge(sems["s_masked"], U - 1)
                    score(G, qb, ps[4 + U % 2][:, 0:keys_of(G, qb)]).then_inc(sems["s_ready"], 1)

                def turn(n):
                    U, G, qb = 4 * G0 + n, G0 + n // 4, n % 4
                    pe.wait_ge(sems["p_scaled"], U + 1)
                    if U >= 2:
                        pe.wait_ge(sems["pT_copied"], U - 1)
                    for kb in range(keys_of(G, qb) // P):
                        r = slice(kb * P, (kb + 1) * P)
                        m = nc.tensor.transpose(ps[6 + U % 2][:, r], probs[:, U % 2, r], ident)
                    m.then_inc(sems["pT_ready"], 1)

                def values_out(n):
                    U, G, qb = 4 * G0 + n, G0 + n // 4, n % 4
                    pe.wait_ge(sems["pT_copied"], U + 1)
                    if qb == 0 and G > 0:
                        pe.wait_ge(sems["o_ready"], G)
                    nk = keys_of(G, qb) // P
                    for kb in range(nk):
                        m = mm(out_of(G)[0][:, qb * P:(qb + 1) * P], value(G, kb),
                               probsT[:, U % 2, kb * P:(kb + 1) * P], kb == 0, kb == nk - 1)
                    m.then_inc(sems["pv_done"], 1)

                scores(0)
                scores(1)
                for n in range(n_units):
                    if hook is not None:
                        hook(n)
                    turn(n)
                    if n + 2 < n_units:
                        scores(n + 2)
                    if n >= 1:
                        values_out(n - 1)
                values_out(n_units - 1)

            pe.wait_ge(consts_landed, 32)
            stat(0, 4, [(sems["squares"], 1, mem_sq[:, k, :]) for k in range(KB)], M)
            stat(1, 5, [(sems["squares"], 2 + k // 2, x_sq[:, k, :]) for k in range(KB)])
            stage("MK", 4, mem_hi, mem_lo, M, sems["start_ready"], 0)
            token_major(CH["MV"], O["MV"], MB, mem_hi, mem_lo)
            stage("QI", 4, a_hi, a_lo, T, sems["start_ready"], KB)
            stage("KI", 1, a_hi, a_lo)
            pe.wait_ge(evac_act, O["KI"] + 1)
            pe.wait_ge(sems["stat_root"], 2)
            for tb in range(TB):
                m = nc.tensor.transpose(ps[5][:, tb * IDX_HEADS:(tb + 1) * IDX_HEADS],
                                        wi_rows[0:IDX_HEADS, tb * P:(tb + 1) * P],
                                        ident[0:IDX_HEADS, 0:IDX_HEADS])
            m.then_inc(sems["wi_turned"], 1)
            for n in range(3 * IDX_HEADS):
                qb, h = 1 + n // IDX_HEADS, n % IDX_HEADS
                r = slice(IDX_DIM * (h % 2), IDX_DIM * (h % 2) + IDX_DIM)
                if n >= 2:
                    pe.wait_ge(sems["relu_ready"], n - 1)
                mm(ps[6 + n % 2][:, 0:(qb + 1) * P], qiT[r, h // 2, qb * P:(qb + 1) * P],
                   kiT[r, 0:(qb + 1) * P]).then_inc(sems["logits_ready"], 1)
            stage("C", 16, a_hi, a_lo)
            stage("G", 16, a_hi, a_lo)
            for half in range(2):
                token_major(CH["V"] + 4 * half, O["V"] + 4 * half, TB, a_hi, a_lo)

            def qk_chunk(n):
                c, o = CH["ATT"] + n, O["ATT"] + n
                pe.wait_ge(evac_act, o - 1 if n >= 2 else O["ATT"])
                chunk(c, c % RING, None, n % 2, a_hi, a_lo)

            def dsa_score(G, qb, o):
                pe.wait_ge(evac_act, O["ATT"] + 2 * G + 2)
                return mm(o, qT[:, G % 2, qb * P:(qb + 1) * P], kT[:, G % 2, 0:(qb + 1) * P])

            def dsa_hook(n):
                h = n // 4
                if n % 4 < 2 and h + 1 < HEADS:
                    qk_chunk(2 * (h + 1) + n % 4)
                if n == LN_VAR_AT:
                    for k in range(KB):
                        pe.wait_ge(sems["ln_squared"], k + 1)
                        m = mm(ps[3][:, :], ones, ln_sq[:, k, :], k == 0, k == KB - 1)
                    m.then_inc(sems["ln_sum"], 1)

            qk_chunk(0)
            qk_chunk(1)
            pe.wait_ge(evac_act, O["ATT"])
            for k in range(KB):
                pe.wait_ge(sems["conv_done"], k + 1)
                m = mm(ps[3][:, :], ones, conv_io[:, k, :], k == 0, k == KB - 1)
            m.then_inc(sems["ln_sum"], 1)
            attend(DSA_G, HEADS, dsa_score,
                   lambda G, kb: values[:, kb, G * P:(G + 1) * P], dsa_hook)
            pe.wait_ge(evac_act, DVE_FROM)
            pe.wait_ge(sems["o_ready"], HEADS)
            pe.wait_ge(sems["ln_root"], 1)
            for j in range(KB):
                chunk(CH["CO"] + j, (CH["CO"] + j) % RING, O["CO"] + j, (O["CO"] + j) % RING, b_hi, b_lo,
                      ready=sems["convact_ready"] if j == 0 else None)
            stage("AO", KB, c_hi, c_lo, ready=sems["o_ready"])
            stage("MX", KB, a_hi, a_lo, ready=sems["mix_ready"])
            stage("QX", XH, b_hi, b_lo, ready=sems["hg_ready"], base=0)
            stat(2, STAT, [(sems["ssq_added"], KB, ssq[:, :])])

            def x_score(G, qb, o):
                h = G - X_G
                pe.wait_ge(evac_dve, O["QX"] + h + 1 - DVE_FROM)
                if h == 0 and qb < 2:
                    pe.wait_ge(sems["stat_root"], 3)
                return mm(o, qxT[:, h, qb * P:(qb + 1) * P], kxT[:, h, :])

            attend(X_G, XH, x_score, lambda G, kb: vx[:, kb, (G - X_G) * P:(G - X_G + 1) * P])
            for j in range(XH):
                c = CH["OX"] + j
                pe.wait_ge(w_lo_done, c + 1)
                for r in range(2):
                    o = O["OX"] + 2 * j + r
                    bank_free(o)
                    for k in range(XH):
                        if j == 0 and r == 0:
                            pe.wait_ge(sems["o_ready"], X_G + k + 1)
                        m = three(ps[o % RING][:, :], w_slot(w_hi, c % RING, r * XH + k),
                                  w_slot(w_lo, c % RING, r * XH + k), xo_hi[:, k, :], xo_lo[:, k, :],
                                  k == 0, k == XH - 1)
                    if r == 0:
                        m.then_inc(sems["ox_first"], 1)
                m.then_inc(chunk_done, 1)

            def feed_forward(name, s, hset):
                c0, o0 = CH[name], O[name]
                with pe.Fori(0, FF_GROUPS) as g:
                    for j in range(KB):
                        chunk(g * 16 + (c0 + j), (c0 + j) % RING, g * 16 + (o0 + j), (o0 + j) % RING,
                              a_hi, a_lo, T, sems["hg_ready"] if j == 0 else None, KB * hset, first=o0 + j)
                    for j in range(KB, 2 * KB):
                        chunk(g * 16 + (c0 + j), (c0 + j) % RING, g * 16 + (o0 + j), (o0 + j) % RING,
                              b_hi, b_lo, T, sems["f_ready"] if j == KB else None, g * KB + 32 * s,
                              first=o0 + j)

            pe.wait_ge(sems["pv_done"], 4 * MLA_G)
            stat(3, STAT, [(sems["ssq_added"], 2 * KB, ssq[:, :])])
            feed_forward("FF1", 0, 1)
            stage("CQ", 2, a_hi, a_lo, ready=sems["hg_ready"], base=2 * KB)
            stat(4, STAT, [(sems["ssq_added"], 3 * KB, ssq[:, :])])
            stat(5, 5, [(sems["ssqg_added"], KB, ssq_g[:, :])])
            stage("CKV", 1, a_hi, a_lo)
            stage("KR", 1, a_hi, a_lo)
            pe.wait_ge(sems["rt_done"], 1)
            for tb in range(TB):
                m = nc.tensor.transpose(ps[6][:, tb * P:(tb + 1) * P], ssq[:, tb * P:(tb + 1) * P], ident)
            m.then_inc(sems["rt_turned"], 1)
            stage("QK", 4, a_hi, a_lo)
            token_major(CH["VM"], O["VM"], TB, a_hi, a_lo)
            stage("OM", 4, a_hi, a_lo)
            stat(6, STAT, [(sems["cq_squared"], k + 1, cq_sq[:, k, :]) for k in range(2)])
            stat(7, 5, [(sems["cq_squared"], 3, cq_sq[:, 2, :])])
            pe.wait_ge(sems["gates_done"], 1)
            for tb in range(TB):
                m = nc.tensor.transpose(ps[7][:, tb * ML_HEADS:(tb + 1) * ML_HEADS],
                                        gt[0:ML_HEADS, 0, tb * P:(tb + 1) * P],
                                        ident[0:ML_HEADS, 0:ML_HEADS])
            m.then_inc(sems["gates_turned"], 1)
            for t in range(2):
                c = CH["UQ"] + t
                pe.wait_ge(w_lo_done, c + 1)
                for j in range(4):
                    o = O["UQ"] + 4 * t + j
                    bank_free(o)
                    for k in range(2):
                        if t == 0 and j == 0:
                            pe.wait_ge(sems["cn_ready"], k + 1)
                        m = three(ps[o % RING][:, :], w_slot(w_hi, c % RING, 2 * j + k),
                                  w_slot(w_lo, c % RING, 2 * j + k), cn_hi[:, k, :], cn_lo[:, k, :],
                                  k == 0, k == 1)
                m.then_inc(chunk_done, 1)
            c = CH["UKV"]
            pe.wait_ge(w_lo_done, c + 1)
            pe.wait_ge(sems["cn_ready"], 3)
            for j in range(4):
                o = O["UKV"] + j
                bank_free(o)
                m = three(ps[o % RING][:, :], w_slot(w_hi, c % RING, j), w_slot(w_lo, c % RING, j),
                          cn_hi[:, 2, :], cn_lo[:, 2, :], True, True)
            m.then_inc(sems["kv_keys_done"], 1)
            for j in range(TB):
                o = O["UKV"] + 4 + j
                bank_free(o)
                xh, xl = cn_hi[:, 2, j * P:(j + 1) * P], cn_lo[:, 2, j * P:(j + 1) * P]
                wh, wl = w_slot(w_hi, c % RING, 1, T), w_slot(w_lo, c % RING, 1, T)
                m = three(ps[o % RING][:, :], xh, xl, wh, wl, True, True)
            m.then_inc(chunk_done, 1)
            pe.wait_ge(evac_dve, O["WO"] - DVE_FROM)
            pe.wait_ge(sems["gcols_done"], 1)
            pe.wait_ge(sems["rstd_ready"], 8)
            pe.wait_ge(sems["late_landed"], 32)
            pe.wait_ge(sems["qk_silu"], 4)
            for h in range(ML_HEADS):
                r = slice(ML_QK * (h % 2), ML_QK * (h % 2) + ML_QK)
                num, dn = ps[2 * (h % 2)], ps[2 * (h % 2) + 1]
                if h >= 1:
                    pe.wait_ge(sems["ml_sT"], 4 * h)
                    pe.wait_ge(sems["ml_root"], h)
                mm(ps[4][:, :], sel[0:ML_HEADS, h * P:(h + 1) * P], gt[0:ML_HEADS, 4, :])
                mm(ps[5][:, :], sel[0:ML_HEADS, h * P:(h + 1) * P], gt[0:ML_HEADS, 3, :]
                   ).then_inc(sems["ml_rows"], 1)

                def ml_scores(jb):
                    u = 4 * h + jb
                    if u >= 2:
                        pe.wait_ge(sems["ml_sT"], u - 1)
                    mm(ps[6 + u % 2][:, 0:T - jb * P], qk_ml[r, 2 + h // 2, jb * P:(jb + 1) * P],
                       qk_ml[r, h // 2, jb * P:T]).then_inc(sems["ml_s"], 1)

                ml_scores(0)
                ml_scores(1)
                for jb in range(TB):
                    u = 4 * h + jb
                    pe.wait_ge(sems["ml_sT"], u + 1)
                    if jb == 0 and h >= 2:
                        pe.wait_ge(sems["ml_num"], h - 1)
                    part = sT[:, u % 2, 0:T - jb * P]
                    mm(num[:, jb * P:T], v_ml[:, jb, h * ML_V:(h + 1) * ML_V], part, jb == 0, jb == TB - 1)
                    mm(dn[:, jb * P:T], ones, part, jb == 0, jb == TB - 1).then_inc(sems["ml_out"], 1)
                    if jb + 2 < TB:
                        ml_scores(jb + 2)
                pe.wait_ge(sems["ml_sq"], h + 1)
                mm(ps[5][:, :], ones, ml_square[:, :]).then_inc(sems["ml_sum"], 1)
            pe.wait_ge(sems["ml_root"], ML_HEADS)

            def mla_score(G, qb, o):
                h = G - MLA_G
                if h == 0 and qb == 0:
                    pe.wait_ge(sems["rope_done"], MLA_HEADS)
                    pe.wait_ge(sems["ml_sT"], 4 * ML_HEADS)
                return mm(o, qh[0:NOPE + ROPE, h, qb * P:(qb + 1) * P], kh[0:NOPE + ROPE, h, 0:(qb + 1) * P])

            pe.wait_ge(sems["ml_ready"], ML_HEADS)
            attend(MLA_G, MLA_HEADS, mla_score,
                   lambda G, kb: v_mla[:, kb, (G - MLA_G) * MLA_V:(G - MLA_G + 1) * MLA_V])
            for j in range(KB):
                c, o = CH["WO"] + j, O["WO"] + j
                pe.wait_ge(w_lo_done, c + 1)
                if j == 0:
                    pe.wait_ge(sems["o_ready"], MLA_G + MLA_HEADS)
                bank_free(o)
                for k in range(KB):
                    m = three(ps[o % RING][:, :], w_slot(w_hi, c % RING, k), w_slot(w_lo, c % RING, k),
                              a_hi[:, k, :], a_lo[:, k, :], k == 0, k == KB - 1)
                m.then_inc(chunk_done, 1)
            stat(8, STAT, [(sems["ssq_added"], 4 * KB, ssq[:, :])])
            pe.wait_ge(sems["rstd_ready"], 9)
            stat(9, STAT, [(sems["ssq_added"], 5 * KB, ssq[:, :])])
            feed_forward("FF2", 1, 3)
            pe.wait_ge(sems["rstd_ready"], 10)
            stat(10, STAT, [(sems["ssq_added"], 6 * KB, ssq[:, :])])

        @block.scalar
        def _(act):
            A = nc.scalar
            rounded = [0]

            def round_chunk(c, slot, turn):
                act.wait_ge(raw_landed[slot], 16 * turn)
                if not isinstance(c, int) or c >= RING:
                    act.wait_ge(chunk_done, c - (RING - 1))
                A.copy(w_hi[:, slot, :], w_raw[:, slot, :]).then_inc(w_hi_done, 1)

            def round_to(c):
                while rounded[0] <= min(c + AHEAD, CHUNKS - 1):
                    n = rounded[0]
                    round_chunk(n, n % RING, n // RING + 1)
                    rounded[0] += 1

            def root(n, dst, bank, scale, width=T, bias_ap=None):
                act.wait_ge(sems["stat_ready"], n + 1)
                A.activation(dst, ps[bank][:, 0:width], ACT.Sqrt, bias=eps, scale=scale).then_inc(sems["stat_root"], 1)

            def empty(c, o, dst, rows=slice(0, P), width=T):
                act.wait_ge(chunk_done, c + 1)
                A.copy(dst, ps[o % RING][rows, 0:width]).then_inc(evac_act, 1)

            def attend(G0, n_heads, hook=None):
                n_units = 4 * n_heads

                def exps(n):
                    U, G, qb = 4 * G0 + n, G0 + n // 4, n % 4
                    act.wait_ge(sems["s_negmax"], U + 1)
                    if U >= 2:
                        act.wait_ge(sems["pT_ready"], U - 1)
                    r = slice(0, keys_of(G, qb))
                    A.activation(probs[:, U % 2, r], masked[:, U % 2, r], ACT.Exp, bias=negmax[:, U % 2:U % 2 + 1],
                                 scale=scale_of(G), accum_out=rowsum[:, U % 2:U % 2 + 1]).then_inc(sems["p_ready"], 1)

                def turned(n):
                    U, G, qb = 4 * G0 + n, G0 + n // 4, n % 4
                    act.wait_ge(sems["pT_ready"], U + 1)
                    if U >= 2:
                        act.wait_ge(sems["pv_done"], U - 1)
                    r = slice(0, keys_of(G, qb))
                    A.copy(probsT[:, U % 2, r], ps[6 + U % 2][:, r]).then_inc(sems["pT_copied"], 1)

                def out_hi(G):
                    o, hi, _ = out_of(G)
                    act.wait_ge(sems["pv_done"], 4 * (G + 1))
                    A.copy(hi, o).then_inc(sems["o_hi"], 1)

                exps(0)
                exps(1)
                for n in range(n_units):
                    if hook is not None:
                        hook(n)
                    turned(n)
                    if n + 2 < n_units:
                        exps(n + 2)
                    if n % 4 == 0 and n >= 4:
                        out_hi(G0 + n // 4 - 1)
                out_hi(G0 + n_heads - 1)

            act.dma_start(cols[:, :], cols_in).then_inc(consts_landed, 16)
            act.dma_start(consts[:, :], consts_in).then_inc(consts_landed, 16)
            act.dma_start(res[:, :, :], xT).then_inc(x_landed, 16)
            act.wait_ge(mem_landed, 16)
            A.activation(mem_sq[:, :, :], mem_raw[:, :, :], ACT.Square).then_inc(sems["squares"], 1)
            act.wait_ge(x_landed, 16)
            for k in range(0, KB, 2):
                A.activation(x_sq[:, k:k + 2, :], res[:, k:k + 2, :], ACT.Square).then_inc(sems["squares"], 1)
            act.wait_ge(consts_landed, 32)
            root(0, mem_rstd[:, :], 4, 1.0 / D, M)
            root(1, x_rstd[:, :], 5, 1.0 / D)
            round_to(-1)
            for k in range(KB):
                act.wait_ge(sems["start_scaled"], k + 1)
                A.copy(mem_hi[:, k, :], mem_raw[:, k, :]).then_inc(sems["start_hi"], 1)
            for k in range(KB):
                act.wait_ge(sems["start_scaled"], KB + k + 1)
                A.copy(a_hi[:, k, :], res[:, k, :]).then_inc(sems["start_hi"], 1)
            for j in range(XH):
                round_to(CH["MK"] + j)
                empty(CH["MK"] + j, O["MK"] + j, kxT[:, j, :], width=M)
            round_to(CH["MV"] + 3)
            for b in range(MB):
                empty(CH["MV"] + 3, O["MV"] + b, vx[:, b, :])
            for j in range(4):
                round_to(CH["QI"] + j)
                empty(CH["QI"] + j, O["QI"] + j, qiT[:, j, :])
            round_to(CH["KI"])
            act.wait_ge(chunk_done, CH["KI"] + 1)
            ki_bank = ps[O["KI"] % RING]
            A.copy(kiT[0:IDX_DIM, :], ki_bank[0:IDX_DIM, :])
            A.copy(kiT[IDX_DIM:2 * IDX_DIM, :], ki_bank[0:IDX_DIM, :])
            A.mul(wi_rows[0:IDX_HEADS, :], ki_bank[IDX_DIM:IDX_DIM + IDX_HEADS, :],
                  float(IDX_HEADS) ** -0.5).then_inc(evac_act, 1)
            for n in range(3 * IDX_HEADS):
                qb = 1 + n // IDX_HEADS
                act.wait_ge(sems["logits_ready"], n + 1)
                if n >= 2:
                    act.wait_ge(sems["score_added"], n - 1)
                A.activation(relu[:, n % 2, 0:(qb + 1) * P], ps[6 + n % 2][:, 0:(qb + 1) * P], ACT.Relu,
                             scale=float(IDX_DIM) ** -0.5).then_inc(sems["relu_ready"], 1)
            for j in range(16):
                c, o = CH["C"] + j, O["C"] + j
                round_to(c)
                act.wait_ge(chunk_done, c + 1)
                if j % 2 == 0:
                    A.activation(conv_io[:, j // 2, :], ps[o % RING][:, :], ACT.Sigmoid).then_inc(evac_act, 1)
                else:
                    A.copy(conv_in[:, j // 2, PAD:PAD + T], ps[o % RING][:, :]).then_inc(evac_act, 1)
            for j in range(16):
                c, o = CH["G"] + j, O["G"] + j
                round_to(c)
                act.wait_ge(chunk_done, c + 1)
                gate = (gate_c if j < KB else gate_a)[:, j % KB, :]
                A.activation(gate, ps[o % RING][:, :], ACT.Sigmoid, bias=col("b_gate", j)).then_inc(evac_act, 1)
            for half in range(2):
                for t in range(4):
                    round_to(CH["V"] + 4 * half + t)
                for b in range(TB):
                    empty(CH["V"] + 4 * half + 3, O["V"] + 4 * half + b, values[:, b, half * T:(half + 1) * T])

            def empty_qk(n):
                c = CH["ATT"] + n
                round_to(c)
                act.wait_ge(chunk_done, c + 1)
                dst = (qT if n % 2 == 0 else kT)[:, (n // 2) % 2, :]
                A.copy(dst, ps[n % 2][:, :]).then_inc(evac_act, 1)

            def dsa_hook(n):
                h = n // 4
                if n % 4 < 2 and h + 1 < HEADS:
                    empty_qk(2 * (h + 1) + n % 4)
                if n == LN_SQ_AT:
                    for k in range(KB):
                        act.wait_ge(sems["centred"], k + 1)
                        A.activation(ln_sq[:, k, :], conv_io[:, k, :], ACT.Square).then_inc(sems["ln_squared"], 1)
                if n == LN_VAR_AT:
                    act.wait_ge(sems["ln_sum"], 2)
                    A.activation(ln_rstd[:, :], ps[3][:, :], ACT.Sqrt, bias=eps, scale=1.0 / D
                                 ).then_inc(sems["ln_root"], 1)
                if n == LN_SILU_AT:
                    for k in range(KB):
                        act.wait_ge(sems["ln_scaled"], k + 1)
                        A.activation(conv_io[:, k, :], conv_io[:, k, :], ACT.Silu, bias=col("conv_ln_b", k)
                                     ).then_inc(sems["ln_silu"], 1)
                        act.wait_ge(sems["ln_silu"], k + 1)
                        A.copy(b_hi[:, k, :], conv_io[:, k, :]).then_inc(sems["ln_hi"], 1)

            empty_qk(0)
            empty_qk(1)
            attend(DSA_G, HEADS, dsa_hook)
            act.wait_ge(sems["pv_done"], 4 * X_G)
            act.dma_start(res[:, :, :], xT).then_inc(x_again, 16)

            for j in range(KB):
                round_to(CH["CO"] + j)
            for j in range(KB):
                round_to(CH["AO"] + j)
                act.wait_ge(sems["mix_added"], j + 1)
                A.copy(a_hi[:, j, :], gate_c[:, j, :]).then_inc(sems["mix_hi"], 1)

            def residual(e, hset, i, gain, dst_hi, done, src=None, gain_g=None):
                src = res if src is None else src
                act.wait_ge(*done)
                if dst_hi is not None:
                    A.activation(dst_hi[:, i, :], src[:, i, :], ACT.Copy, scale=gain).then_inc(sems["hg_hi"], 1)
                if KB * e + i >= 2:
                    act.wait_ge(sems["ssq_added"], KB * e + i - 1)
                A.activation(sq[:, i % 2, :], src[:, i, :], ACT.Square).then_inc(sems["res_sq"], 1)
                if gain_g is not None:
                    if i >= 1:
                        act.wait_ge(sems["ssqg_added"], i)
                    A.activation(sq_g[:, :], src[:, i, :], ACT.Square, scale=gain_g).then_inc(sems["res_sqg"], 1)

            for j in range(KB):
                round_to(CH["MX"] + j)
                residual(0, 0, j, col("norm_x_g", j), b_hi, (evac_dve, O["MX"] + j + 1 - DVE_FROM))
            for j in range(XH):
                round_to(CH["QX"] + j)
                if j == 0:
                    root(2, rstd[:, :], STAT, 1.0 / D)
            attend(X_G, XH)
            for j in range(KB):
                round_to(CH["OX"] + j // 2)
                residual(1, 1, j, col("norm_ffn_g", j), a_hi, (evac_dve, O["OX"] + j + 1 - DVE_FROM))
            root(3, rstd[:, :], STAT, 1.0 / D)

            def ff_group(name, s, g, last=None):
                c0, o0 = CH[name], O[name]
                for j in range(2 * KB):
                    n = g * 16 + (c0 + j)
                    if not isinstance(n, int):
                        m = c0 + j + AHEAD
                        round_chunk(g * 16 + m, m % RING, g * 4 + (m // RING + 1))
                    else:
                        round_to(n)
                    if j < KB:
                        f = g * KB + (32 * s + j)
                        act.wait_ge(evac_dve, g * 16 + (o0 + j + 1 - DVE_FROM))
                        if not isinstance(f, int) or f >= 2:
                            if not (s == 0 and j < 2 and not isinstance(f, int)):
                                act.wait_ge(sems["f_ready"], f - 1)
                        A.activation(ff_f[:, j % 2, :], ff_t[:, j % 2, :], ACT.Square).then_inc(sems["f_sq"], 1)
                        act.wait_ge(sems["f_sq"], f + 1)
                        A.copy(b_hi[:, j, :], ff_f[:, j % 2, :]).then_inc(sems["f_hi"], 1)
                    elif last is not None:
                        last(j - KB, g * 16 + (o0 + j))

            def feed_forward(name, s, last):
                ff_group(name, s, 0)
                with act.Fori(1, FF_GROUPS - 1) as g:
                    ff_group(name, s, g)
                rounded[0] = CH[name] + 16 * (FF_GROUPS - 1) + AHEAD
                ff_group(name, s, FF_GROUPS - 1, last)

            feed_forward("FF1", 0, lambda i, o: residual(
                2, 2, i, g2g[:, i:i + 1], a_hi, (evac_dve, o + 1 - DVE_FROM), gain_g=col("norm_final_g", i)))
            act.wait_ge(chunk_done, CH["CQ"])
            act.dma_start(sel[0:ML_HEADS, :], sel_in).then_inc(sems["late_landed"], 16)
            act.dma_start(posi[NOPE:NOPE + ROPE, :], pos_in.to_broadcast([ROPE, T])).then_inc(sems["late_landed"], 16)
            round_to(CH["CQ"])
            root(4, rstd[:, :], STAT, 1.0 / D)
            round_to(CH["CQ"] + 1)
            act.wait_ge(sems["mean2"], 1)
            A.activation(sq[:, 0, :], sq[:, 0, :], ACT.Sqrt, bias=eps).then_inc(sems["stat_root"], 1)
            round_to(CH["CKV"])
            for i in range(3):
                act.wait_ge(evac_dve, O["CQ"] + i + 1 - DVE_FROM)
                A.activation(cq_sq[:, i, :], cq[:, i, :], ACT.Square).then_inc(sems["cq_squared"], 1)
                round_to(CH["CQ"] + 1 + i)
            act.wait_ge(evac_dve, O["KR"] + 1 - DVE_FROM)
            g4 = slice(0, ML_HEADS)
            A.activation(gt[g4, 0, :], krT[g4, :], ACT.Identity, bias=col("b_gates_2", 0, p1=ML_HEADS)
                         ).then_inc(sems["gate_step"], 1)
            A.copy(gt[g4, 1, :], krT[32:32 + ML_HEADS, :]).then_inc(sems["gate_step"], 1)
            act.wait_ge(sems["gate_step"], 2)
            A.activation(gt[g4, 2, :], gt[g4, 1, :], ACT.Abs, bias=col("b_gates_2", 1, p1=ML_HEADS)
                         ).then_inc(sems["gate_step"], 1)
            act.wait_ge(sems["gate_step"], 3)
            A.activation(gt[g4, 2, :], gt[g4, 2, :], ACT.Exp, scale=-1.0).then_inc(sems["gate_step"], 1)
            act.wait_ge(sems["gate_step"], 4)
            A.activation(gt[g4, 2, :], gt[g4, 2, :], ACT.Ln, bias=con("misc", 1, ONE_COL, p1=ML_HEADS)
                         ).then_inc(sems["gate_step"], 1)
            A.copy(rot[NOPE:NOPE + ROPE, 1, :], krT[96:128, :]).then_inc(sems["kr_moved"], 1)
            for j in range(4):
                round_to(CH["QK"] + j)
            act.wait_ge(sems["angles"], 2)
            rr = slice(NOPE, NOPE + ROPE)
            A.activation(ropet[rr, 3, :], ropet[rr, 3, :], ACT.Sin).then_inc(sems["sines"], 1)
            A.activation(ropet[rr, 2, :], ropet[rr, 2, :], ACT.Sin).then_inc(sems["sines"], 1)
            for j in range(4):
                round_to(CH["VM"] + j)
                act.wait_ge(sems["ml_conv"], ML_TAPS * (j + 1))
                A.activation(qk_ml[:, j, :], qk_ml[:, j, :], ACT.Silu).then_inc(sems["qk_silu"], 1)
            for j in range(4):
                round_to(CH["OM"] + j)
                act.wait_ge(evac_dve, O["OM"] + j + 1 - DVE_FROM)
                A.activation(ogate[:, j, :], ogate[:, j, :], ACT.Sigmoid).then_inc(sems["o_gated"], 1)
            root(6, cq_rstd[:, 0, :], STAT, 1.0 / (2 * P))
            root(7, cq_rstd[:, 1, :], 5, 1.0 / P)
            for i in range(3):
                act.wait_ge(sems["cn_scaled"], i + 1)
                A.copy(cn_hi[:, i, :], cq[:, i, :]).then_inc(sems["cn_hi_done"], 1)
            for h in range(MLA_HEADS):
                c, o = CH["UQ"] + h // 4, O["UQ"] + h
                round_to(c)
                act.wait_ge(chunk_done, c + 1)
                A.copy(qh[0:NOPE, h, :], ps[o % RING][0:NOPE, :])
                if h >= 2:
                    act.wait_ge(sems["rope_q"], h - 1)
                A.copy(rot[rr, h % 2, :], ps[o % RING][96:128, :]).then_inc(sems["q_moved"], 1)
            round_to(CH["UKV"])
            round_to(CH["UKV"] + 1)
            for h in range(ML_HEADS):
                act.wait_ge(sems["ml_rows"], h + 1)
                if h >= 1:
                    act.wait_ge(sems["ml_floor"], h)
                A.activation(floor_[:, :], ps[5][:, :], ACT.Exp, scale=-1.0).then_inc(sems["ml_fl"], 1)
                act.wait_ge(sems["ml_diag"], TB * (h + 1))
                for jb in range(TB):
                    u = 4 * h + jb
                    if u >= 2:
                        act.wait_ge(sems["ml_sT"], u - 1)
                    g = gcols[:, jb, h:h + 1]
                    m = A.activation(decay[:, u % 2, 0:P], negm_diag[:, jb, :], ACT.Exp, bias=g)
                    if jb < TB - 1:
                        m = A.activation(decay[:, u % 2, P:T - jb * P], ps[4][:, (jb + 1) * P:T], ACT.Exp,
                                         bias=g, scale=-1.0)
                    m.then_inc(sems["ml_decay"], 1)
                act.wait_ge(sems["ml_out"], 4 * (h + 1))
                A.activation(den[:, :], ps[2 * (h % 2) + 1][:, :], ACT.Abs).then_inc(sems["ml_abs"], 1)
                act.wait_ge(sems["ml_num"], h + 1)
                A.activation(ml_square[:, :], hml[:, h % 2, :], ACT.Square).then_inc(sems["ml_sq"], 1)
                act.wait_ge(sems["ml_sum"], h + 1)
                A.activation(den[:, :], ps[5][:, :], ACT.Sqrt, bias=eps, scale=1.0 / ML_V).then_inc(sems["ml_root"], 1)
                act.wait_ge(sems["ml_gated"], h + 1)
                A.copy(a_hi[:, h, :], hml[:, h % 2, :]).then_inc(sems["ml_hi"], 1)
            attend(MLA_G, MLA_HEADS)
            for j in range(KB):
                round_to(CH["WO"] + j)
                residual(3, None, j, None, None, (evac_dve, O["WO"] + j + 1 - DVE_FROM), src=mixed)
            root(8, rstd[:, :], STAT, 1.0 / D)
            for j in range(KB):
                residual(4, 3, j, col("norm_pre_mlp_2", j), a_hi, (sems["post_added"], j + 1))
            root(9, rstd[:, :], STAT, 1.0 / D)
            feed_forward("FF2", 1, lambda i, o: residual(
                5, None, i, None, None, (evac_dve, o + 1 - DVE_FROM), src=ffy))
            root(10, rstd[:, :], STAT, 1.0 / D)

        @block.vector
        def _(dve):
            V = nc.vector

            def inverse(n, t):
                dve.wait_ge(sems["stat_root"], n + 1)
                V.reciprocal(t, t).then_inc(sems["rstd_ready"], 1)
                dve.wait_ge(sems["rstd_ready"], n + 1)

            def out_lo(G):
                o, hi, lo = out_of(G)
                dve.wait_ge(sems["o_hi"], G + 1)
                V.tensor_tensor(lo, o, hi.bitcast(F32), ALU.subtract).then_inc(sems["o_ready"], 1)

            def attend(G0, n_heads, hook=None):
                n_units = 4 * n_heads

                def mask(n):
                    U, G, qb = 4 * G0 + n, G0 + n // 4, n % 4
                    b = U % 2
                    dve.wait_ge(sems["s_ready"], U + 1)
                    if U >= 2:
                        dve.wait_ge(sems["p_ready"], U - 1)
                    r = slice(0, keys_of(G, qb))
                    V.tensor_tensor_reduce(masked[:, b, r], ps[4 + b][:, r], bias_of(G, qb), 1.0, TAKEN,
                                           ALU.add, ALU.max, rowmax[:, b:b + 1]).then_inc(sems["s_masked"], 1)
                    dve.wait_ge(sems["s_masked"], U + 1)
                    V.tensor_scalar(negmax[:, b:b + 1], rowmax[:, b:b + 1], -scale_of(G), None, ALU.mult
                                    ).then_inc(sems["s_negmax"], 1)

                def normalise(n):
                    U, G, qb = 4 * G0 + n, G0 + n // 4, n % 4
                    b = U % 2
                    dve.wait_ge(sems["p_ready"], U + 1)
                    V.reciprocal(rowinv[:, b:b + 1], rowsum[:, b:b + 1]).then_inc(sems["p_inv"], 1)
                    dve.wait_ge(sems["p_inv"], U + 1)
                    p = probs[:, b, 0:keys_of(G, qb)]
                    V.tensor_scalar(p, p, rowinv[:, b:b + 1], None, ALU.mult).then_inc(sems["p_scaled"], 1)

                mask(0)
                mask(1)
                for n in range(n_units):
                    if hook is not None:
                        hook(n)
                    normalise(n)
                    if n + 2 < n_units:
                        mask(n + 2)
                    if n % 4 == 0 and n >= 4:
                        out_lo(G0 + n // 4 - 1)
                out_lo(G0 + n_heads - 1)

            dve.wait_ge(consts_landed, 32)
            V.tensor_tensor(g2g[:, :], col("norm_final_g", 0, KB), col("norm_pre_mix_2", 0, KB), ALU.mult
                            ).then_inc(sems["gains_ready"], 1)
            for n, (raw, rs, hi, lo, g) in enumerate(((mem_raw, mem_rstd, mem_hi, mem_lo, "norm_mem_g"),
                                                      (res, x_rstd, a_hi, a_lo, "norm_mix_g"))):
                inverse(n, rs[:, :])
                for k in range(KB):
                    V.scalar_tensor_tensor(out=raw[:, k, :], in0=raw[:, k, :], scalar=col(g, k), in1=rs[:, :],
                                           op0=ALU.mult, op1=ALU.mult).then_inc(sems["start_scaled"], 1)
                for k in range(KB):
                    dve.wait_ge(sems["start_hi"], KB * n + k + 1)
                    V.tensor_tensor(lo[:, k, :], raw[:, k, :], hi[:, k, :].bitcast(F32), ALU.subtract
                                    ).then_inc(sems["start_ready"], 1)
            dve.wait_ge(sems["wi_turned"], 1)
            V.tensor_copy(wiT[:, :, :], ps[5][:, 0:TB * IDX_HEADS].rearrange("p (t h) -> p t h", t=TB)
                          ).then_inc(sems["wi_copied"], 1)
            dve.wait_ge(sems["wi_copied"], 1)
            for n in range(3 * IDX_HEADS):
                qb, h = 1 + n // IDX_HEADS, n % IDX_HEADS
                s, r, w = score[:, qb, 0:(qb + 1) * P], relu[:, n % 2, 0:(qb + 1) * P], wiT[:, qb, h:h + 1]
                dve.wait_ge(sems["relu_ready"], n + 1)
                if h == 0:
                    V.tensor_scalar(s, r, w, None, ALU.mult).then_inc(sems["score_added"], 1)
                else:
                    dve.wait_ge(sems["score_added"], n)
                    V.scalar_tensor_tensor(out=s, in0=r, scalar=w, in1=s, op0=ALU.mult, op1=ALU.add
                                           ).then_inc(sems["score_added"], 1)
            for qb in range(1, TB):
                dve.wait_ge(sems["score_added"], 3 * IDX_HEADS)
                s = score[:, qb, qb * P:(qb + 1) * P]
                V.tensor_tensor(s, s, con("bias", P, T - P), ALU.add).then_inc(sems["score_masked"], 1)
            steps = 0
            dve.wait_ge(sems["score_masked"], TB - 1)
            for _ in range(TOPK // 8):
                for b in range(1, TB):
                    if steps >= 3:
                        dve.wait_ge(sems["topk_step"], steps - 2)
                    V.max(top8[:, b - 1, :], score[:, b, 0:(b + 1) * P]).then_inc(sems["topk_step"], 1)
                    steps += 1
                for b in range(1, TB):
                    dve.wait_ge(sems["topk_step"], steps - 2)
                    s = score[:, b, 0:(b + 1) * P]
                    V.match_replace(s, top8[:, b - 1, :], s, TAKEN).then_inc(sems["topk_step"], 1)
                    steps += 1
            dve.wait_ge(sems["topk_step"], steps)
            for b in range(1, TB):
                s = score[:, b, 0:(b + 1) * P]
                V.tensor_scalar(s, s, TAKEN_BELOW, MASKED, ALU.is_gt, ALU.mult).then_inc(sems["topk_done"], 1)
            dve.wait_ge(sems["pad_zeroed"], 1)
            with dve.Fori(0, KB // 2) as r:
                def blk(t, e, a, b):
                    return t[:, bass.ds(2 * r + e, 1), a:b].rearrange("p o n -> p (o n)")

                for e in range(2):
                    dve.wait_ge(evac_act, 4 * r + (O["C"] + 2 * e + 2))
                    u = blk(conv_in, e, PAD, PAD + T)
                    V.tensor_tensor(u, u, blk(conv_io, e, 0, T), ALU.mult).then_inc(sems["gated"], 1)
                for k in range(TAPS):
                    for e in range(2):
                        acc = ps[4 + e][:, :]
                        u = blk(conv_in, e, k, k + T)
                        w = cols[:, bass.ds((2 * r + e) * TAPS + (COL["conv_w"] + k), 1)]
                        if k == 0:
                            dve.wait_ge(sems["gated"], 2 * r + (e + 1))
                            V.tensor_scalar(acc, u, w, cols[:, bass.ds(2 * r + (COL["conv_b"] + e), 1)],
                                            ALU.mult, ALU.add).then_inc(sems["tap_done"], 1)
                            continue
                        dve.wait_ge(sems["tap_done"], 2 * (TAPS - 1) * r + (2 * (k - 1) + e + 1))
                        last = k == TAPS - 1
                        V.scalar_tensor_tensor(out=blk(conv_io, e, 0, T) if last else acc, in0=u, scalar=w,
                                               in1=acc, op0=ALU.mult, op1=ALU.add
                                               ).then_inc(sems["conv_done"] if last else sems["tap_done"], 1)

            def dsa_hook(n):
                if n == LN_SQ_AT:
                    dve.wait_ge(sems["ln_sum"], 1)
                    for k in range(KB):
                        V.scalar_tensor_tensor(out=conv_io[:, k, :], in0=ps[3][:, :], scalar=-1.0 / D,
                                               in1=conv_io[:, k, :], op0=ALU.mult, op1=ALU.add
                                               ).then_inc(sems["centred"], 1)
                if n == LN_VAR_AT + 1:
                    dve.wait_ge(sems["ln_root"], 1)
                    V.reciprocal(ln_rstd[:, :], ln_rstd[:, :]).then_inc(sems["ln_inv"], 1)
                    dve.wait_ge(sems["ln_inv"], 1)
                    for k in range(KB):
                        V.scalar_tensor_tensor(out=conv_io[:, k, :], in0=conv_io[:, k, :],
                                               scalar=col("conv_ln_g", k), in1=ln_rstd[:, :],
                                               op0=ALU.mult, op1=ALU.mult).then_inc(sems["ln_scaled"], 1)
                if n == LN_SILU_AT + 1:
                    for k in range(KB):
                        dve.wait_ge(sems["ln_hi"], k + 1)
                        V.tensor_tensor(b_lo[:, k, :], conv_io[:, k, :], b_hi[:, k, :].bitcast(F32), ALU.subtract
                                        ).then_inc(sems["convact_ready"], 1)

            attend(DSA_G, HEADS, dsa_hook)
            for j in range(KB):
                dve.wait_ge(chunk_done, CH["CO"] + j + 1)
                V.tensor_tensor(gate_c[:, j, :], ps[(O["CO"] + j) % RING][:, :], gate_c[:, j, :], ALU.mult
                                ).then_inc(evac_dve, 1)
            for j in range(KB):
                dve.wait_ge(chunk_done, CH["AO"] + j + 1)
                V.tensor_tensor(gate_a[:, j, :], ps[(O["AO"] + j) % RING][:, :], gate_a[:, j, :], ALU.mult
                                ).then_inc(evac_dve, 1)
                dve.wait_ge(evac_dve, O["AO"] + j + 1 - DVE_FROM)
                V.tensor_tensor(gate_c[:, j, :], gate_c[:, j, :], gate_a[:, j, :], ALU.add).then_inc(sems["mix_added"], 1)
                dve.wait_ge(sems["mix_hi"], j + 1)
                V.tensor_tensor(a_lo[:, j, :], gate_c[:, j, :], a_hi[:, j, :].bitcast(F32), ALU.subtract
                                ).then_inc(sems["mix_ready"], 1)

            def add_square(e, i):
                n = KB * e + i
                dve.wait_ge(sems["res_sq"], n + 1)
                if i == 0:
                    V.tensor_copy(ssq[:, :], sq[:, 0, :]).then_inc(sems["ssq_added"], 1)
                else:
                    dve.wait_ge(sems["ssq_added"], n)
                    V.tensor_tensor(ssq[:, :], ssq[:, :], sq[:, i % 2, :], ALU.add).then_inc(sems["ssq_added"], 1)

            def split_residual(hset, i, gain, hi, lo):
                dve.wait_ge(sems["hg_hi"], KB * (min(hset, 3)) + i + 1)
                V.scalar_tensor_tensor(out=lo[:, i, :], in0=res[:, i, :], scalar=gain,
                                       in1=hi[:, i, :].bitcast(F32), op0=ALU.mult, op1=ALU.subtract
                                       ).then_inc(sems["hg_ready"], 1)

            def accumulate(o, t, i, own=True):
                if own:
                    dve.wait_ge(evac_dve, o - DVE_FROM)
                V.tensor_tensor(t[:, i, :], ps_of(o), t[:, i, :], ALU.add).then_inc(evac_dve, 1)

            def ps_of(o):
                return ps[o % RING][:, :]

            dve.wait_ge(x_again, 16)
            for j in range(KB):
                dve.wait_ge(chunk_done, CH["MX"] + j + 1)
                accumulate(O["MX"] + j, res, j, False)
                split_residual(0, j, col("norm_x_g", j), b_hi, b_lo)
                add_square(0, j)
            inverse(2, rstd[:, :])
            for j in range(XH):
                dve.wait_ge(chunk_done, CH["QX"] + j + 1)
                V.tensor_tensor(qxT[:, j, :], ps_of(O["QX"] + j), rstd[:, :], ALU.mult).then_inc(evac_dve, 1)
            attend(X_G, XH)
            for j in range(KB):
                if j % 2 == 0:
                    dve.wait_ge(sems["ox_first"], j // 2 + 1)
                else:
                    dve.wait_ge(chunk_done, CH["OX"] + j // 2 + 1)
                accumulate(O["OX"] + j, res, j)
                split_residual(1, j, col("norm_ffn_g", j), a_hi, a_lo)
                add_square(1, j)
            inverse(3, rstd[:, :])

            def ff_group(name, s, g, dst, last=None):
                c0, o0 = CH[name], O[name]
                for j in range(2 * KB):
                    dve.wait_ge(chunk_done, g * 16 + (c0 + j + 1))
                    o = g * 16 + (o0 + j)
                    bank = ps[(o0 + j) % RING][:, :]
                    if j < KB:
                        f = g * KB + (32 * s + j)
                        if not isinstance(f, int) or f >= 2:
                            if not (s == 0 and j < 2 and not isinstance(f, int)):
                                dve.wait_ge(sems["f_sq"], f - 1)
                        V.scalar_tensor_tensor(out=ff_t[:, j % 2, :], in0=bank, scalar=0.0, in1=rstd[:, :],
                                               op0=ALU.max, op1=ALU.mult).then_inc(evac_dve, 1)
                        dve.wait_ge(sems["f_hi"], f + 1)
                        V.tensor_tensor(b_lo[:, j, :], ff_f[:, j % 2, :], b_hi[:, j, :].bitcast(F32), ALU.subtract
                                        ).then_inc(sems["f_ready"], 1)
                    else:
                        i = j - KB
                        dve.wait_ge(evac_dve, g * 16 + (o0 + j - DVE_FROM))
                        V.tensor_tensor(dst[:, i, :], bank, dst[:, i, :], ALU.add).then_inc(evac_dve, 1)
                        if last is not None:
                            last(i)

            def feed_forward(name, s, dst, last):
                ff_group(name, s, 0, dst)
                with dve.Fori(1, FF_GROUPS - 1) as g:
                    ff_group(name, s, g, dst)
                ff_group(name, s, FF_GROUPS - 1, dst, last)

            def last_ff1(i):
                split_residual(2, i, g2g[:, i:i + 1], a_hi, a_lo)
                add_square(2, i)
                dve.wait_ge(sems["res_sqg"], i + 1)
                if i == 0:
                    V.tensor_copy(ssq_g[:, :], sq_g[:, :]).then_inc(sems["ssqg_added"], 1)
                else:
                    dve.wait_ge(sems["ssqg_added"], i)
                    V.tensor_tensor(ssq_g[:, :], ssq_g[:, :], sq_g[:, :], ALU.add).then_inc(sems["ssqg_added"], 1)

            dve.wait_ge(sems["gains_ready"], 1)
            feed_forward("FF1", 0, res, last_ff1)
            rt = ssq
            inverse(4, rstd[:, :])
            V.tensor_tensor(sq[:, 0, :], rstd[:, :], rstd[:, :], ALU.mult).then_inc(sems["norm2"], 1)
            dve.wait_ge(sems["norm2"], 1)
            dve.wait_ge(sems["stat_ready"], 6)
            V.scalar_tensor_tensor(out=sq[:, 0, :], in0=ps[5][:, :], scalar=1.0 / D, in1=sq[:, 0, :],
                                   op0=ALU.mult, op1=ALU.mult).then_inc(sems["mean2"], 1)
            inverse(5, sq[:, 0, :])
            V.tensor_tensor(rt[:, :], sq[:, 0, :], rstd[:, :], ALU.mult).then_inc(sems["rt_done"], 1)
            dve.wait_ge(sems["rt_done"], 1)
            for i in range(2):
                dve.wait_ge(chunk_done, CH["CQ"] + i + 1)
                V.tensor_tensor(cq[:, i, :], ps_of(O["CQ"] + i), rt[:, :], ALU.mult).then_inc(evac_dve, 1)
            for i in range(KB):
                V.scalar_tensor_tensor(out=res[:, i, :], in0=res[:, i, :], scalar=col("norm_final_g", i),
                                       in1=rstd[:, :], op0=ALU.mult, op1=ALU.mult).then_inc(sems["x2_done"], 1)
            dve.wait_ge(chunk_done, CH["CKV"] + 1)
            V.tensor_tensor(cq[:, 2, :], ps_of(O["CKV"]), rt[:, :], ALU.mult).then_inc(evac_dve, 1)
            dve.wait_ge(chunk_done, CH["KR"] + 1)
            V.tensor_tensor(krT[:, :], ps_of(O["KR"]), rt[:, :], ALU.mult).then_inc(evac_dve, 1)
            dve.wait_ge(sems["rt_turned"], 1)
            V.tensor_copy(rtcol[:, :], ps[6][:, 0:T:P]).then_inc(sems["rt_cols"], 1)
            V.memset(qk_in[:, :, 0:ML_TAPS - 1], 0.0).then_inc(sems["qk_pad"], 1)
            g4 = slice(0, ML_HEADS)

            def chained(ins, n):
                ins.then_inc(sems["row_step"], 1)
                dve.wait_ge(sems["row_step"], n)

            chained(V.memset(gt[g4, 5, :], 0.0), 1)
            dve.wait_ge(sems["gate_step"], 5)
            chained(V.tensor_scalar(gt[g4, 1, :], gt[g4, 1, :], col("b_gates_2", 1, p1=ML_HEADS), 0.0,
                                    ALU.add, ALU.min), 2)
            chained(V.tensor_tensor(gt[g4, 1, :], gt[g4, 1, :], gt[g4, 2, :], ALU.subtract), 3)
            chained(V.tensor_tensor_scan(gt[g4, 3, :], gt[g4, 1, :], gt[g4, 5, :], 0.0, ALU.add, ALU.add), 4)
            chained(V.tensor_tensor(gt[g4, 0, :], gt[g4, 0, :], gt[g4, 3, :], ALU.subtract), 5)
            chained(V.tensor_tensor_scan(gt[g4, 4, :], gt[g4, 5, :], gt[g4, 0, :], 0.0, ALU.add, ALU.max), 6)
            V.tensor_tensor(gt[g4, 3, :], gt[g4, 3, :], gt[g4, 4, :], ALU.add).then_inc(sems["gates_done"], 1)
            rr = slice(NOPE, NOPE + ROPE)
            ang, kq, cosT, sinT = (ropet[rr, i, :] for i in range(4))
            n = 6
            dve.wait_ge(sems["late_landed"], 32)
            n += 1
            chained(V.tensor_copy(ang, posi[rr, :]), n)
            n += 1
            chained(V.tensor_scalar(ang, ang, con("misc", 1, INV_COL, NOPE, NOPE + ROPE), None, ALU.mult), n)
            for dst, turn_off, off in ((sinT, 0.0, 0.0), (cosT, 0.25, float(np.pi / 2))):
                n += 1
                chained(V.tensor_scalar(kq, ang, 1.0 / TWO_PI, turn_off, ALU.mult, ALU.add), n)
                n += 1
                chained(V.tensor_scalar(kq, kq, ROUND, ROUND, ALU.add, ALU.subtract), n)
                src = ang
                for part in (PI_HI, PI_MID, PI_LO):
                    n += 1
                    chained(V.scalar_tensor_tensor(out=dst, in0=kq, scalar=-part, in1=src, op0=ALU.mult,
                                                   op1=ALU.add), n)
                    src = dst
                n += 1
                chained(V.tensor_scalar(dst, dst, off, PI_SAFE, ALU.add, ALU.min), n)
                V.tensor_scalar(dst, dst, -PI_SAFE, None, ALU.max).then_inc(sems["angles"], 1)
            dve.wait_ge(sems["qk_pad"], 1)
            taps = 0
            for j in range(4):
                dve.wait_ge(chunk_done, CH["QK"] + j + 1)
                V.tensor_tensor(qk_in[:, j, ML_TAPS - 1:], ps_of(O["QK"] + j), rt[:, :], ALU.mult
                                ).then_inc(evac_dve, 1)
                dve.wait_ge(evac_dve, O["QK"] + j + 1 - DVE_FROM)
                for k in range(ML_TAPS):
                    x, w = qk_in[:, j, k:k + T], col("conv_w_2", j * ML_TAPS + k)
                    if k == 0:
                        V.tensor_scalar(qk_ml[:, j, :], x, w, col("conv_b_2", j), ALU.mult, ALU.add
                                        ).then_inc(sems["ml_conv"], 1)
                    else:
                        dve.wait_ge(sems["ml_conv"], taps)
                        V.scalar_tensor_tensor(out=qk_ml[:, j, :], in0=x, scalar=w, in1=qk_ml[:, j, :],
                                               op0=ALU.mult, op1=ALU.add).then_inc(sems["ml_conv"], 1)
                    taps += 1
            dve.wait_ge(sems["rt_cols"], 1)
            for b in range(TB):
                dve.wait_ge(chunk_done, CH["VM"] + 4)
                V.tensor_scalar(v_ml[:, b, :], ps_of(O["VM"] + b), rtcol[:, b:b + 1], None, ALU.mult
                                ).then_inc(evac_dve, 1)
            dve.wait_ge(sems["sines"], 2)
            dve.wait_ge(sems["kr_moved"], 1)
            n += 1
            chained(V.tensor_scalar(sinT, sinT, con("misc", 1, SIGN_COL, NOPE, NOPE + ROPE), None, ALU.mult), n)
            n += 1
            chained(V.tensor_tensor(rot[rr, 0, :], krT[rr, :], cosT, ALU.mult), n)
            n += 1
            chained(V.tensor_tensor(rot[rr, 1, :], rot[rr, 1, :], sinT, ALU.mult), n)
            n += 1
            chained(V.tensor_tensor(krT[rr, :], rot[rr, 0, :], rot[rr, 1, :], ALU.add), n)
            for j in range(4):
                dve.wait_ge(chunk_done, CH["OM"] + j + 1)
                V.tensor_tensor(ogate[:, j, :], ps_of(O["OM"] + j), rt[:, :], ALU.mult).then_inc(evac_dve, 1)
            dve.wait_ge(sems["gates_turned"], 1)
            V.tensor_copy(gcols[:, :, :], ps[7][:, 0:TB * ML_HEADS].rearrange("p (t h) -> p t h", t=TB)
                          ).then_inc(sems["gcols_done"], 1)
            inverse(6, cq_rstd[:, 0, :])
            inverse(7, cq_rstd[:, 1, :])
            for i in range(3):
                g = col("q_norm_2", i) if i < 2 else col("kv_norm_2")
                V.scalar_tensor_tensor(out=cq[:, i, :], in0=cq[:, i, :], scalar=g, in1=cq_rstd[:, i // 2, :],
                                       op0=ALU.mult, op1=ALU.mult).then_inc(sems["cn_scaled"], 1)
            for i in range(3):
                dve.wait_ge(sems["cn_hi_done"], i + 1)
                V.tensor_tensor(cn_lo[:, i, :], cq[:, i, :], cn_hi[:, i, :].bitcast(F32), ALU.subtract
                                ).then_inc(sems["cn_ready"], 1)
            for h in range(MLA_HEADS):
                bank = ps_of(O["UQ"] + h)
                dve.wait_ge(sems["q_moved"], h + 1)
                V.tensor_tensor(qh[rr, h, :], bank[rr, :], cosT, ALU.mult).then_inc(evac_dve, 1)
                V.tensor_tensor(rot[rr, h % 2, :], rot[rr, h % 2, :], sinT, ALU.mult).then_inc(sems["rope_half"], 1)
                dve.wait_ge(evac_dve, O["UQ"] + h + 1 - DVE_FROM)
                dve.wait_ge(sems["rope_half"], h + 1)
                V.tensor_tensor(qh[rr, h, :], qh[rr, h, :], rot[rr, h % 2, :], ALU.add).then_inc(sems["rope_q"], 1)
            dve.wait_ge(sems["kv_keys_done"], 1)
            for j in range(4):
                bank = ps_of(O["UKV"] + j)
                V.tensor_copy(kh[0:NOPE, 2 * j, :], bank[0:NOPE, :])
                V.tensor_copy(kh[0:NOPE, 2 * j + 1, :], bank[NOPE:2 * NOPE, :]).then_inc(evac_dve, 1)
            dve.wait_ge(chunk_done, CH["UKV"] + 1)
            for j in range(TB):
                V.tensor_copy(v_mla[:, j, :], ps_of(O["UKV"] + 4 + j)).then_inc(evac_dve, 1)
            dve.wait_ge(sems["rope_q"], MLA_HEADS)
            dve.wait_ge(sems["row_step"], n)
            for h in range(MLA_HEADS):
                V.tensor_copy(kh[rr, h, :], krT[rr, :]).then_inc(sems["rope_done"], 1)
            for h in range(ML_HEADS):
                dve.wait_ge(sems["ml_rows"], h + 1)
                for b in range(TB):
                    V.scalar_tensor_tensor(out=negm_diag[:, b, :], in0=ps[4][:, b * P:(b + 1) * P], scalar=-1.0,
                                           in1=con("maskT", P), op0=ALU.mult, op1=ALU.add).then_inc(sems["ml_diag"], 1)
                for jb in range(TB):
                    u = 4 * h + jb
                    dve.wait_ge(sems["ml_s"], u + 1)
                    dve.wait_ge(sems["ml_decay"], u + 1)
                    if u >= 2:
                        dve.wait_ge(sems["ml_out"], u - 1)
                    w = slice(0, T - jb * P)
                    V.scalar_tensor_tensor(out=sT[:, u % 2, w], in0=ps[6 + u % 2][:, w], scalar=float(ML_QK) ** -0.5,
                                           in1=decay[:, u % 2, w], op0=ALU.mult, op1=ALU.mult
                                           ).then_inc(sems["ml_sT"], 1)
                dve.wait_ge(sems["ml_abs"], h + 1)
                dve.wait_ge(sems["ml_fl"], h + 1)
                V.tensor_tensor(den[:, :], den[:, :], floor_[:, :], ALU.max).then_inc(sems["ml_floor"], 1)
                dve.wait_ge(sems["ml_floor"], h + 1)
                V.reciprocal(den[:, :], den[:, :]).then_inc(sems["ml_inv"], 1)
                dve.wait_ge(sems["ml_inv"], 2 * h + 1)
                hm = hml[:, h % 2, :]
                V.tensor_tensor(hm, ps[2 * (h % 2)][:, :], den[:, :], ALU.mult).then_inc(sems["ml_num"], 1)
                dve.wait_ge(sems["ml_root"], h + 1)
                V.reciprocal(den[:, :], den[:, :]).then_inc(sems["ml_inv"], 1)
                dve.wait_ge(sems["ml_inv"], 2 * h + 2)
                V.scalar_tensor_tensor(out=hm, in0=hm, scalar=col("ml_head_norm_2", h), in1=den[:, :],
                                       op0=ALU.mult, op1=ALU.mult).then_inc(sems["ml_normed"], 1)
                dve.wait_ge(sems["ml_normed"], h + 1)
                dve.wait_ge(sems["o_gated"], h + 1)
                V.tensor_tensor(hm, hm, ogate[:, h, :], ALU.mult).then_inc(sems["ml_gated"], 1)
                dve.wait_ge(sems["ml_hi"], h + 1)
                V.tensor_tensor(a_lo[:, h, :], hm, a_hi[:, h, :].bitcast(F32), ALU.subtract).then_inc(sems["ml_ready"], 1)
            attend(MLA_G, MLA_HEADS)
            for j in range(KB):
                dve.wait_ge(chunk_done, CH["WO"] + j + 1)
                V.tensor_copy(mixed[:, j, :], ps_of(O["WO"] + j)).then_inc(evac_dve, 1)
                add_square(3, j)
            V.memset(ffy[:, :, :], 0.0).then_inc(sems["y_zeroed"], 1)
            inverse(8, rstd[:, :])
            for j in range(KB):
                V.scalar_tensor_tensor(out=mixed[:, j, :], in0=mixed[:, j, :], scalar=col("norm_post_mix_2", j),
                                       in1=rstd[:, :], op0=ALU.mult, op1=ALU.mult).then_inc(sems["post_scaled"], 1)
                dve.wait_ge(sems["post_scaled"], j + 1)
                V.tensor_tensor(res[:, j, :], res[:, j, :], mixed[:, j, :], ALU.add).then_inc(sems["post_added"], 1)
                if j >= 1:
                    split_residual(3, j - 1, col("norm_pre_mlp_2", j - 1), a_hi, a_lo)
                    add_square(4, j - 1)
            split_residual(3, KB - 1, col("norm_pre_mlp_2", KB - 1), a_hi, a_lo)
            add_square(4, KB - 1)
            inverse(9, rstd[:, :])
            dve.wait_ge(sems["y_zeroed"], 1)
            feed_forward("FF2", 1, ffy, lambda i: add_square(5, i))
            inverse(10, rstd[:, :])
            for j in range(KB):
                V.scalar_tensor_tensor(out=ffy[:, j, :], in0=ffy[:, j, :], scalar=col("norm_post_mlp_2", j),
                                       in1=rstd[:, :], op0=ALU.mult, op1=ALU.mult).then_inc(sems["y_scaled"], 1)
                dve.wait_ge(sems["y_scaled"], j + 1)
                V.tensor_tensor(y_out[:, j, :], ffy[:, j, :], res[:, j, :], ALU.add).then_inc(sems["y_written"], 1)


def _columns(v, n):
    return np.ascontiguousarray(np.reshape(v, (n, P)).T)


def _block(w, cols):
    s = w[:, cols]
    return s.reshape(-1, P, s.shape[1]).transpose(1, 0, 2).reshape(P, -1)


def _stream(i):
    w1, w2 = i["w_in"][0], i["w_in_2"][0]
    kv, chunks = i["wx_kv"][0], []

    def blocks(w, n, c0=0):
        chunks.extend(_block(w, slice(c0 + P * j, c0 + P * (j + 1))) for j in range(n))

    def rows(w, c0):
        chunks.extend(_block(w[2 * P * t:2 * P * (t + 1)], slice(c0, c0 + T)) for t in range(4))

    ca, cg, q0, k0, v0 = 0, D, 2 * D, 3 * D, 4 * D
    qi0 = 5 * D
    ki0 = qi0 + IDX_HEADS * IDX_DIM
    wi0 = ki0 + IDX_DIM
    g0 = wi0 + IDX_HEADS
    blocks(kv, 4)
    rows(kv, T)
    blocks(w1, 4, qi0)
    ki = np.zeros((D, P), w1.dtype)
    ki[:, 0:IDX_DIM + IDX_HEADS] = w1[:, ki0:g0]
    blocks(ki, 1)
    for j in range(KB):
        blocks(w1, 1, cg + P * j)
        blocks(w1, 1, ca + P * j)
    blocks(w1, 16, g0)
    rows(w1, v0)
    rows(w1, v0 + T)
    for h in range(HEADS):
        blocks(w1, 1, q0 + P * h)
        blocks(w1, 1, k0 + P * h)
    blocks(i["w_conv_out"][0], KB)
    blocks(i["w_attn_out"][0], KB)
    blocks(i["w_mix_out"][0], KB)
    blocks(i["wx_q"][0], XH)
    wo = i["wx_o"][0]
    for j in range(XH):
        chunks.append(np.concatenate([_block(wo, slice(P * (2 * j + r), P * (2 * j + r + 1))) for r in range(2)], 1))

    def feed_forward(up, down):
        for g in range(FF_GROUPS):
            blocks(up, KB, D * g)
            blocks(down[D * g:D * (g + 1)], KB)

    feed_forward(i["w_ff1"][0], i["w_ff2"][0])
    o0 = 2 * ML_HEADS * ML_QK
    o1 = o0 + ML_HEADS * ML_V
    o2 = o1 + ML_HEADS * ML_V
    o3 = o2 + 2 * ML_HEADS
    o4 = o3 + 2 * P
    o5 = o4 + P
    blocks(w2, 2, o3)
    blocks(w2, 1, o4)
    kr = np.zeros((D, P), w2.dtype)
    kr[:, 0:ML_HEADS] = w2[:, o2:o2 + ML_HEADS]
    kr[:, 32:32 + ML_HEADS] = w2[:, o2 + ML_HEADS:o3]
    kr[:, 64:96] = w2[:, o5:]
    kr[:, 96:112] = w2[:, o5 + ROPE // 2:]
    kr[:, 112:128] = w2[:, o5:o5 + ROPE // 2]
    blocks(kr, 1)
    blocks(w2, 4)
    rows(w2, o0)
    blocks(w2, 4, o1)
    uq = i["w_uq_2"][0]
    per = NOPE + ROPE
    heads = []
    for h in range(MLA_HEADS):
        w = uq[:, per * h:per * (h + 1)]
        heads.append(_block(np.concatenate([w, w[:, NOPE + ROPE // 2:], w[:, NOPE:NOPE + ROPE // 2]], 1),
                            slice(0, P)))
    chunks.append(np.concatenate(heads[0:4], 1))
    chunks.append(np.concatenate(heads[4:8], 1))
    ukv = i["w_ukv_2"][0].reshape(P, MLA_HEADS, NOPE + MLA_V)
    chunks.append(np.concatenate([ukv[:, :, 0:NOPE].reshape(P, -1), ukv[:, :, NOPE:].reshape(P, -1)], 1))
    blocks(i["w_out_2"][0], KB)
    feed_forward(i["w_up_2"][0], i["w_down_2"][0])
    assert len(chunks) == CHUNKS
    return np.stack(chunks)


def _packed(i):
    c = np.zeros((P, NCOLS), np.float32)
    for name, n in COLS:
        if name == "conv_w":
            c[:, COL[name]:COL[name] + n] = i[name][0].reshape(TAPS, KB, P).transpose(2, 1, 0).reshape(P, n)
        elif name == "conv_w_2":
            c[:, COL[name]:COL[name] + n] = i[name][0].reshape(ML_TAPS, 4, P).transpose(2, 1, 0).reshape(P, n)
        elif name == "b_gates_2":
            c[0:ML_HEADS, COL[name]:COL[name] + 2] = i[name][0].reshape(2, ML_HEADS).T
        else:
            c[:, COL[name]:COL[name] + n] = _columns(i[name], n)
    return c


def _constants():
    c = np.zeros((P, NCONST), np.float32)
    c[:, CON["ident"]:CON["ident"] + P] = np.eye(P, dtype=np.float32)
    c[:, CON["ones"]:CON["ones"] + P] = 1.0
    r = np.arange(P)
    later = np.where(r[None, :] > r[:, None], np.float32(MASKED), np.float32(0))
    c[:, CON["bias"] + T - P:CON["bias"] + T] = later
    c[:, CON["maskT"]:CON["maskT"] + P] = later.T
    misc = CON["misc"]
    c[:, misc + EPS_COL] = EPS
    inv = (1.0 / (np.float32(10000.0) ** (np.arange(0, ROPE, 2, dtype=np.float32) / ROPE))).astype(np.float32)
    c[NOPE:NOPE + ROPE, misc + INV_COL] = np.concatenate([inv, inv])
    c[NOPE:NOPE + ROPE, misc + SIGN_COL] = np.concatenate([-np.ones(ROPE // 2), np.ones(ROPE // 2)])
    c[:, misc + ONE_COL] = 1.0
    s = np.zeros((ML_HEADS, ML_HEADS * P), np.float32)
    for h in range(ML_HEADS):
        s[h, h * P:(h + 1) * P] = 1.0
    return c, s


def _feature_major(a, n):
    return np.ascontiguousarray(a.reshape(n, KB, P).transpose(2, 1, 0))


def kernel(**inputs):
    import concourse.bacc as bacc
    from concourse.bass_utils import run_bass_kernel_spmd as run

    i = {k: np.asarray(v) for k, v in inputs.items()}
    consts, sel = _constants()
    arrays = {
        "in_stream": _stream(i),
        "in_xT": _feature_major(i["x"], T),
        "in_memT": _feature_major(i["mem"], M),
        "in_cols": _packed(i),
        "in_consts": consts,
        "in_sel": sel,
        "in_positions": np.ascontiguousarray(i["positions_2"].reshape(1, T)),
    }
    nc = bacc.Bacc("TRN2", target_bir_lowering=False, num_devices=1, dynamic_dma_scratch_size=1024)
    args = [nc.dram_tensor(n, a.shape, mybir.dt.from_np(a.dtype), kind="ExternalInput").ap()
            for n, a in arrays.items()]
    out = nc.dram_tensor("out_y", (P, KB, T), F32, kind="ExternalOutput").ap()
    program(nc, *args, out)
    r = run(nc, [arrays], core_ids=[0])
    y = r.results[0]["out_y"]
    return np.ascontiguousarray(y.transpose(2, 1, 0)).reshape(1, T, D)
```

```python
from contextlib import ExitStack

import numpy as np

import concourse.bass as bass
from concourse import mybir

ALU = mybir.AluOpType
ACT = mybir.ActivationFunctionType
AX = mybir.AxisListType
F32 = mybir.dt.float32
F32R = mybir.dt.float32r
I32 = mybir.dt.int32

P = 128
D = 1024
KB = D // P
T = 512
TB = T // P
M = 256
MB = M // P
EPS = 1e-6
TAPS = 31
PAD = TAPS - 1
HEADS = 8
IDX_HEADS = 8
IDX_DIM = 64
TOPK = 128
XH = 4
ML_HEADS = 4
ML_QK = 64
ML_V = 128
ML_TAPS = 4
MLA_HEADS = 8
NOPE = 64
ROPE = 32
MLA_V = 64
FF_GROUPS = 4
RING = 4
AHEAD = 3
MASKED = -3.0e38
TAKEN = -3.4e38
TAKEN_BELOW = -3.2e38

STAGES = [("MK", 4), ("MV", 4), ("QI", 4), ("KI", 1), ("C", 16), ("G", 16), ("V", 8), ("ATT", 16),
          ("CO", 8), ("AO", 8), ("MX", 8), ("QX", 4), ("OX", 4), ("FF1", 64), ("CQ", 2), ("CKV", 1),
          ("KR", 1), ("QK", 4), ("VM", 4), ("OM", 4), ("UQ", 2), ("UKV", 1), ("WO", 8), ("FF2", 64)]
CH = {}
_n = 0
for _name, _count in STAGES:
    CH[_name] = _n
    _n += _count
CHUNKS = _n
OUTS = [("MK", 4), ("MV", 2), ("QI", 4), ("KI", 1), ("C", 16), ("G", 16), ("V", 8), ("ATT", 16),
        ("CO", 8), ("AO", 8), ("MX", 8), ("QX", 4), ("OX", 8), ("FF1", 64), ("CQ", 2), ("CKV", 1),
        ("KR", 1), ("QK", 4), ("VM", 4), ("OM", 4), ("UQ", 8), ("UKV", 8), ("WO", 8), ("FF2", 64)]
O = {}
_n = 0
for _name, _count in OUTS:
    O[_name] = _n
    _n += _count
DVE_FROM = O["CO"]

COLS = [("norm_mix_g", 8), ("b_gate", 16), ("conv_w", KB * TAPS), ("conv_b", 8), ("conv_ln_g", 8),
        ("conv_ln_b", 8), ("norm_x_g", 8), ("norm_mem_g", 8), ("norm_ffn_g", 8), ("norm_final_g", 8),
        ("norm_pre_mix_2", 8), ("conv_w_2", 4 * ML_TAPS), ("conv_b_2", 4), ("ml_head_norm_2", 4),
        ("q_norm_2", 2), ("kv_norm_2", 1), ("norm_post_mix_2", 8), ("norm_pre_mlp_2", 8),
        ("norm_post_mlp_2", 8), ("b_gates_2", 2)]
COL = {}
_n = 0
for _name, _count in COLS:
    COL[_name] = _n
    _n += _count
NCOLS = _n
CONSTS = [("ident", P), ("ones", P), ("bias", T), ("maskT", P), ("misc", 8)]
CON = {}
_n = 0
for _name, _count in CONSTS:
    CON[_name] = _n
    _n += _count
NCONST = _n
EPS_COL, INV_COL, SIGN_COL, ONE_COL = 0, 1, 2, 3
TWO_PI = float(2 * np.pi)
PI_SAFE = float(np.nextafter(np.float32(np.pi), np.float32(0)))
PI_HI = 6.28125
PI_MID = float(np.float32(np.floor((TWO_PI - PI_HI) * 2.0 ** 21) / 2.0 ** 21))
PI_LO = float(np.float32(TWO_PI - PI_HI - PI_MID))
ROUND = 12582912.0


SEMAPHORES = """
angles centred cn_hi_done cn_ready cn_scaled conv_done convact_ready cq_squared f_hi f_ready f_sq
gains_ready gate_step gated gates_done gates_turned gcols_done hg_hi hg_ready kr_moved kv_keys_done kv_odd
late_landed ln_added ln_hi ln_inv ln_root ln_scaled ln_silu ln_squared ln_sum logits_ready mean2 mix_added
mix_hi mix_ready ml_abs ml_conv ml_decay ml_diag ml_fl ml_floor ml_gated ml_hi ml_inv ml_normed
mem_added mem_scaled mem_squared ml_num ml_out ml_ready ml_mrow ml_root ml_rows ml_s ml_sT ml_sq ml_sum norm2 o_gated o_hi o_ready ox_first
pT_copied pT_ready p_inv p_ready p_scaled pad_zeroed post_added post_scaled post_summed pv_done q_moved qk_pad
qk_silu relu_ready res_sq res_sqg rope_done rope_half rope_q rope_step row_step rstd_ready rt_cols rt_done
rt_turned s_masked s_negmax s_ready score_added score_masked sines squares squares_added ssq_added ssqg_added
start_hi start_ready start_scaled stat_ready stat_root tap_done topk_done topk_step wi_copied
wi_turned x2_done y_scaled y_written
"""
CO_BESIDE = 3
ML_EVERY, ML_LEAD = 7, 2
ML_END = ML_EVERY * (ML_HEADS - 1) - ML_LEAD + 14
LN_MEAN_AT, LN_VAR_AT, LN_SILU_AT, LN_SPLIT_AT = 4, 9, 14, 15


def program(nc, stream, xT, memT, cols_in, consts_in, sel_in, pos_in, out):
    with ExitStack() as ctx:
        def sem(name):
            return ctx.enter_context(nc.semaphore(name))

        def at(name, shape, offset, dt=F32):
            return nc.alloc_sbuf_tensor_at(name, shape, dt, offset=offset)

        W0, A0, B0, C0 = 2048, 34816, 67584, 101376
        G0, H0, QK0, BIAS0, KX0, TMP0, CON0 = 134144, 166912, 183296, 191488, 199680, 207872, 220160
        w_hi = at("w_hi", [P, RING, 1024], W0, F32R)
        w_raw = at("w_raw", [P, RING, 1024], W0 + 16384)
        w_lo = at("w_lo", [P, RING, 1024], W0 + 16384, F32R)
        a_hi = at("a_hi", [P, KB, T], A0, F32R)
        a_lo = at("a_lo", [P, KB, T], A0 + 16384, F32R)
        b_hi = at("b_hi", [P, KB, T], B0, F32R)
        b_lo = at("b_lo", [P, KB, T], B0 + 17408, F32R)
        c_hi = at("c_hi", [P, KB, T], C0, F32R)
        c_lo = at("c_lo", [P, KB, T], C0 + 16384, F32R)
        conv_in = at("conv_in", [P, KB, PAD + T], B0)
        conv_io = at("conv_io", [P, KB, T], B0 + 17408)
        gate_c = at("gate_c", [P, KB, T], G0)
        gate_a = at("gate_a", [P, KB, T], G0 + 16384)
        res = at("res", [P, KB, T], H0)
        values = at("values", [P, TB, D], H0)
        qT = at("qT", [P, 2, T], QK0)
        kT = at("kT", [P, 2, T], QK0 + 4096)
        rstd = at("rstd", [P, T], QK0)
        ssq = at("ssq", [P, T], QK0 + 2048)
        sq = at("sq", [P, 2, T], QK0 + 4096)
        bias = at("bias", [P, TB, T], BIAS0)
        kxT = at("kxT", [P, XH, M], KX0)
        vx = at("vx", [P, MB, XH * P], KX0 + 4096)
        probs = at("probs", [P, 2, T], TMP0 + 4096)
        probsT = at("probsT", [P, 2, T], TMP0 + 8192)
        cols = at("cols", [P, NCOLS], CON0)
        consts = at("consts", [P, NCONST], CON0 + 1792)
        small0 = CON0 + 1792 + NCONST * 4
        top8 = at("top8", [P, 3, 8], small0)
        wiT = at("wiT", [P, TB, IDX_HEADS], small0 + 96)
        rowmax = at("rowmax", [P, 2], small0 + 224)
        negmax = at("negmax", [P, 2], small0 + 256)
        rowsum = at("rowsum", [P, 2], small0 + 288)
        rowinv = at("rowinv", [P, 2], small0 + 320)
        g2g = at("g2g", [P, KB], small0 + 352)
        gcols = at("gcols", [P, TB, ML_HEADS], small0 + 384)
        rtcol = at("rtcol", [P, TB], small0 + 448)
        mem_raw = at("mem_raw", [P, KB, M], G0)
        mem_sq = at("mem_sq", [P, KB, M], G0 + 8192)
        mem_hi = at("mem_hi", [P, KB, M], G0 + 16384, F32R)
        mem_lo = at("mem_lo", [P, KB, M], G0 + 24576, F32R)
        mem_rstd = at("mem_rstd", [P, M + MB], C0 + 28672)
        x_sq = at("x_sq", [P, KB, T], C0)
        x_rstd = at("x_rstd", [P, T], QK0)
        qiT = at("qiT", [P, IDX_HEADS // 2, T], C0 + 16384)
        kiT = at("kiT", [P, T], C0 + 24576)
        wi_rows = at("wi_rows", [P, T], C0 + 26624)
        relu = at("relu", [P, 2, T], TMP0)
        score = bias
        ln_rstd = at("ln_rstd", [P, T], small0 + 480)
        ln_sq = at("ln_sq", [P, KB, T], B0)
        qxT = at("qxT", [P, XH, T], G0)
        xo_hi = at("xo_hi", [P, XH, T], C0, F32R)
        xo_lo = at("xo_lo", [P, XH, T], C0 + 16384, F32R)
        ff_t = at("ff_t", [P, 2, T], TMP0)
        ff_f = at("ff_f", [P, 2, T], TMP0 + 4096)
        ssq_g = at("ssq_g", [P, T], TMP0 + 8192)
        sq_g = at("sq_g", [P, T], TMP0 + 10240)
        cq_sq = at("cq_sq", [P, 3, T], TMP0)
        cq_rstd = at("cq_rstd", [P, 2, T], TMP0 + 6144)
        cq = at("cq", [P, 3, T], C0)
        cn_hi = at("cn_hi", [P, 3, T], TMP0, F32R)
        cn_lo = at("cn_lo", [P, 3, T], C0 + 24576, F32R)
        ogate = at("ogate", [P, ML_HEADS, T], C0 + 16384)
        qk_in = at("qk_in", [P, 4, ML_TAPS - 1 + T], G0)
        qk_ml = at("qk_ml", [P, 4, T], G0 + 8256)
        v_ml = at("v_ml", [P, TB, ML_HEADS * ML_V], G0 + 16448)
        v_mla = at("v_mla", [P, TB, MLA_HEADS * MLA_V], G0)
        qh = at("qh", [P, MLA_HEADS, T], BIAS0)
        kh = at("kh", [P, MLA_HEADS, T], C0)
        gt = at("gt", [P, 6, T], B0)
        ropet = at("ropet", [P, 2, T], G0 + 24640)
        angle = at("angle", [P, 2, T], G0)
        rot = at("rot", [P, 2, T], B0 + 22528)
        krT = at("krT", [P, T], B0 + 26624)
        sel = at("sel", [P, ML_HEADS * P], G0 + 28736)
        posi = at("posi", [P, T], G0 + 4096, I32)
        sT = at("sT", [P, 2, T], TMP0)
        decay = at("decay", [P, 2, T], B0 + 12288)
        negm_diag = at("negm_diag", [P, TB, P], B0 + 16384)
        mrow = at("mrow", [P, T], B0 + 18432)
        ml_square = at("ml_square", [P, T], B0 + 20480)
        den = at("den", [P, T], C0 + 24576)
        floor_ = at("floor_", [P, T], QK0 + 2048)
        hml = at("hml", [P, 2, T], QK0 + 4096)
        mixed = at("mixed", [P, KB, T], C0)
        ffy = at("ffy", [P, KB, T], C0 + 16384)
        y_out = at("y_out", [P, KB, T], G0)

        def col(name, i=0, n=1, p0=0, p1=P):
            return cols[p0:p1, COL[name] + i:COL[name] + i + n]

        def con(name, n, i=0, p0=0, p1=P):
            return consts[p0:p1, CON[name] + i:CON[name] + i + n]

        ident = con("ident", P)
        ones = con("ones", P)
        eps = con("misc", 1, EPS_COL)

        ps = [ctx.enter_context(nc.psum_tensor(f"bank{i}", [P, 512], F32)) for i in range(8)]
        STAT = 4

        raw_landed = [sem(f"raw_landed{i}") for i in range(RING)]
        w_hi_done = sem("w_hi_done")
        w_lo_done = sem("w_lo_done")
        chunk_done = sem("chunk_done")
        evac_act = sem("evac_act")
        evac_dve = sem("evac_dve")
        consts_landed = sem("consts_landed")
        mem_landed = sem("mem_landed")
        x_landed = sem("x_landed")
        x_again = sem("x_landed_again")
        out_landed = sem("out_landed")
        sems = {n: sem(n) for n in SEMAPHORES.split()}
        block = ctx.enter_context(nc.Block())

        def w_slot(t, slot, k, n=P):
            return t[:, slot, k * n:(k + 1) * n]

        DSA_G, X_G, MLA_G = 0, HEADS, HEADS + XH

        def keys_of(G, qb):
            return M if X_G <= G < MLA_G else (qb + 1) * P

        def scale_of(G):
            if G < MLA_G:
                return float(P) ** -0.5
            return float(NOPE + ROPE) ** -0.5

        def bias_of(G, qb):
            n = keys_of(G, qb)
            if G < X_G and qb > 0:
                return bias[:, qb, 0:n]
            if G < X_G or G >= MLA_G:
                return con("bias", n, T - n)
            return con("bias", n, 0)

        def out_of(G):
            if G < X_G:
                return ps[2][:, :], c_hi[:, G, :], c_lo[:, G, :]
            if G < MLA_G:
                return ps[2][:, :], xo_hi[:, G - X_G, :], xo_lo[:, G - X_G, :]
            h = G - MLA_G
            r = slice(MLA_V * (h % 2), MLA_V * (h % 2) + MLA_V)
            return ps[2][r, :], a_hi[r, ML_HEADS + h // 2, :], a_lo[r, ML_HEADS + h // 2, :]

        @block.sync
        def _(sp):
            sp.dma_start(mem_raw[:, :, :], memT).then_inc(mem_landed, 16)
            for j in range(RING):
                sp.dma_start(w_raw[:, j, :], stream[j]).then_inc(raw_landed[j], 16)
            with sp.Fori(1, CHUNKS // RING) as i:
                for j in range(RING):
                    sp.wait_ge(chunk_done, RING * i + j - (RING - 1))
                    sp.dma_start(w_raw[:, j, :],
                                 stream[bass.ds(RING * i + j, 1), :, :].rearrange("o p n -> (o p) n")
                                 ).then_inc(raw_landed[j], 16)
            for i in range(KB):
                sp.wait_ge(sems["y_written"], i + 1)
                sp.dma_start(out[:, i, :], y_out[:, i, :]).then_inc(out_landed, 16)
            sp.wait_ge(out_landed, 16 * KB)

        @block.gpsimd
        def _(pool):
            nc.gpsimd.memset(conv_in[:, :, 0:PAD], 0.0).then_inc(sems["pad_zeroed"], 1)
            with pool.Fori(0, CHUNKS // RING) as i:
                for j in range(RING):
                    pool.wait_ge(w_hi_done, RING * i + j + 1)
                    nc.gpsimd.tensor_tensor(w_lo[:, j, :], w_raw[:, j, :], w_hi[:, j, :].bitcast(F32),
                                            ALU.subtract).then_inc(w_lo_done, 1)

        @block.tensor
        def _(pe):
            def mm(o, l, r, start=True, stop=True):
                return nc.tensor.matmul(o, l, r, start=start, stop=stop)

            def three(o, wh, wl, xh, xl, start, stop):
                mm(o, wh, xh, start, False)
                mm(o, wh, xl, False, False)
                return mm(o, wl, xh, False, stop)

            def bank_free(o, first=None):
                if (o if first is None else first) >= DVE_FROM + RING:
                    pe.wait_ge(evac_dve, o - RING + 1 - DVE_FROM)
                elif first is not None or RING <= o <= DVE_FROM:
                    pe.wait_ge(evac_act, o - RING + 1)

            def chunk(c, slot, o, bank, hi, lo, width=T, ready=None, base=0, first=None, ks=range(KB)):
                if ks[0] == 0:
                    pe.wait_ge(w_lo_done, c + 1)
                    if o is not None:
                        bank_free(o, first)
                for k in ks:
                    if ready is not None:
                        pe.wait_ge(ready, base + k + 1)
                    m = three(ps[bank][:, 0:width], w_slot(w_hi, slot, k), w_slot(w_lo, slot, k),
                              hi[:, k, 0:width], lo[:, k, 0:width], k == 0, k == KB - 1)
                if ks[-1] == KB - 1:
                    m.then_inc(chunk_done, 1)

            def stage(name, n, hi, lo, width=T, ready=None, base=0):
                c0, o0 = CH[name], O[name]
                if n <= RING:
                    for j in range(n):
                        chunk(c0 + j, (c0 + j) % RING, o0 + j, (o0 + j) % RING, hi, lo, width,
                              ready if j == 0 else None, base)
                    return
                with pe.Fori(0, n // RING) as i:
                    for j in range(RING):
                        chunk(RING * i + c0 + j, (c0 + j) % RING, RING * i + (o0 + j), (o0 + j) % RING,
                              hi, lo, width, ready if j == 0 else None, base, first=o0 + j)

            def token_major(c0, o0, blocks, hi, lo, ready=None, base=0):
                for t in range(RING):
                    slot = (c0 + t) % RING
                    pe.wait_ge(w_lo_done, c0 + t + 1)
                    for b in range(blocks):
                        if t == 0:
                            bank_free(o0 + b)
                        for kk in range(2):
                            k = 2 * t + kk
                            if ready is not None and b == 0:
                                pe.wait_ge(ready, base + k + 1)
                            o = ps[(o0 + b) % RING][:, :]
                            xh, xl = hi[:, k, b * P:(b + 1) * P], lo[:, k, b * P:(b + 1) * P]
                            wh, wl = w_slot(w_hi, slot, kk, T), w_slot(w_lo, slot, kk, T)
                            mm(o, xh, wh, k == 0, False)
                            mm(o, xh, wl, False, False)
                            m = mm(o, xl, wh, False, k == KB - 1)
                    m.then_inc(chunk_done, 1)

            def stat(n, bank, parts, width=T):
                for k, (s, v, part) in enumerate(parts):
                    if s is not None:
                        pe.wait_ge(s, v)
                    m = mm(ps[bank][:, 0:width], ones, part, k == 0, k == len(parts) - 1)
                m.then_inc(sems["stat_ready"], 1)

            def attend(G0, n_heads, score, value, hook=None):
                n_units = 4 * n_heads

                def scores(n):
                    U, G, qb = 4 * G0 + n, G0 + n // 4, n % 4
                    if U >= 2:
                        pe.wait_ge(sems["p_ready"], U - 1)
                    score(G, qb, ps[4 + U % 2][:, 0:keys_of(G, qb)]).then_inc(sems["s_ready"], 1)

                def turn(n):
                    U, G, qb = 4 * G0 + n, G0 + n // 4, n % 4
                    pe.wait_ge(sems["p_scaled"], U + 1)
                    if U >= 2:
                        pe.wait_ge(sems["pT_copied"], U - 1)
                    for kb in range(keys_of(G, qb) // P):
                        r = slice(kb * P, (kb + 1) * P)
                        m = nc.tensor.transpose(ps[6 + U % 2][:, r], probs[:, U % 2, r], ident)
                    m.then_inc(sems["pT_ready"], 1)

                def values_out(n):
                    U, G, qb = 4 * G0 + n, G0 + n // 4, n % 4
                    pe.wait_ge(sems["pT_copied"], U + 1)
                    if qb == 0 and G > 0:
                        pe.wait_ge(sems["o_ready"], G)
                    nk = keys_of(G, qb) // P
                    for kb in range(nk):
                        m = mm(out_of(G)[0][:, qb * P:(qb + 1) * P], value(G, kb),
                               probsT[:, U % 2, kb * P:(kb + 1) * P], kb == 0, kb == nk - 1)
                    m.then_inc(sems["pv_done"], 1)

                scores(0)
                scores(1)
                for n in range(n_units):
                    if n + 2 < n_units:
                        scores(n + 2)
                    if hook is not None:
                        hook(n)
                    turn(n)
                    if n >= 1:
                        values_out(n - 1)
                values_out(n_units - 1)

            pe.wait_ge(consts_landed, 32)
            for j in range(4):
                if j == 3:
                    stat(0, 5, [(sems["squares_added"], KB - 1, x_sq[:, 0, :])])
                chunk(CH["MK"] + j, j, O["MK"] + j, j, mem_hi, mem_lo, M, sems["start_ready"] if j == 0 else None)
            token_major(CH["MV"], O["MV"], MB, mem_hi, mem_lo)
            stage("QI", 4, a_hi, a_lo, T, sems["start_ready"], KB)
            stage("KI", 1, a_hi, a_lo)
            pe.wait_ge(sems["mem_added"], 3)
            mm(ps[4][:, 0:M], ones, mem_sq[:, 0, :])
            for b in range(MB):
                m = mm(ps[4][:, M + b:M + b + 1], mem_sq[:, 0, b * P:(b + 1) * P], ones[:, 0:1])
            m.then_inc(sems["stat_ready"], 1)
            pe.wait_ge(evac_act, O["KI"] + 1)
            pe.wait_ge(sems["stat_root"], 1)
            for tb in range(TB):
                m = nc.tensor.transpose(ps[5][:, tb * IDX_HEADS:(tb + 1) * IDX_HEADS],
                                        wi_rows[0:IDX_HEADS, tb * P:(tb + 1) * P],
                                        ident[0:IDX_HEADS, 0:IDX_HEADS])
            m.then_inc(sems["wi_turned"], 1)
            for n in range(3 * IDX_HEADS):
                qb, h = 1 + n // IDX_HEADS, n % IDX_HEADS
                r = slice(IDX_DIM * (h % 2), IDX_DIM * (h % 2) + IDX_DIM)
                if n >= 2:
                    pe.wait_ge(sems["relu_ready"], n - 1)
                mm(ps[6 + n % 2][:, 0:(qb + 1) * P], qiT[r, h // 2, qb * P:(qb + 1) * P],
                   kiT[r, 0:(qb + 1) * P]).then_inc(sems["logits_ready"], 1)
            stage("C", 16, a_hi, a_lo)
            stage("G", 16, a_hi, a_lo)
            for half in range(2):
                token_major(CH["V"] + 4 * half, O["V"] + 4 * half, TB, a_hi, a_lo)

            def qk_chunk(n, ks=range(KB)):
                c, o = CH["ATT"] + n, O["ATT"] + n
                if ks[0] == 0:
                    pe.wait_ge(evac_act, o - 1 if n >= 2 else O["ATT"])
                chunk(c, c % RING, None, n % 2, a_hi, a_lo, ks=ks)

            def conv_out_chunk(j, ks=range(KB)):
                c = CH["CO"] + j
                if ks[0] == 0 and j < 2:
                    pe.wait_ge(evac_act, DVE_FROM)
                elif ks[0] == 0:
                    pe.wait_ge(evac_dve, j - 1)
                chunk(c, c % RING, None, j % 2, b_hi, b_lo, ready=sems["convact_ready"] if j == 0 else None, ks=ks)

            def dsa_score(G, qb, o):
                pe.wait_ge(evac_act, O["ATT"] + 2 * G + 2)
                return mm(o, qT[:, G % 2, qb * P:(qb + 1) * P], kT[:, G % 2, 0:(qb + 1) * P])

            def dsa_hook(n):
                filler, ks = (n - 2) // 2, range(4 * (n % 2), 4 * (n % 2) + 4)
                if 0 <= filler < 2 * (HEADS - 2):
                    qk_chunk(4 + filler, ks)
                elif filler >= 0:
                    conv_out_chunk(filler - 2 * (HEADS - 2), ks)
                if n in (LN_MEAN_AT, LN_VAR_AT):
                    pe.wait_ge(sems["ln_added"], (KB - 1) * (1 if n == LN_MEAN_AT else 2))
                    mm(ps[3][:, :], ones, ln_rstd[:, :]).then_inc(sems["ln_sum"], 1)

            for n in range(4):
                qk_chunk(n)
            pe.wait_ge(sems["conv_done"], KB)
            attend(DSA_G, HEADS, dsa_score,
                   lambda G, kb: values[:, kb, G * P:(G + 1) * P], dsa_hook)
            for j in range(CO_BESIDE, KB):
                conv_out_chunk(j)
            pe.wait_ge(sems["ln_root"], 1)
            pe.wait_ge(evac_dve, KB)
            stage("AO", KB, c_hi, c_lo, ready=sems["o_ready"])
            stage("MX", KB, a_hi, a_lo, ready=sems["mix_ready"])
            def xq_chunk(h, ks=range(KB)):
                if ks[0] == 0:
                    last = O["QX"] + (h - RING if h < XH - 1 else 0)
                    pe.wait_ge(evac_dve, last + 1 - DVE_FROM)
                chunk(CH["QX"] + h, (CH["QX"] + h) % RING, None, (3, 0, 1, 3)[h], b_hi, b_lo,
                      ready=sems["hg_ready"] if h == 0 else None, ks=ks)

            def x_hook(n):
                quarter = n + 2 + 4
                if quarter < XH * 4:
                    xq_chunk(quarter // 4, range(2 * (quarter % 4), 2 * (quarter % 4) + 2))

            xq_chunk(0)
            stat(2, STAT, [(sems["ssq_added"], KB, ssq[:, :])])
            xq_chunk(1, range(4))

            def x_score(G, qb, o):
                h = G - X_G
                pe.wait_ge(evac_dve, O["QX"] + h + 1 - DVE_FROM)
                if h == 0 and qb < 2:
                    pe.wait_ge(sems["stat_root"], 3)
                return mm(o, qxT[:, h, qb * P:(qb + 1) * P], kxT[:, h, :])

            attend(X_G, XH, x_score, lambda G, kb: vx[:, kb, (G - X_G) * P:(G - X_G + 1) * P], x_hook)
            for j in range(XH):
                c = CH["OX"] + j
                pe.wait_ge(w_lo_done, c + 1)
                for r in range(2):
                    o = O["OX"] + 2 * j + r
                    bank_free(o)
                    for k in range(XH):
                        if j == 0 and r == 0:
                            pe.wait_ge(sems["o_ready"], X_G + k + 1)
                        m = three(ps[o % RING][:, :], w_slot(w_hi, c % RING, r * XH + k),
                                  w_slot(w_lo, c % RING, r * XH + k), xo_hi[:, k, :], xo_lo[:, k, :],
                                  k == 0, k == XH - 1)
                    if r == 0:
                        m.then_inc(sems["ox_first"], 1)
                m.then_inc(chunk_done, 1)

            def feed_forward(name, s, hset, norm):
                c0, o0 = CH[name], O[name]

                def ff_chunk(g, j, ready=None, base=0, ks=range(KB)):
                    hi, lo = (a_hi, a_lo) if j < KB else (b_hi, b_lo)
                    chunk(g * 16 + (c0 + j), (c0 + j) % RING, g * 16 + (o0 + j), (o0 + j) % RING, hi, lo, T,
                          ready, base, first=o0 + j, ks=ks)

                for k in range(KB):
                    ff_chunk(0, 0, sems["hg_ready"], KB * hset, range(k, k + 1))
                    norm(k)
                for j in range(1, 2 * KB):
                    ff_chunk(0, j, sems["f_ready"] if j == KB else None, 32 * s)
                with pe.Fori(1, FF_GROUPS) as g:
                    for j in range(2 * KB):
                        ff_chunk(g, j, sems["f_ready"] if j == KB else None, g * KB + 32 * s)

            def norm_ffn(k):
                if k == KB - 1:
                    stat(3, STAT, [(sems["ssq_added"], 2 * KB, ssq[:, :])])

            feed_forward("FF1", 0, 1, norm_ffn)
            stage("CQ", 2, a_hi, a_lo, ready=sems["hg_ready"], base=2 * KB)
            stat(4, STAT, [(sems["ssq_added"], 3 * KB, ssq[:, :])])
            stat(5, 5, [(sems["ssqg_added"], KB, ssq_g[:, :])])
            stage("CKV", 1, a_hi, a_lo)
            stage("KR", 1, a_hi, a_lo)
            pe.wait_ge(sems["rt_done"], 1)
            for tb in range(TB):
                m = nc.tensor.transpose(ps[6][:, tb * P:(tb + 1) * P], ssq[:, tb * P:(tb + 1) * P], ident)
            m.then_inc(sems["rt_turned"], 1)
            stage("QK", 4, a_hi, a_lo)
            stat(6, STAT, [(sems["cq_squared"], k + 1, cq_sq[:, k, :]) for k in range(2)])
            stat(7, 5, [(sems["cq_squared"], 3, cq_sq[:, 2, :])])
            token_major(CH["VM"], O["VM"], TB, a_hi, a_lo)
            stage("OM", 4, a_hi, a_lo)
            for t in range(2):
                c = CH["UQ"] + t
                pe.wait_ge(w_lo_done, c + 1)
                for j in range(4):
                    o = O["UQ"] + 4 * t + j
                    bank_free(o)
                    for k in range(2):
                        if t == 0 and j == 0:
                            pe.wait_ge(sems["cn_ready"], k + 1)
                        m = three(ps[o % RING][:, :], w_slot(w_hi, c % RING, 2 * j + k),
                                  w_slot(w_lo, c % RING, 2 * j + k), cn_hi[:, k, :], cn_lo[:, k, :],
                                  k == 0, k == 1)
                m.then_inc(chunk_done, 1)
            c = CH["UKV"]
            pe.wait_ge(w_lo_done, c + 1)
            pe.wait_ge(sems["cn_ready"], 3)
            for j in range(4):
                o = O["UKV"] + j
                bank_free(o)
                m = three(ps[o % RING][:, :], w_slot(w_hi, c % RING, j), w_slot(w_lo, c % RING, j),
                          cn_hi[:, 2, :], cn_lo[:, 2, :], True, True)
            m.then_inc(sems["kv_keys_done"], 1)
            for j in range(TB):
                o = O["UKV"] + 4 + j
                bank_free(o)
                xh, xl = cn_hi[:, 2, j * P:(j + 1) * P], cn_lo[:, 2, j * P:(j + 1) * P]
                wh, wl = w_slot(w_hi, c % RING, 1, T), w_slot(w_lo, c % RING, 1, T)
                m = three(ps[o % RING][:, :], xh, xl, wh, wl, True, True)
            m.then_inc(chunk_done, 1)
            pe.wait_ge(sems["gates_done"], 1)
            for tb in range(TB):
                m = nc.tensor.transpose(ps[7][:, tb * ML_HEADS:(tb + 1) * ML_HEADS],
                                        gt[0:ML_HEADS, 0, tb * P:(tb + 1) * P],
                                        ident[0:ML_HEADS, 0:ML_HEADS])
            m.then_inc(sems["gates_turned"], 1)
            pe.wait_ge(evac_dve, O["WO"] - DVE_FROM)
            pe.wait_ge(sems["gcols_done"], 1)
            pe.wait_ge(sems["rstd_ready"], 8)
            pe.wait_ge(sems["late_landed"], 32)
            pe.wait_ge(sems["qk_silu"], 4)
            num, dn, shared = ps[0], ps[1], ps[3]

            def ml_step(h, st):
                r = slice(ML_QK * (h % 2), ML_QK * (h % 2) + ML_QK)
                if 0 <= st < 2:
                    if st == 0 and h >= 1:
                        pe.wait_ge(sems["ml_sT"], 4 * h)
                    elif st == 1:
                        pe.wait_ge(sems["ml_mrow"], h + 1)
                    mm(shared[:, :], sel[0:ML_HEADS, h * P:(h + 1) * P], gt[0:ML_HEADS, 4 - st, :]
                       ).then_inc(sems["ml_rows"], 1)
                if 3 <= st < 3 + TB:
                    jb = st - 3
                    if jb == 0:
                        pe.wait_ge(sems["ml_fl"], h + 1)
                    else:
                        pe.wait_ge(sems["ml_sT"], 4 * h + jb)
                    mm(shared[:, 0:T - jb * P], qk_ml[r, 2 + h // 2, jb * P:(jb + 1) * P],
                       qk_ml[r, h // 2, jb * P:T]).then_inc(sems["ml_s"], 1)
                if 4 <= st < 4 + TB:
                    jb = st - 4
                    u = 4 * h + jb
                    pe.wait_ge(sems["ml_sT"], u + 1)
                    if jb == 0 and h >= 1:
                        pe.wait_ge(sems["ml_num"], h)
                        pe.wait_ge(sems["ml_root"], h)
                    part = sT[:, u % 2, 0:T - jb * P]
                    mm(num[:, jb * P:T], v_ml[:, jb, h * ML_V:(h + 1) * ML_V], part, jb == 0, jb == TB - 1)
                    mm(dn[:, jb * P:T], ones, part, jb == 0, jb == TB - 1).then_inc(sems["ml_out"], 1)
                if st == 10:
                    pe.wait_ge(sems["ml_sq"], h + 1)
                    mm(dn[:, :], ones, ml_square[:, :]).then_inc(sems["ml_sum"], 1)

            def ml_hook(n):
                for h in range(ML_HEADS):
                    ml_step(h, n + ML_LEAD - ML_EVERY * h)

            def mla_score(G, qb, o):
                h = G - MLA_G
                if qb == 0:
                    pe.wait_ge(sems["rope_done"], h + 1)
                return mm(o, qh[0:NOPE + ROPE, h, qb * P:(qb + 1) * P], kh[0:NOPE + ROPE, h, 0:(qb + 1) * P])

            for n in range(-ML_LEAD, 0):
                ml_hook(n)
            attend(MLA_G, MLA_HEADS, mla_score,
                   lambda G, kb: v_mla[:, kb, (G - MLA_G) * MLA_V:(G - MLA_G + 1) * MLA_V], ml_hook)
            for n in range(4 * MLA_HEADS, ML_END):
                ml_hook(n)
            for j in range(KB):
                c, o = CH["WO"] + j, O["WO"] + j
                pe.wait_ge(w_lo_done, c + 1)
                if j == 0:
                    pe.wait_ge(sems["o_ready"], MLA_G + MLA_HEADS)
                bank_free(o)
                order = [k for k in range(KB) if k != ML_HEADS - 1] + [ML_HEADS - 1]
                for k in order:
                    if j == 0 and k < ML_HEADS:
                        pe.wait_ge(sems["ml_ready"], k + 1)
                    m = three(ps[o % RING][:, :], w_slot(w_hi, c % RING, k), w_slot(w_lo, c % RING, k),
                              a_hi[:, k, :], a_lo[:, k, :], k == order[0], k == order[-1])
                m.then_inc(chunk_done, 1)
            stat(8, STAT, [(sems["ssq_added"], 4 * KB, ssq[:, :])])

            def norm_pre_mlp(k):
                pe.wait_ge(sems["res_sq"], 4 * KB + k + 1)
                mm(ps[STAT][:, :], ones, sq[:, k % 2, :], k == 0, k == KB - 1).then_inc(sems["post_summed"], 1)

            feed_forward("FF2", 1, 3, norm_pre_mlp)
            pe.wait_ge(sems["rstd_ready"], 10)
            stat(9, STAT, [(sems["ssq_added"], 5 * KB, ssq[:, :])])

        @block.scalar
        def _(act):
            A = nc.scalar
            rounded = [0]

            def round_chunk(c, slot, turn):
                act.wait_ge(raw_landed[slot], 16 * turn)
                if not isinstance(c, int) or c >= RING:
                    act.wait_ge(chunk_done, c - (RING - 1))
                A.copy(w_hi[:, slot, :], w_raw[:, slot, :]).then_inc(w_hi_done, 1)

            def round_to(c):
                while rounded[0] <= min(c + AHEAD, CHUNKS - 1):
                    n = rounded[0]
                    round_chunk(n, n % RING, n // RING + 1)
                    rounded[0] += 1

            def root(n, dst, bank, scale, width=T, sums=None):
                if sums is None:
                    act.wait_ge(sems["stat_ready"], n + 1 if n < 9 else n)
                else:
                    act.wait_ge(*sums)
                A.activation(dst, ps[bank][:, 0:width], ACT.Sqrt, bias=eps, scale=scale).then_inc(sems["stat_root"], 1)

            def empty(c, o, dst, rows=slice(0, P), width=T):
                act.wait_ge(chunk_done, c + 1)
                A.copy(dst, ps[o % RING][rows, 0:width]).then_inc(evac_act, 1)

            def attend(G0, n_heads, hook=None, after=None):
                n_units = 4 * n_heads

                def exps(n):
                    U, G, qb = 4 * G0 + n, G0 + n // 4, n % 4
                    act.wait_ge(sems["s_masked"], U + 1)
                    if U >= 2:
                        act.wait_ge(sems["pT_ready"], U - 1)
                    r = slice(0, keys_of(G, qb))
                    A.activation(probs[:, U % 2, r], ps[4 + U % 2][:, r], ACT.Exp, bias=negmax[:, U % 2:U % 2 + 1],
                                 scale=-1.0, accum_out=rowsum[:, U % 2:U % 2 + 1]).then_inc(sems["p_ready"], 1)

                def turned(n):
                    U, G, qb = 4 * G0 + n, G0 + n // 4, n % 4
                    act.wait_ge(sems["pT_ready"], U + 1)
                    if U >= 2:
                        act.wait_ge(sems["pv_done"], U - 1)
                    r = slice(0, keys_of(G, qb))
                    A.copy(probsT[:, U % 2, r], ps[6 + U % 2][:, r]).then_inc(sems["pT_copied"], 1)

                def out_hi(G):
                    o, hi, _ = out_of(G)
                    act.wait_ge(sems["pv_done"], 4 * (G + 1))
                    A.copy(hi, o).then_inc(sems["o_hi"], 1)

                exps(0)
                exps(1)
                for n in range(n_units):
                    if hook is not None:
                        hook(n)
                    turned(n)
                    if n + 2 < n_units:
                        exps(n + 2)
                    if n % 4 == 0 and n >= 4:
                        out_hi(G0 + n // 4 - 1)
                    if after is not None:
                        after(n)
                out_hi(G0 + n_heads - 1)

            act.dma_start(cols[:, :], cols_in).then_inc(consts_landed, 16)
            act.dma_start(consts[:, :], consts_in).then_inc(consts_landed, 16)
            act.dma_start(res[:, :, :], xT).then_inc(x_landed, 16)
            act.wait_ge(consts_landed, 32)
            act.wait_ge(mem_landed, 16)
            for k in range(KB):
                A.activation(mem_hi[:, k, :], mem_raw[:, k, :], ACT.Copy, scale=col("norm_mem_g", k)
                             ).then_inc(sems["start_hi"], 1)
                if k % 4 == 1:
                    round_to(k // 4 - AHEAD)
            act.wait_ge(x_landed, 16)
            for k in range(KB):
                A.activation(x_sq[:, k, :], res[:, k, :], ACT.Square).then_inc(sems["squares"], 1)
            round_to(0)
            for j in range(XH):
                if j == 2:
                    root(0, x_rstd[:, :], 5, 1.0 / D)
                empty(CH["MK"] + j, O["MK"] + j, kxT[:, j, :], width=M)
                round_to(CH["MK"] + j + 1)
            for k in range(KB):
                act.wait_ge(sems["start_scaled"], k + 1)
                A.copy(a_hi[:, k, :], res[:, k, :]).then_inc(sems["start_hi"], 1)
                if k % 2 == 1:
                    round_to(CH["MV"] + k // 2)
            for b in range(MB):
                empty(CH["MV"] + 3, O["MV"] + b, vx[:, b, :])
            for j in range(4):
                round_to(CH["QI"] + j)
                empty(CH["QI"] + j, O["QI"] + j, qiT[:, j, :])
            round_to(CH["KI"])
            act.wait_ge(chunk_done, CH["KI"] + 1)
            ki_bank = ps[O["KI"] % RING]
            A.copy(kiT[0:IDX_DIM, :], ki_bank[0:IDX_DIM, :])
            A.copy(kiT[IDX_DIM:2 * IDX_DIM, :], ki_bank[0:IDX_DIM, :])
            A.mul(wi_rows[0:IDX_HEADS, :], ki_bank[IDX_DIM:IDX_DIM + IDX_HEADS, :],
                  float(IDX_HEADS) ** -0.5).then_inc(evac_act, 1)
            root(1, mem_rstd[:, :], 4, 1.0 / D, M + MB)
            for n in range(3 * IDX_HEADS):
                qb = 1 + n // IDX_HEADS
                act.wait_ge(sems["logits_ready"], n + 1)
                if n >= 2:
                    act.wait_ge(sems["score_added"], n - 1)
                A.activation(relu[:, n % 2, 0:(qb + 1) * P], ps[6 + n % 2][:, 0:(qb + 1) * P], ACT.Relu,
                             scale=float(IDX_DIM) ** -0.5).then_inc(sems["relu_ready"], 1)
            for j in range(16):
                c, o = CH["C"] + j, O["C"] + j
                round_to(c)
                act.wait_ge(chunk_done, c + 1)
                if j % 2 == 0:
                    A.activation(conv_io[:, j // 2, :], ps[o % RING][:, :], ACT.Sigmoid).then_inc(evac_act, 1)
                else:
                    A.copy(conv_in[:, j // 2, PAD:PAD + T], ps[o % RING][:, :]).then_inc(evac_act, 1)
            for j in range(16):
                c, o = CH["G"] + j, O["G"] + j
                round_to(c)
                act.wait_ge(chunk_done, c + 1)
                gate = (gate_c if j < KB else gate_a)[:, j % KB, :]
                A.activation(gate, ps[o % RING][:, :], ACT.Sigmoid, bias=col("b_gate", j)).then_inc(evac_act, 1)
            for half in range(2):
                for t in range(4):
                    round_to(CH["V"] + 4 * half + t)
                for b in range(TB):
                    empty(CH["V"] + 4 * half + 3, O["V"] + 4 * half + b, values[:, b, half * T:(half + 1) * T])

            def empty_qk(n):
                c = CH["ATT"] + n
                round_to(c)
                act.wait_ge(chunk_done, c + 1)
                dst = (qT if n % 2 == 0 else kT)[:, (n // 2) % 2, :]
                A.copy(dst, ps[n % 2][:, :]).then_inc(evac_act, 1)

            def dsa_hook(n):
                filler = (n - 2) // 2
                if n % 2 == 0 and filler >= 0:
                    round_to(CH["ATT"] + 4 + filler)
                if n % 2 == 1 and 0 <= filler < 2 * (HEADS - 2):
                    empty_qk(4 + filler)
                if LN_MEAN_AT < n <= LN_MEAN_AT + KB // 2:
                    for k in range(2 * (n - LN_MEAN_AT) - 2, 2 * (n - LN_MEAN_AT)):
                        act.wait_ge(sems["centred"], k + 1)
                        A.activation(ln_sq[:, k, :], conv_io[:, k, :], ACT.Square).then_inc(sems["ln_squared"], 1)
                if n == LN_VAR_AT + 1:
                    act.wait_ge(sems["ln_sum"], 2)
                    A.activation(ln_rstd[:, :], ps[3][:, :], ACT.Sqrt, bias=eps, scale=1.0 / D
                                 ).then_inc(sems["ln_root"], 1)
                if n in (LN_SILU_AT, LN_SILU_AT + 4):
                    for k in range(n - LN_SILU_AT, n - LN_SILU_AT + 4):
                        act.wait_ge(sems["ln_scaled"], k + 1)
                        A.activation(conv_io[:, k, :], conv_io[:, k, :], ACT.Silu, bias=col("conv_ln_b", k)
                                     ).then_inc(sems["ln_silu"], 1)
                if 0 <= n - LN_SPLIT_AT < KB:
                    k = n - LN_SPLIT_AT
                    act.wait_ge(sems["ln_silu"], k + 1)
                    A.copy(b_hi[:, k, :], conv_io[:, k, :]).then_inc(sems["ln_hi"], 1)

            for n in range(4):
                empty_qk(n)
            attend(DSA_G, HEADS, dsa_hook)
            act.wait_ge(sems["pv_done"], 4 * X_G)
            act.dma_start(res[:, :, :], xT).then_inc(x_again, 16)

            for j in range(CO_BESIDE, KB):
                round_to(CH["CO"] + j)
            for j in range(KB):
                round_to(CH["AO"] + j)
                act.wait_ge(sems["mix_added"], j + 1)
                A.copy(a_hi[:, j, :], gate_c[:, j, :]).then_inc(sems["mix_hi"], 1)

            def residual(e, hset, i, gain, dst_hi, done, src=None, gain_g=None):
                src = res if src is None else src
                act.wait_ge(*done)
                if dst_hi is not None:
                    A.activation(dst_hi[:, i, :], src[:, i, :], ACT.Copy, scale=gain).then_inc(sems["hg_hi"], 1)
                if e == 4 and i >= 2:
                    act.wait_ge(sems["post_summed"], i - 1)
                elif e == 5 and i < 2:
                    act.wait_ge(sems["post_summed"], KB - 1 + i)
                elif KB * e + i >= 2:
                    act.wait_ge(sems["ssq_added"], KB * (e if e < 5 else 4) + i - 1)
                A.activation(sq[:, i % 2, :], src[:, i, :], ACT.Square).then_inc(sems["res_sq"], 1)
                if gain_g is not None:
                    if i >= 1:
                        act.wait_ge(sems["ssqg_added"], i)
                    A.activation(sq_g[:, :], src[:, i, :], ACT.Square, scale=gain_g).then_inc(sems["res_sqg"], 1)

            for j in range(KB):
                round_to(CH["MX"] + j)
                residual(0, 0, j, col("norm_x_g", j), b_hi, (evac_dve, O["MX"] + j + 1 - DVE_FROM))
            round_to(CH["QX"])
            root(2, rstd[:, :], STAT, 1.0 / D)
            round_to(CH["QX"] + 1)

            def x_hook(n):
                if n in (2, 6):
                    round_to(CH["QX"] + 2 + (n - 2) // 4)

            attend(X_G, XH, x_hook)
            for j in range(KB):
                round_to(CH["OX"] + j // 2)
                residual(1, 1, j, col("norm_ffn_g", j), a_hi, (evac_dve, O["OX"] + j + 1 - DVE_FROM))
            root(3, rstd[:, :], STAT, 1.0 / D)

            def ff_group(name, s, g, last=None, beside=None):
                c0, o0 = CH[name], O[name]
                for j in range(2 * KB):
                    if beside is not None:
                        beside(j)
                    n = g * 16 + (c0 + j)
                    if not isinstance(n, int):
                        m = c0 + j + AHEAD
                        round_chunk(g * 16 + m, m % RING, g * 4 + (m // RING + 1))
                    else:
                        round_to(n)
                    if j < KB:
                        f = g * KB + (32 * s + j)
                        act.wait_ge(evac_dve, g * 16 + (o0 + j + 1 - DVE_FROM))
                        if not isinstance(f, int) or f >= 2:
                            if not (s == 0 and j < 2 and not isinstance(f, int)):
                                act.wait_ge(sems["f_ready"], f - 1)
                        A.activation(ff_f[:, j % 2, :], ff_t[:, j % 2, :], ACT.Square).then_inc(sems["f_sq"], 1)
                        act.wait_ge(sems["f_sq"], f + 1)
                        A.copy(b_hi[:, j, :], ff_f[:, j % 2, :]).then_inc(sems["f_hi"], 1)
                    elif last is not None:
                        last(j - KB, g * 16 + (o0 + j))

            def feed_forward(name, s, last, beside=None):
                ff_group(name, s, 0, beside=beside)
                with act.Fori(1, FF_GROUPS - 1) as g:
                    ff_group(name, s, g)
                rounded[0] = CH[name] + 16 * (FF_GROUPS - 1) + AHEAD
                ff_group(name, s, FF_GROUPS - 1, last)

            act.wait_ge(sems["pv_done"], 4 * MLA_G)
            act.dma_start(posi[NOPE:NOPE + ROPE, :], pos_in.to_broadcast([ROPE, T])).then_inc(sems["late_landed"], 16)
            act.dma_start(sel[0:ML_HEADS, :], sel_in).then_inc(sems["late_landed"], 16)
            rr = slice(NOPE, NOPE + ROPE)

            def rotary(j):
                if j == KB + 5:
                    act.wait_ge(sems["angles"], 2)
                    A.activation(ropet[rr, 1, :], ropet[rr, 1, :], ACT.Sin).then_inc(sems["sines"], 1)
                    A.activation(ropet[rr, 0, :], ropet[rr, 0, :], ACT.Sin).then_inc(sems["sines"], 1)

            feed_forward("FF1", 0, lambda i, o: residual(
                2, 2, i, g2g[:, i:i + 1], a_hi, (evac_dve, o + 1 - DVE_FROM), gain_g=col("norm_final_g", i)),
                rotary)
            round_to(CH["CQ"])
            root(4, rstd[:, :], STAT, 1.0 / D)
            round_to(CH["CQ"] + 1)
            act.wait_ge(sems["mean2"], 1)
            A.activation(sq[:, 0, :], sq[:, 0, :], ACT.Sqrt, bias=eps).then_inc(sems["stat_root"], 1)
            round_to(CH["CKV"])
            for i in range(3):
                act.wait_ge(evac_dve, O["CQ"] + i + 1 - DVE_FROM)
                A.activation(cq_sq[:, i, :], cq[:, i, :], ACT.Square).then_inc(sems["cq_squared"], 1)
                round_to(CH["CQ"] + 1 + i)
            act.wait_ge(evac_dve, O["KR"] + 1 - DVE_FROM)
            g4 = slice(0, ML_HEADS)
            A.activation(gt[g4, 0, :], krT[g4, :], ACT.Identity, bias=col("b_gates_2", 0, p1=ML_HEADS)
                         ).then_inc(sems["gate_step"], 1)
            A.copy(gt[g4, 1, :], krT[32:32 + ML_HEADS, :]).then_inc(sems["gate_step"], 1)
            act.wait_ge(sems["gate_step"], 2)
            A.activation(gt[g4, 2, :], gt[g4, 1, :], ACT.Abs, bias=col("b_gates_2", 1, p1=ML_HEADS)
                         ).then_inc(sems["gate_step"], 1)
            act.wait_ge(sems["gate_step"], 3)
            A.activation(gt[g4, 2, :], gt[g4, 2, :], ACT.Exp, scale=-1.0).then_inc(sems["gate_step"], 1)
            act.wait_ge(sems["gate_step"], 4)
            A.activation(gt[g4, 2, :], gt[g4, 2, :], ACT.Ln, bias=con("misc", 1, ONE_COL, p1=ML_HEADS)
                         ).then_inc(sems["gate_step"], 1)
            A.copy(rot[NOPE:NOPE + ROPE, 1, :], krT[96:128, :]).then_inc(sems["kr_moved"], 1)
            for j in range(4):
                round_to(CH["QK"] + j)
            root(6, cq_rstd[:, 0, :], STAT, 1.0 / (2 * P))
            root(7, cq_rstd[:, 1, :], 5, 1.0 / P)
            for i in range(3):
                act.wait_ge(sems["cn_scaled"], i + 1)
                A.copy(cn_hi[:, i, :], cq[:, i, :]).then_inc(sems["cn_hi_done"], 1)
            for j in range(4):
                round_to(CH["VM"] + j)
                act.wait_ge(sems["ml_conv"], ML_TAPS * (j + 1))
                A.activation(qk_ml[:, j, :], qk_ml[:, j, :], ACT.Silu).then_inc(sems["qk_silu"], 1)
            for j in range(4):
                round_to(CH["OM"] + j)
                act.wait_ge(evac_dve, O["OM"] + j + 1 - DVE_FROM)
                A.activation(ogate[:, j, :], ogate[:, j, :], ACT.Sigmoid).then_inc(sems["o_gated"], 1)
            for h in range(MLA_HEADS):
                c, o = CH["UQ"] + h // 4, O["UQ"] + h
                round_to(c)
                act.wait_ge(chunk_done, c + 1)
                A.copy(qh[0:NOPE, h, :], ps[o % RING][0:NOPE, :])
                if h >= 2:
                    act.wait_ge(sems["rope_q"], h - 1)
                A.copy(rot[rr, h % 2, :], ps[o % RING][96:128, :]).then_inc(sems["q_moved"], 1)
            round_to(CH["UKV"])
            act.wait_ge(sems["kv_keys_done"], 1)
            for j in range(4):
                A.copy(kh[0:NOPE, 2 * j + 1, :], ps[(O["UKV"] + j) % RING][NOPE:2 * NOPE, :]
                       ).then_inc(sems["kv_odd"], 1)
            round_to(CH["UKV"] + 1)
            def ml_step(h, st):
                if st == 0:
                    act.wait_ge(sems["ml_rows"], 2 * h + 1)
                    if h >= 1:
                        act.wait_ge(sems["ml_diag"], TB * h)
                    A.copy(mrow[:, :], ps[3][:, :]).then_inc(sems["ml_mrow"], 1)
                if st == 1:
                    act.wait_ge(sems["ml_rows"], 2 * h + 2)
                    if h >= 1:
                        act.wait_ge(sems["ml_floor"], h)
                    A.activation(floor_[:, :], ps[3][:, :], ACT.Exp, scale=-1.0).then_inc(sems["ml_fl"], 1)
                if 2 <= st < 2 + TB:
                    jb = st - 2
                    u = 4 * h + jb
                    act.wait_ge(sems["ml_diag"], TB * (h + 1))
                    if u >= 2:
                        act.wait_ge(sems["ml_sT"], u - 1)
                    g = gcols[:, jb, h:h + 1]
                    m = A.activation(decay[:, u % 2, 0:P], negm_diag[:, jb, :], ACT.Exp, bias=g)
                    if jb < TB - 1:
                        m = A.activation(decay[:, u % 2, P:T - jb * P], mrow[:, (jb + 1) * P:T], ACT.Exp,
                                         bias=g, scale=-1.0)
                    m.then_inc(sems["ml_decay"], 1)
                if st == 7:
                    act.wait_ge(sems["ml_out"], 4 * (h + 1))
                    if h >= 1:
                        act.wait_ge(sems["ml_normed"], h)
                    A.activation(den[:, :], ps[1][:, :], ACT.Abs).then_inc(sems["ml_abs"], 1)
                if st == 9:
                    act.wait_ge(sems["ml_num"], h + 1)
                    A.activation(ml_square[:, :], hml[:, h % 2, :], ACT.Square).then_inc(sems["ml_sq"], 1)
                if st == 10:
                    act.wait_ge(sems["ml_sum"], h + 1)
                    A.activation(den[:, :], ps[1][:, :], ACT.Sqrt, bias=eps, scale=1.0 / ML_V
                                 ).then_inc(sems["ml_root"], 1)
                if st == 12:
                    act.wait_ge(sems["ml_gated"], h + 1)
                    A.copy(a_hi[:, h, :], hml[:, h % 2, :]).then_inc(sems["ml_hi"], 1)

            def ml_hook(n):
                for h in range(ML_HEADS):
                    ml_step(h, n + ML_LEAD - ML_EVERY * h)

            for n in range(-ML_LEAD, 0):
                ml_hook(n)
            attend(MLA_G, MLA_HEADS, after=ml_hook)
            for n in range(4 * MLA_HEADS, ML_END):
                ml_hook(n)
            for j in range(KB):
                round_to(CH["WO"] + j)
                residual(3, None, j, None, None, (evac_dve, O["WO"] + j + 1 - DVE_FROM), src=mixed)
            root(8, rstd[:, :], STAT, 1.0 / D)
            for j in range(KB):
                residual(4, 3, j, col("norm_pre_mlp_2", j), a_hi, (sems["post_added"], j + 1))
            root(9, rstd[:, :], STAT, 1.0 / D, sums=(sems["post_summed"], KB))
            feed_forward("FF2", 1, lambda i, o: residual(
                5, None, i, None, None, (evac_dve, o + 1 - DVE_FROM), src=ffy))
            root(10, rstd[:, :], STAT, 1.0 / D)

        @block.vector
        def _(dve):
            V = nc.vector

            def inverse(n, t):
                dve.wait_ge(sems["stat_root"], n + 1)
                V.reciprocal(t, t).then_inc(sems["rstd_ready"], 1)
                dve.wait_ge(sems["rstd_ready"], n + 1)

            def out_lo(G):
                o, hi, lo = out_of(G)
                dve.wait_ge(sems["o_hi"], G + 1)
                V.tensor_tensor(lo, o, hi.bitcast(F32), ALU.subtract).then_inc(sems["o_ready"], 1)

            def attend(G0, n_heads, hook=None):
                n_units = 4 * n_heads

                def mask(n):
                    U, G, qb = 4 * G0 + n, G0 + n // 4, n % 4
                    b = U % 2
                    dve.wait_ge(sems["s_ready"], U + 1)
                    if U >= 2:
                        dve.wait_ge(sems["p_ready"], U - 1)
                    r = slice(0, keys_of(G, qb))
                    o = ps[4 + b][:, r]
                    V.tensor_tensor_reduce(o, o, bias_of(G, qb), -scale_of(G), -TAKEN,
                                           ALU.add, ALU.min, negmax[:, b:b + 1]).then_inc(sems["s_masked"], 1)

                def normalise(n):
                    U, G, qb = 4 * G0 + n, G0 + n // 4, n % 4
                    b = U % 2
                    dve.wait_ge(sems["p_ready"], U + 1)
                    p = probs[:, b, 0:keys_of(G, qb)]
                    V.reciprocal(rowinv[:, b:b + 1], rowsum[:, b:b + 1]).then_inc(sems["p_inv"], 1)
                    dve.wait_ge(sems["p_inv"], U + 1)
                    V.tensor_scalar(p, p, rowinv[:, b:b + 1], None, ALU.mult).then_inc(sems["p_scaled"], 1)

                mask(0)
                mask(1)
                for n in range(n_units):
                    normalise(n)
                    if n + 2 < n_units:
                        mask(n + 2)
                    if hook is not None:
                        hook(n)
                    if n % 4 == 0 and n >= 4:
                        out_lo(G0 + n // 4 - 1)
                out_lo(G0 + n_heads - 1)

            def split_x(k):
                dve.wait_ge(sems["start_hi"], KB + k + 1)
                V.tensor_tensor(a_lo[:, k, :], res[:, k, :], a_hi[:, k, :].bitcast(F32), ALU.subtract
                                ).then_inc(sems["start_ready"], 1)

            dve.wait_ge(consts_landed, 32)
            V.tensor_tensor(g2g[:, :], col("norm_final_g", 0, KB), col("norm_pre_mix_2", 0, KB), ALU.mult
                            ).then_inc(sems["gains_ready"], 1)
            for k in range(KB):
                dve.wait_ge(sems["start_hi"], k + 1)
                V.scalar_tensor_tensor(out=mem_lo[:, k, :], in0=mem_raw[:, k, :], scalar=col("norm_mem_g", k),
                                       in1=mem_hi[:, k, :].bitcast(F32), op0=ALU.mult, op1=ALU.subtract
                                       ).then_inc(sems["start_ready"], 1)
            for k in range(1, KB):
                dve.wait_ge(sems["squares"], k + 1)
                if k >= 2:
                    dve.wait_ge(sems["squares_added"], k - 1)
                V.tensor_tensor(x_sq[:, 0, :], x_sq[:, 0, :], x_sq[:, k, :], ALU.add).then_inc(sems["squares_added"], 1)
            inverse(0, x_rstd[:, :])
            for k in range(KB):
                V.scalar_tensor_tensor(out=res[:, k, :], in0=res[:, k, :], scalar=col("norm_mix_g", k),
                                       in1=x_rstd[:, :], op0=ALU.mult, op1=ALU.mult).then_inc(sems["start_scaled"], 1)
                if k >= 1:
                    split_x(k - 1)
            split_x(KB - 1)
            V.tensor_tensor(mem_sq[:, :, :], mem_raw[:, :, :], mem_raw[:, :, :], ALU.mult).then_inc(sems["mem_squared"], 1)
            dve.wait_ge(sems["mem_squared"], 1)
            for n, half in enumerate((4, 2, 1)):
                V.tensor_tensor(mem_sq[:, 0:half, :], mem_sq[:, 0:half, :], mem_sq[:, half:2 * half, :], ALU.add
                                ).then_inc(sems["mem_added"], 1)
                dve.wait_ge(sems["mem_added"], n + 1)
            inverse(1, mem_rstd[:, :])
            dve.wait_ge(evac_act, O["QI"])
            for h in range(XH):
                V.tensor_tensor(kxT[:, h, :], kxT[:, h, :], mem_rstd[:, 0:M], ALU.mult).then_inc(sems["mem_scaled"], 1)
            for b in range(MB):
                V.tensor_scalar(vx[:, b, :], vx[:, b, :], mem_rstd[:, M + b:M + b + 1], None, ALU.mult
                                ).then_inc(sems["mem_scaled"], 1)
            dve.wait_ge(sems["wi_turned"], 1)
            V.tensor_copy(wiT[:, :, :], ps[5][:, 0:TB * IDX_HEADS].rearrange("p (t h) -> p t h", t=TB)
                          ).then_inc(sems["wi_copied"], 1)
            dve.wait_ge(sems["wi_copied"], 1)
            for n in range(3 * IDX_HEADS):
                qb, h = 1 + n // IDX_HEADS, n % IDX_HEADS
                s, r, w = score[:, qb, 0:(qb + 1) * P], relu[:, n % 2, 0:(qb + 1) * P], wiT[:, qb, h:h + 1]
                dve.wait_ge(sems["relu_ready"], n + 1)
                if h == 0:
                    V.tensor_scalar(s, r, w, None, ALU.mult).then_inc(sems["score_added"], 1)
                else:
                    dve.wait_ge(sems["score_added"], n)
                    V.scalar_tensor_tensor(out=s, in0=r, scalar=w, in1=s, op0=ALU.mult, op1=ALU.add
                                           ).then_inc(sems["score_added"], 1)
            for qb in range(1, TB):
                dve.wait_ge(sems["score_added"], 3 * IDX_HEADS)
                s = score[:, qb, qb * P:(qb + 1) * P]
                V.tensor_tensor(s, s, con("bias", P, T - P), ALU.add).then_inc(sems["score_masked"], 1)
            steps = 0
            dve.wait_ge(sems["score_masked"], TB - 1)
            for _ in range(TOPK // 8):
                for b in range(1, TB):
                    if steps >= 3:
                        dve.wait_ge(sems["topk_step"], steps - 2)
                    V.max(top8[:, b - 1, :], score[:, b, 0:(b + 1) * P]).then_inc(sems["topk_step"], 1)
                    steps += 1
                for b in range(1, TB):
                    dve.wait_ge(sems["topk_step"], steps - 2)
                    s = score[:, b, 0:(b + 1) * P]
                    V.match_replace(s, top8[:, b - 1, :], s, TAKEN).then_inc(sems["topk_step"], 1)
                    steps += 1
            dve.wait_ge(sems["topk_step"], steps)
            for b in range(1, TB):
                s = score[:, b, 0:(b + 1) * P]
                V.tensor_scalar(s, s, TAKEN_BELOW, MASKED, ALU.is_gt, ALU.mult).then_inc(sems["topk_done"], 1)
            dve.wait_ge(sems["pad_zeroed"], 1)
            with dve.Fori(0, KB // 2) as r:
                def blk(t, e, a, b):
                    return t[:, bass.ds(2 * r + e, 1), a:b].rearrange("p o n -> p (o n)")

                for e in range(2):
                    dve.wait_ge(evac_act, 4 * r + (O["C"] + 2 * e + 2))
                    u = blk(conv_in, e, PAD, PAD + T)
                    V.tensor_tensor(u, u, blk(conv_io, e, 0, T), ALU.mult).then_inc(sems["gated"], 1)
                for k in range(TAPS):
                    for e in range(2):
                        acc = ps[4 + e][:, :]
                        u = blk(conv_in, e, k, k + T)
                        w = cols[:, bass.ds((2 * r + e) * TAPS + (COL["conv_w"] + k), 1)]
                        if k == 0:
                            dve.wait_ge(sems["gated"], 2 * r + (e + 1))
                            V.tensor_scalar(acc, u, w, cols[:, bass.ds(2 * r + (COL["conv_b"] + e), 1)],
                                            ALU.mult, ALU.add).then_inc(sems["tap_done"], 1)
                            continue
                        dve.wait_ge(sems["tap_done"], 2 * (TAPS - 1) * r + (2 * (k - 1) + e + 1))
                        last = k == TAPS - 1
                        V.scalar_tensor_tensor(out=blk(conv_io, e, 0, T) if last else acc, in0=u, scalar=w,
                                               in1=acc, op0=ALU.mult, op1=ALU.add
                                               ).then_inc(sems["conv_done"] if last else sems["tap_done"], 1)

            def gate_conv(j):
                dve.wait_ge(chunk_done, CH["CO"] + j + 1)
                V.tensor_tensor(gate_c[:, j, :], ps[j % 2][:, :], gate_c[:, j, :], ALU.mult).then_inc(evac_dve, 1)

            def dsa_hook(n):
                beside = (n - 2) // 2 - 2 * (HEADS - 2)
                if n % 2 == 1 and beside >= 0:
                    gate_conv(beside)
                if n < LN_MEAN_AT:
                    for k in range(max(2 * n, 1), 2 * n + 2):
                        if k >= 2:
                            dve.wait_ge(sems["ln_added"], k - 1)
                        dve.wait_ge(sems["conv_done"], KB)
                        V.tensor_tensor(ln_rstd[:, :], conv_io[:, 0, :] if k == 1 else ln_rstd[:, :],
                                        conv_io[:, k, :], ALU.add).then_inc(sems["ln_added"], 1)
                if 0 <= n - LN_MEAN_AT < KB // 2:
                    dve.wait_ge(sems["ln_sum"], 1)
                    for k in range(2 * (n - LN_MEAN_AT), 2 * (n - LN_MEAN_AT) + 2):
                        V.scalar_tensor_tensor(out=conv_io[:, k, :], in0=ps[3][:, :], scalar=-1.0 / D,
                                               in1=conv_io[:, k, :], op0=ALU.mult, op1=ALU.add
                                               ).then_inc(sems["centred"], 1)
                if LN_MEAN_AT < n <= LN_MEAN_AT + KB // 2:
                    for k in range(max(2 * (n - LN_MEAN_AT) - 2, 1), 2 * (n - LN_MEAN_AT)):
                        dve.wait_ge(sems["ln_squared"], k + 1)
                        if k >= 2:
                            dve.wait_ge(sems["ln_added"], KB - 1 + k - 1)
                        V.tensor_tensor(ln_rstd[:, :], ln_sq[:, 0, :] if k == 1 else ln_rstd[:, :],
                                        ln_sq[:, k, :], ALU.add).then_inc(sems["ln_added"], 1)
                if n == LN_VAR_AT + 1:
                    dve.wait_ge(sems["ln_root"], 1)
                    V.reciprocal(ln_rstd[:, :], ln_rstd[:, :]).then_inc(sems["ln_inv"], 1)
                    dve.wait_ge(sems["ln_inv"], 1)
                if 0 <= n - LN_VAR_AT - 1 < KB // 2:
                    for k in range(2 * (n - LN_VAR_AT - 1), 2 * (n - LN_VAR_AT)):
                        V.scalar_tensor_tensor(out=conv_io[:, k, :], in0=conv_io[:, k, :],
                                               scalar=col("conv_ln_g", k), in1=ln_rstd[:, :],
                                               op0=ALU.mult, op1=ALU.mult).then_inc(sems["ln_scaled"], 1)
                if 0 <= n - LN_SPLIT_AT < KB:
                    k = n - LN_SPLIT_AT
                    dve.wait_ge(sems["ln_hi"], k + 1)
                    V.tensor_tensor(b_lo[:, k, :], conv_io[:, k, :], b_hi[:, k, :].bitcast(F32), ALU.subtract
                                    ).then_inc(sems["convact_ready"], 1)

            attend(DSA_G, HEADS, dsa_hook)
            for j in range(CO_BESIDE, KB):
                gate_conv(j)
            for j in range(KB):
                dve.wait_ge(chunk_done, CH["AO"] + j + 1)
                V.tensor_tensor(gate_a[:, j, :], ps[(O["AO"] + j) % RING][:, :], gate_a[:, j, :], ALU.mult
                                ).then_inc(evac_dve, 1)
                dve.wait_ge(evac_dve, O["AO"] + j + 1 - DVE_FROM)
                V.tensor_tensor(gate_c[:, j, :], gate_c[:, j, :], gate_a[:, j, :], ALU.add).then_inc(sems["mix_added"], 1)
                dve.wait_ge(sems["mix_hi"], j + 1)
                V.tensor_tensor(a_lo[:, j, :], gate_c[:, j, :], a_hi[:, j, :].bitcast(F32), ALU.subtract
                                ).then_inc(sems["mix_ready"], 1)

            def add_square(e, i):
                n = KB * (e if e < 5 else 4) + i
                dve.wait_ge(sems["res_sq"], KB * e + i + 1)
                if i == 0:
                    V.tensor_copy(ssq[:, :], sq[:, 0, :]).then_inc(sems["ssq_added"], 1)
                else:
                    dve.wait_ge(sems["ssq_added"], n)
                    V.tensor_tensor(ssq[:, :], ssq[:, :], sq[:, i % 2, :], ALU.add).then_inc(sems["ssq_added"], 1)

            def split_residual(hset, i, gain, hi, lo):
                dve.wait_ge(sems["hg_hi"], KB * (min(hset, 3)) + i + 1)
                V.scalar_tensor_tensor(out=lo[:, i, :], in0=res[:, i, :], scalar=gain,
                                       in1=hi[:, i, :].bitcast(F32), op0=ALU.mult, op1=ALU.subtract
                                       ).then_inc(sems["hg_ready"], 1)

            def accumulate(o, t, i, own=True):
                if own:
                    dve.wait_ge(evac_dve, o - DVE_FROM)
                V.tensor_tensor(t[:, i, :], ps_of(o), t[:, i, :], ALU.add).then_inc(evac_dve, 1)

            def ps_of(o):
                return ps[o % RING][:, :]

            dve.wait_ge(x_again, 16)
            for j in range(KB):
                dve.wait_ge(chunk_done, CH["MX"] + j + 1)
                accumulate(O["MX"] + j, res, j, False)
                split_residual(0, j, col("norm_x_g", j), b_hi, b_lo)
                add_square(0, j)
            inverse(2, rstd[:, :])

            def x_queries(h):
                dve.wait_ge(chunk_done, CH["QX"] + h + 1)
                V.tensor_tensor(qxT[:, h, :], ps[(3, 0, 1, 3)[h]][:, :], rstd[:, :], ALU.mult).then_inc(evac_dve, 1)

            def x_hook(n):
                if n % 4 == 1 and n // 4 + 1 < XH:
                    x_queries(n // 4 + 1)

            x_queries(0)
            attend(X_G, XH, x_hook)
            for j in range(KB):
                if j % 2 == 0:
                    dve.wait_ge(sems["ox_first"], j // 2 + 1)
                else:
                    dve.wait_ge(chunk_done, CH["OX"] + j // 2 + 1)
                accumulate(O["OX"] + j, res, j)
                split_residual(1, j, col("norm_ffn_g", j), a_hi, a_lo)
                add_square(1, j)
            inverse(3, rstd[:, :])

            def ff_group(name, s, g, dst, last=None, beside=None):
                c0, o0 = CH[name], O[name]
                for j in range(2 * KB):
                    if beside is not None:
                        beside(j)
                    dve.wait_ge(chunk_done, g * 16 + (c0 + j + 1))
                    o = g * 16 + (o0 + j)
                    bank = ps[(o0 + j) % RING][:, :]
                    if j < KB:
                        f = g * KB + (32 * s + j)
                        if not isinstance(f, int) or f >= 2:
                            if not (s == 0 and j < 2 and not isinstance(f, int)):
                                dve.wait_ge(sems["f_sq"], f - 1)
                        V.scalar_tensor_tensor(out=ff_t[:, j % 2, :], in0=bank, scalar=0.0, in1=rstd[:, :],
                                               op0=ALU.max, op1=ALU.mult).then_inc(evac_dve, 1)
                        dve.wait_ge(sems["f_hi"], f + 1)
                        V.tensor_tensor(b_lo[:, j, :], ff_f[:, j % 2, :], b_hi[:, j, :].bitcast(F32), ALU.subtract
                                        ).then_inc(sems["f_ready"], 1)
                    else:
                        i = j - KB
                        if s == 1 and isinstance(g, int) and g == 0:
                            V.tensor_copy(dst[:, i, :], bank).then_inc(evac_dve, 1)
                        else:
                            dve.wait_ge(evac_dve, g * 16 + (o0 + j - DVE_FROM))
                            V.tensor_tensor(dst[:, i, :], bank, dst[:, i, :], ALU.add).then_inc(evac_dve, 1)
                        if last is not None:
                            last(i)

            def feed_forward(name, s, dst, last, beside=None):
                ff_group(name, s, 0, dst, beside=beside)
                with dve.Fori(1, FF_GROUPS - 1) as g:
                    ff_group(name, s, g, dst)
                ff_group(name, s, FF_GROUPS - 1, dst, last)

            def last_ff1(i):
                split_residual(2, i, g2g[:, i:i + 1], a_hi, a_lo)
                add_square(2, i)
                dve.wait_ge(sems["res_sqg"], i + 1)
                if i == 0:
                    V.tensor_copy(ssq_g[:, :], sq_g[:, :]).then_inc(sems["ssqg_added"], 1)
                else:
                    dve.wait_ge(sems["ssqg_added"], i)
                    V.tensor_tensor(ssq_g[:, :], ssq_g[:, :], sq_g[:, :], ALU.add).then_inc(sems["ssqg_added"], 1)

            rr = slice(NOPE, NOPE + ROPE)
            ang, kq = angle[rr, 0, :], angle[rr, 1, :]
            cosT, sinT = ropet[rr, 0, :], ropet[rr, 1, :]

            def stepwise(ins, n):
                ins.then_inc(sems["rope_step"], 1)
                dve.wait_ge(sems["rope_step"], n)

            def rotary(j):
                if j == KB:
                    dve.wait_ge(sems["late_landed"], 32)
                    stepwise(V.tensor_copy(ang, posi[rr, :]), 1)
                    stepwise(V.tensor_scalar(ang, ang, con("misc", 1, INV_COL, NOPE, NOPE + ROPE), None, ALU.mult), 2)
                if KB < j < KB + 3:
                    dst, turn_off, off = ((sinT, 0.0, 0.0), (cosT, 0.25, float(np.pi / 2)))[j - KB - 1]
                    n = 2 + 6 * (j - KB - 1)
                    stepwise(V.tensor_scalar(kq, ang, 1.0 / TWO_PI, turn_off, ALU.mult, ALU.add), n + 1)
                    stepwise(V.tensor_scalar(kq, kq, ROUND, ROUND, ALU.add, ALU.subtract), n + 2)
                    src = ang
                    for i, part in enumerate((PI_HI, PI_MID, PI_LO)):
                        stepwise(V.scalar_tensor_tensor(out=dst, in0=kq, scalar=-part, in1=src, op0=ALU.mult,
                                                        op1=ALU.add), n + 3 + i)
                        src = dst
                    stepwise(V.tensor_scalar(dst, dst, off, PI_SAFE, ALU.add, ALU.min), n + 6)
                    V.tensor_scalar(dst, dst, -PI_SAFE, None, ALU.max).then_inc(sems["angles"], 1)
                if j == 2 * KB - 1:
                    dve.wait_ge(sems["sines"], 2)
                    V.tensor_scalar(sinT, sinT, con("misc", 1, SIGN_COL, NOPE, NOPE + ROPE), None, ALU.mult
                                    ).then_inc(sems["rope_step"], 1)

            dve.wait_ge(sems["gains_ready"], 1)
            feed_forward("FF1", 0, res, last_ff1, rotary)
            rt = ssq
            inverse(4, rstd[:, :])
            V.tensor_tensor(sq[:, 0, :], rstd[:, :], rstd[:, :], ALU.mult).then_inc(sems["norm2"], 1)
            dve.wait_ge(sems["norm2"], 1)
            dve.wait_ge(sems["stat_ready"], 6)
            V.scalar_tensor_tensor(out=sq[:, 0, :], in0=ps[5][:, :], scalar=1.0 / D, in1=sq[:, 0, :],
                                   op0=ALU.mult, op1=ALU.mult).then_inc(sems["mean2"], 1)
            inverse(5, sq[:, 0, :])
            V.tensor_tensor(rt[:, :], sq[:, 0, :], rstd[:, :], ALU.mult).then_inc(sems["rt_done"], 1)
            dve.wait_ge(sems["rt_done"], 1)
            for i in range(2):
                dve.wait_ge(chunk_done, CH["CQ"] + i + 1)
                V.tensor_tensor(cq[:, i, :], ps_of(O["CQ"] + i), rt[:, :], ALU.mult).then_inc(evac_dve, 1)
            dve.wait_ge(chunk_done, CH["CKV"] + 1)
            V.tensor_tensor(cq[:, 2, :], ps_of(O["CKV"]), rt[:, :], ALU.mult).then_inc(evac_dve, 1)
            dve.wait_ge(chunk_done, CH["KR"] + 1)
            V.tensor_tensor(krT[:, :], ps_of(O["KR"]), rt[:, :], ALU.mult).then_inc(evac_dve, 1)
            dve.wait_ge(sems["rt_turned"], 1)
            V.tensor_copy(rtcol[:, :], ps[6][:, 0:T:P]).then_inc(sems["rt_cols"], 1)
            V.memset(qk_in[:, :, 0:ML_TAPS - 1], 0.0).then_inc(sems["qk_pad"], 1)
            dve.wait_ge(sems["qk_pad"], 1)
            taps = 0
            for j in range(4):
                dve.wait_ge(chunk_done, CH["QK"] + j + 1)
                V.tensor_tensor(qk_in[:, j, ML_TAPS - 1:], ps_of(O["QK"] + j), rt[:, :], ALU.mult
                                ).then_inc(evac_dve, 1)
                dve.wait_ge(evac_dve, O["QK"] + j + 1 - DVE_FROM)
                for k in range(ML_TAPS):
                    x, w = qk_in[:, j, k:k + T], col("conv_w_2", j * ML_TAPS + k)
                    if k == 0:
                        V.tensor_scalar(qk_ml[:, j, :], x, w, col("conv_b_2", j), ALU.mult, ALU.add
                                        ).then_inc(sems["ml_conv"], 1)
                    else:
                        dve.wait_ge(sems["ml_conv"], taps)
                        V.scalar_tensor_tensor(out=qk_ml[:, j, :], in0=x, scalar=w, in1=qk_ml[:, j, :],
                                               op0=ALU.mult, op1=ALU.add).then_inc(sems["ml_conv"], 1)
                    taps += 1
            inverse(6, cq_rstd[:, 0, :])
            inverse(7, cq_rstd[:, 1, :])
            for i in range(3):
                g = col("q_norm_2", i) if i < 2 else col("kv_norm_2")
                V.scalar_tensor_tensor(out=cq[:, i, :], in0=cq[:, i, :], scalar=g, in1=cq_rstd[:, i // 2, :],
                                       op0=ALU.mult, op1=ALU.mult).then_inc(sems["cn_scaled"], 1)
            g4 = slice(0, ML_HEADS)

            def chained(ins, n):
                ins.then_inc(sems["row_step"], 1)
                dve.wait_ge(sems["row_step"], n)

            chained(V.memset(gt[g4, 5, :], 0.0), 1)
            dve.wait_ge(sems["gate_step"], 5)
            chained(V.tensor_scalar(gt[g4, 1, :], gt[g4, 1, :], col("b_gates_2", 1, p1=ML_HEADS), 0.0,
                                    ALU.add, ALU.min), 2)
            chained(V.tensor_tensor(gt[g4, 1, :], gt[g4, 1, :], gt[g4, 2, :], ALU.subtract), 3)
            chained(V.tensor_tensor_scan(gt[g4, 3, :], gt[g4, 1, :], gt[g4, 5, :], 0.0, ALU.add, ALU.add), 4)
            chained(V.tensor_tensor(gt[g4, 0, :], gt[g4, 0, :], gt[g4, 3, :], ALU.subtract), 5)
            chained(V.tensor_tensor_scan(gt[g4, 4, :], gt[g4, 5, :], gt[g4, 0, :], 0.0, ALU.add, ALU.max), 6)
            V.tensor_tensor(gt[g4, 3, :], gt[g4, 3, :], gt[g4, 4, :], ALU.add).then_inc(sems["gates_done"], 1)
            for i in range(3):
                dve.wait_ge(sems["cn_hi_done"], i + 1)
                V.tensor_tensor(cn_lo[:, i, :], cq[:, i, :], cn_hi[:, i, :].bitcast(F32), ALU.subtract
                                ).then_inc(sems["cn_ready"], 1)
            dve.wait_ge(sems["rt_cols"], 1)
            for b in range(TB):
                dve.wait_ge(chunk_done, CH["VM"] + 4)
                V.tensor_scalar(v_ml[:, b, :], ps_of(O["VM"] + b), rtcol[:, b:b + 1], None, ALU.mult
                                ).then_inc(evac_dve, 1)
            dve.wait_ge(sems["kr_moved"], 1)
            dve.wait_ge(sems["rope_step"], 15)
            chained(V.tensor_tensor(rot[rr, 0, :], krT[rr, :], cosT, ALU.mult), 7)
            chained(V.tensor_tensor(rot[rr, 1, :], rot[rr, 1, :], sinT, ALU.mult), 8)
            chained(V.tensor_tensor(krT[rr, :], rot[rr, 0, :], rot[rr, 1, :], ALU.add), 9)
            for j in range(4):
                dve.wait_ge(chunk_done, CH["OM"] + j + 1)
                V.tensor_tensor(ogate[:, j, :], ps_of(O["OM"] + j), rt[:, :], ALU.mult).then_inc(evac_dve, 1)
            for h in range(MLA_HEADS):
                bank = ps_of(O["UQ"] + h)
                dve.wait_ge(sems["q_moved"], h + 1)
                V.tensor_tensor(qh[rr, h, :], bank[rr, :], cosT, ALU.mult).then_inc(evac_dve, 1)
                V.tensor_tensor(rot[rr, h % 2, :], rot[rr, h % 2, :], sinT, ALU.mult).then_inc(sems["rope_half"], 1)
                dve.wait_ge(evac_dve, O["UQ"] + h + 1 - DVE_FROM)
                dve.wait_ge(sems["rope_half"], h + 1)
                V.tensor_tensor(qh[rr, h, :], qh[rr, h, :], rot[rr, h % 2, :], ALU.add).then_inc(sems["rope_q"], 1)
            dve.wait_ge(sems["kv_keys_done"], 1)
            for j in range(4):
                dve.wait_ge(sems["kv_odd"], j + 1)
                V.tensor_copy(kh[0:NOPE, 2 * j, :], ps_of(O["UKV"] + j)[0:NOPE, :]).then_inc(evac_dve, 1)
            dve.wait_ge(chunk_done, CH["UKV"] + 1)
            for j in range(TB):
                V.tensor_copy(v_mla[:, j, :], ps_of(O["UKV"] + 4 + j)).then_inc(evac_dve, 1)
            dve.wait_ge(sems["rope_q"], MLA_HEADS)
            V.tensor_copy(kh[rr, 0, :], krT[rr, :]).then_inc(sems["rope_done"], 1)
            dve.wait_ge(sems["gates_turned"], 1)
            V.tensor_copy(gcols[:, :, :], ps[7][:, 0:TB * ML_HEADS].rearrange("p (t h) -> p t h", t=TB)
                          ).then_inc(sems["gcols_done"], 1)

            def ml_step(h, st):
                hm = hml[:, h % 2, :]
                if st == 1:
                    dve.wait_ge(sems["ml_mrow"], h + 1)
                    if h >= 1:
                        dve.wait_ge(sems["ml_decay"], TB * h)
                    for b in range(TB):
                        V.scalar_tensor_tensor(out=negm_diag[:, b, :], in0=mrow[:, b * P:(b + 1) * P], scalar=-1.0,
                                               in1=con("maskT", P), op0=ALU.mult, op1=ALU.add
                                               ).then_inc(sems["ml_diag"], 1)
                if 3 <= st < 3 + TB:
                    jb = st - 3
                    u = 4 * h + jb
                    dve.wait_ge(sems["ml_s"], u + 1)
                    dve.wait_ge(sems["ml_decay"], u + 1)
                    if u >= 2:
                        dve.wait_ge(sems["ml_out"], u - 1)
                    w = slice(0, T - jb * P)
                    V.scalar_tensor_tensor(out=sT[:, u % 2, w], in0=ps[3][:, w], scalar=float(ML_QK) ** -0.5,
                                           in1=decay[:, u % 2, w], op0=ALU.mult, op1=ALU.mult
                                           ).then_inc(sems["ml_sT"], 1)
                if st == 8:
                    dve.wait_ge(sems["ml_abs"], h + 1)
                    dve.wait_ge(sems["ml_fl"], h + 1)
                    V.tensor_tensor(den[:, :], den[:, :], floor_[:, :], ALU.max).then_inc(sems["ml_floor"], 1)
                    dve.wait_ge(sems["ml_floor"], h + 1)
                    V.reciprocal(den[:, :], den[:, :]).then_inc(sems["ml_inv"], 1)
                    dve.wait_ge(sems["ml_inv"], 2 * h + 1)
                    V.tensor_tensor(hm, ps[0][:, :], den[:, :], ALU.mult).then_inc(sems["ml_num"], 1)
                if st == 11:
                    dve.wait_ge(sems["ml_root"], h + 1)
                    V.reciprocal(den[:, :], den[:, :]).then_inc(sems["ml_inv"], 1)
                    dve.wait_ge(sems["ml_inv"], 2 * h + 2)
                    V.scalar_tensor_tensor(out=hm, in0=hm, scalar=col("ml_head_norm_2", h), in1=den[:, :],
                                           op0=ALU.mult, op1=ALU.mult).then_inc(sems["ml_normed"], 1)
                    dve.wait_ge(sems["ml_normed"], h + 1)
                    dve.wait_ge(sems["o_gated"], h + 1)
                    V.tensor_tensor(hm, hm, ogate[:, h, :], ALU.mult).then_inc(sems["ml_gated"], 1)
                if st == 13:
                    dve.wait_ge(sems["ml_hi"], h + 1)
                    V.tensor_tensor(a_lo[:, h, :], hm, a_hi[:, h, :].bitcast(F32), ALU.subtract
                                    ).then_inc(sems["ml_ready"], 1)

            def ml_hook(n):
                for h in range(ML_HEADS):
                    ml_step(h, n + ML_LEAD - ML_EVERY * h)
                if n >= 0 and n % 4 == 0 and n // 4 + 1 < MLA_HEADS:
                    V.tensor_copy(kh[rr, n // 4 + 1, :], krT[rr, :]).then_inc(sems["rope_done"], 1)
                if 0 <= n < KB:
                    V.scalar_tensor_tensor(out=res[:, n, :], in0=res[:, n, :], scalar=col("norm_final_g", n),
                                           in1=rstd[:, :], op0=ALU.mult, op1=ALU.mult).then_inc(sems["x2_done"], 1)

            for n in range(-ML_LEAD, 0):
                ml_hook(n)
            attend(MLA_G, MLA_HEADS, ml_hook)
            for n in range(4 * MLA_HEADS, ML_END):
                ml_hook(n)
            for j in range(KB):
                dve.wait_ge(chunk_done, CH["WO"] + j + 1)
                V.tensor_copy(mixed[:, j, :], ps_of(O["WO"] + j)).then_inc(evac_dve, 1)
                add_square(3, j)
            inverse(8, rstd[:, :])
            for j in range(KB):
                V.scalar_tensor_tensor(out=mixed[:, j, :], in0=mixed[:, j, :], scalar=col("norm_post_mix_2", j),
                                       in1=rstd[:, :], op0=ALU.mult, op1=ALU.mult).then_inc(sems["post_scaled"], 1)
                dve.wait_ge(sems["post_scaled"], j + 1)
                V.tensor_tensor(res[:, j, :], res[:, j, :], mixed[:, j, :], ALU.add).then_inc(sems["post_added"], 1)
                if j >= 1:
                    split_residual(3, j - 1, col("norm_pre_mlp_2", j - 1), a_hi, a_lo)
            split_residual(3, KB - 1, col("norm_pre_mlp_2", KB - 1), a_hi, a_lo)
            inverse(9, rstd[:, :])
            feed_forward("FF2", 1, ffy, lambda i: add_square(5, i))
            inverse(10, rstd[:, :])
            for j in range(KB):
                V.scalar_tensor_tensor(out=ffy[:, j, :], in0=ffy[:, j, :], scalar=col("norm_post_mlp_2", j),
                                       in1=rstd[:, :], op0=ALU.mult, op1=ALU.mult).then_inc(sems["y_scaled"], 1)
                dve.wait_ge(sems["y_scaled"], j + 1)
                V.tensor_tensor(y_out[:, j, :], ffy[:, j, :], res[:, j, :], ALU.add).then_inc(sems["y_written"], 1)


def _columns(v, n):
    return np.ascontiguousarray(np.reshape(v, (n, P)).T)


def _block(w, cols):
    s = w[:, cols]
    return s.reshape(-1, P, s.shape[1]).transpose(1, 0, 2).reshape(P, -1)


def _stream(i):
    w1, w2 = i["w_in"][0], i["w_in_2"][0]
    kv, chunks = i["wx_kv"][0], []

    def blocks(w, n, c0=0):
        chunks.extend(_block(w, slice(c0 + P * j, c0 + P * (j + 1))) for j in range(n))

    def rows(w, c0):
        chunks.extend(_block(w[2 * P * t:2 * P * (t + 1)], slice(c0, c0 + T)) for t in range(4))

    ca, cg, q0, k0, v0 = 0, D, 2 * D, 3 * D, 4 * D
    qi0 = 5 * D
    ki0 = qi0 + IDX_HEADS * IDX_DIM
    wi0 = ki0 + IDX_DIM
    g0 = wi0 + IDX_HEADS
    blocks(kv, 4)
    rows(kv, T)
    blocks(w1, 4, qi0)
    ki = np.zeros((D, P), w1.dtype)
    ki[:, 0:IDX_DIM + IDX_HEADS] = w1[:, ki0:g0]
    blocks(ki, 1)
    for j in range(KB):
        blocks(w1, 1, cg + P * j)
        blocks(w1, 1, ca + P * j)
    blocks(w1, 16, g0)
    rows(w1, v0)
    rows(w1, v0 + T)
    for h in range(HEADS):
        blocks(w1, 1, q0 + P * h)
        blocks(w1, 1, k0 + P * h)
    blocks(i["w_conv_out"][0], KB)
    blocks(i["w_attn_out"][0], KB)
    blocks(i["w_mix_out"][0], KB)
    blocks(i["wx_q"][0], XH)
    wo = i["wx_o"][0]
    for j in range(XH):
        chunks.append(np.concatenate([_block(wo, slice(P * (2 * j + r), P * (2 * j + r + 1))) for r in range(2)], 1))

    def feed_forward(up, down):
        for g in range(FF_GROUPS):
            blocks(up, KB, D * g)
            blocks(down[D * g:D * (g + 1)], KB)

    feed_forward(i["w_ff1"][0], i["w_ff2"][0])
    o0 = 2 * ML_HEADS * ML_QK
    o1 = o0 + ML_HEADS * ML_V
    o2 = o1 + ML_HEADS * ML_V
    o3 = o2 + 2 * ML_HEADS
    o4 = o3 + 2 * P
    o5 = o4 + P
    blocks(w2, 2, o3)
    blocks(w2, 1, o4)
    kr = np.zeros((D, P), w2.dtype)
    kr[:, 0:ML_HEADS] = w2[:, o2:o2 + ML_HEADS]
    kr[:, 32:32 + ML_HEADS] = w2[:, o2 + ML_HEADS:o3]
    kr[:, 64:96] = w2[:, o5:]
    kr[:, 96:112] = w2[:, o5 + ROPE // 2:]
    kr[:, 112:128] = w2[:, o5:o5 + ROPE // 2]
    blocks(kr, 1)
    blocks(w2, 4)
    rows(w2, o0)
    blocks(w2, 4, o1)
    uq = i["w_uq_2"][0]
    per = NOPE + ROPE
    heads = []
    for h in range(MLA_HEADS):
        w = uq[:, per * h:per * (h + 1)]
        heads.append(_block(np.concatenate([w, w[:, NOPE + ROPE // 2:], w[:, NOPE:NOPE + ROPE // 2]], 1),
                            slice(0, P)))
    chunks.append(np.concatenate(heads[0:4], 1))
    chunks.append(np.concatenate(heads[4:8], 1))
    ukv = i["w_ukv_2"][0].reshape(P, MLA_HEADS, NOPE + MLA_V)
    chunks.append(np.concatenate([ukv[:, :, 0:NOPE].reshape(P, -1), ukv[:, :, NOPE:].reshape(P, -1)], 1))
    blocks(i["w_out_2"][0], KB)
    feed_forward(i["w_up_2"][0], i["w_down_2"][0])
    assert len(chunks) == CHUNKS
    return np.stack(chunks)


def _packed(i):
    c = np.zeros((P, NCOLS), np.float32)
    for name, n in COLS:
        if name == "conv_w":
            c[:, COL[name]:COL[name] + n] = i[name][0].reshape(TAPS, KB, P).transpose(2, 1, 0).reshape(P, n)
        elif name == "conv_w_2":
            c[:, COL[name]:COL[name] + n] = i[name][0].reshape(ML_TAPS, 4, P).transpose(2, 1, 0).reshape(P, n)
        elif name == "b_gates_2":
            c[0:ML_HEADS, COL[name]:COL[name] + 2] = i[name][0].reshape(2, ML_HEADS).T
        else:
            c[:, COL[name]:COL[name] + n] = _columns(i[name], n)
    return c


def _constants():
    c = np.zeros((P, NCONST), np.float32)
    c[:, CON["ident"]:CON["ident"] + P] = np.eye(P, dtype=np.float32)
    c[:, CON["ones"]:CON["ones"] + P] = 1.0
    r = np.arange(P)
    later = np.where(r[None, :] > r[:, None], np.float32(MASKED), np.float32(0))
    c[:, CON["bias"] + T - P:CON["bias"] + T] = later
    c[:, CON["maskT"]:CON["maskT"] + P] = later.T
    misc = CON["misc"]
    c[:, misc + EPS_COL] = EPS
    inv = (1.0 / (np.float32(10000.0) ** (np.arange(0, ROPE, 2, dtype=np.float32) / ROPE))).astype(np.float32)
    c[NOPE:NOPE + ROPE, misc + INV_COL] = np.concatenate([inv, inv])
    c[NOPE:NOPE + ROPE, misc + SIGN_COL] = np.concatenate([-np.ones(ROPE // 2), np.ones(ROPE // 2)])
    c[:, misc + ONE_COL] = 1.0
    s = np.zeros((ML_HEADS, ML_HEADS * P), np.float32)
    for h in range(ML_HEADS):
        s[h, h * P:(h + 1) * P] = 1.0
    return c, s


def _feature_major(a, n):
    return np.ascontiguousarray(a.reshape(n, KB, P).transpose(2, 1, 0))


def kernel(**inputs):
    import concourse.bacc as bacc
    from concourse.bass_utils import run_bass_kernel_spmd as run

    i = {k: np.asarray(v) for k, v in inputs.items()}
    consts, sel = _constants()
    arrays = {
        "in_stream": _stream(i),
        "in_xT": _feature_major(i["x"], T),
        "in_memT": _feature_major(i["mem"], M),
        "in_cols": _packed(i),
        "in_consts": consts,
        "in_sel": sel,
        "in_positions": np.ascontiguousarray(i["positions_2"].reshape(1, T)),
    }
    nc = bacc.Bacc("TRN2", target_bir_lowering=False, num_devices=1, dynamic_dma_scratch_size=1024)
    args = [nc.dram_tensor(n, a.shape, mybir.dt.from_np(a.dtype), kind="ExternalInput").ap()
            for n, a in arrays.items()]
    out = nc.dram_tensor("out_y", (P, KB, T), F32, kind="ExternalOutput").ap()
    program(nc, *args, out)
    r = run(nc, [arrays], core_ids=[0])
    y = r.results[0]["out_y"]
    return np.ascontiguousarray(y.transpose(2, 1, 0)).reshape(1, T, D)
```

```python
from contextlib import ExitStack

import numpy as np

import concourse.bass as bass
from concourse import mybir

ALU = mybir.AluOpType
ACT = mybir.ActivationFunctionType
AX = mybir.AxisListType
F32 = mybir.dt.float32
F32R = mybir.dt.float32r
I32 = mybir.dt.int32

P = 128
D = 1024
KB = D // P
T = 512
TB = T // P
M = 256
MB = M // P
EPS = 1e-6
TAPS = 31
PAD = TAPS - 1
HEADS = 8
IDX_HEADS = 8
IDX_DIM = 64
TOPK = 128
XH = 4
ML_HEADS = 4
ML_QK = 64
ML_V = 128
ML_TAPS = 4
MLA_HEADS = 8
NOPE = 64
ROPE = 32
MLA_V = 64
FF_GROUPS = 4
RING = 4
AHEAD = 3
X_FILLED = (0, 2, 3, 5, 6, 7, 8, 9)
POOL_ADDS = (0, 2, 4)
MASKED = -3.0e38
TAKEN = -3.4e38
TAKEN_BELOW = -3.2e38

STAGES = [("MK", 4), ("MV", 4), ("QI", 4), ("KI", 1), ("C", 16), ("G", 16), ("V", 8), ("ATT", 16),
          ("CO", 8), ("AO", 8), ("MX", 8), ("QX", 4), ("OX", 4), ("FF1", 64), ("CQ", 2), ("CKV", 1),
          ("KR", 1), ("QK", 4), ("VM", 4), ("OM", 4), ("UQ", 2), ("UKV", 1), ("WO", 8), ("FF2", 64)]
CH = {}
_n = 0
for _name, _count in STAGES:
    CH[_name] = _n
    _n += _count
CHUNKS = _n
OUTS = [("MK", 4), ("MV", 2), ("QI", 4), ("KI", 1), ("C", 16), ("G", 16), ("V", 8), ("ATT", 16),
        ("CO", 8), ("AO", 8), ("MX", 8), ("QX", 4), ("OX", 8), ("FF1", 64), ("CQ", 2), ("CKV", 1),
        ("KR", 1), ("QK", 4), ("VM", 4), ("OM", 4), ("UQ", 8), ("UKV", 8), ("WO", 8), ("FF2", 64)]
O = {}
_n = 0
for _name, _count in OUTS:
    O[_name] = _n
    _n += _count
DVE_FROM = O["CO"]

COLS = [("norm_mix_g", 8), ("b_gate", 16), ("conv_w", KB * TAPS), ("conv_b", 8), ("conv_ln_g", 8),
        ("conv_ln_b", 8), ("norm_x_g", 8), ("norm_mem_g", 8), ("norm_ffn_g", 8), ("norm_final_g", 8),
        ("norm_pre_mix_2", 8), ("conv_w_2", 4 * ML_TAPS), ("conv_b_2", 4), ("ml_head_norm_2", 4),
        ("q_norm_2", 2), ("kv_norm_2", 1), ("norm_post_mix_2", 8), ("norm_pre_mlp_2", 8),
        ("norm_post_mlp_2", 8), ("b_gates_2", 2)]
COL = {}
_n = 0
for _name, _count in COLS:
    COL[_name] = _n
    _n += _count
NCOLS = _n
CONSTS = [("ident", P), ("ones", P), ("bias", T), ("maskT", P), ("misc", 8)]
CON = {}
_n = 0
for _name, _count in CONSTS:
    CON[_name] = _n
    _n += _count
NCONST = _n
EPS_COL, INV_COL, SIGN_COL, ONE_COL = 0, 1, 2, 3
TWO_PI = float(2 * np.pi)
PI_SAFE = float(np.nextafter(np.float32(np.pi), np.float32(0)))
PI_HI = 6.28125
PI_MID = float(np.float32(np.floor((TWO_PI - PI_HI) * 2.0 ** 21) / 2.0 ** 21))
PI_LO = float(np.float32(TWO_PI - PI_HI - PI_MID))
ROUND = 12582912.0


SEMAPHORES = """
angles centred cn_hi_done cn_ready cn_scaled conv_done convact_ready cq_squared f_hi f_ready f_sq
floors_done gains_ready gate_step gated gates_done gates_turned gcols_done hg_hi hg_ready ki_split
kr_moved kv_keys_done kv_odd kv_values_done late_landed ln_added ln_hi ln_inv ln_root ln_scaled ln_silu ln_squared
ln_sum logits_ready mean2 mem_added mem_scaled mem_squared mix_added mix_hi mix_ready ml_conv ml_decay
ml_den ml_diag ml_floor ml_gated ml_hi ml_inv ml_mrow ml_num ml_out ml_ready ml_root ml_rows ml_s ml_sT
ml_scale ml_spread ml_sq ml_sum ml_var norm2 o_gated o_hi o_ready ox_first pT_copied pT_ready p_inv
p_ready p_scaled pad_zeroed post_added post_first post_scaled post_summed pv_done q_moved q_roped qi_split qk_pad
qk_silu relu_ready res_sq res_sqg rope_done rope_q rope_step row_step rstd_ready rt_cols rt_done
rt_turned s_masked s_ready scales_ready score_added score_masked sines spread_done squares squares_added
ssq_added ssqg_added start_hi start_ready start_scaled stat_ready stat_root tap_done topk_done topk_step
uq_out wi_copied wi_turned x2_done x2_gained y_pool y_scaled y_written rows_done
"""
CO_BESIDE = 3
ML_EVERY, ML_LEAD = 7, 0
ML_END = ML_EVERY * (ML_HEADS - 1) - ML_LEAD + 13
LN_MEAN_AT, LN_VAR_AT, LN_SCALE_AT, LN_SILU_AT, LN_SPLIT_AT = 4, 9, 12, 16, 17
MEM_SCALE_AT = 26


def program(nc, stream, xT, memT, cols_in, consts_in, sel_in, pos_in, out):
    with ExitStack() as ctx:
        def sem(name):
            return ctx.enter_context(nc.semaphore(name))

        def at(name, shape, offset, dt=F32):
            return nc.alloc_sbuf_tensor_at(name, shape, dt, offset=offset)

        W0, A0, B0, C0 = 2048, 34816, 67584, 101376
        G0, H0, QK0, BIAS0, KX0, TMP0, CON0 = 134144, 166912, 183296, 191488, 199680, 207872, 220160
        w_hi = at("w_hi", [P, RING, 1024], W0, F32R)
        w_raw = at("w_raw", [P, RING, 1024], W0 + 16384)
        w_lo = at("w_lo", [P, RING, 1024], W0 + 16384, F32R)
        a_hi = at("a_hi", [P, KB, T], A0, F32R)
        a_lo = at("a_lo", [P, KB, T], A0 + 16384, F32R)
        b_hi = at("b_hi", [P, KB, T], B0, F32R)
        b_lo = at("b_lo", [P, KB, T], B0 + 17408, F32R)
        c_hi = at("c_hi", [P, KB, T], C0, F32R)
        c_lo = at("c_lo", [P, KB, T], C0 + 16384, F32R)
        conv_in = at("conv_in", [P, KB, PAD + T], B0)
        conv_io = at("conv_io", [P, KB, T], B0 + 17408)
        gate_c = at("gate_c", [P, KB, T], G0)
        gate_a = at("gate_a", [P, KB, T], G0 + 16384)
        res = at("res", [P, KB, T], H0)
        values = at("values", [P, TB, D], H0)
        qT = at("qT", [P, 2, T], QK0)
        kT = at("kT", [P, 2, T], QK0 + 4096)
        rstd = at("rstd", [P, T], QK0)
        ssq = at("ssq", [P, T], QK0 + 2048)
        sq = at("sq", [P, 2, T], QK0 + 4096)
        bias = at("bias", [P, TB, T], BIAS0)
        kxT = at("kxT", [P, XH, M], KX0)
        vx = at("vx", [P, MB, XH * P], KX0 + 4096)
        probs = at("probs", [P, 2, T], TMP0 + 4096)
        probsT = at("probsT", [P, 2, T], TMP0 + 8192)
        cols = at("cols", [P, NCOLS], CON0)
        consts = at("consts", [P, NCONST], CON0 + 1792)
        small0 = CON0 + 1792 + NCONST * 4
        top8 = at("top8", [P, 3, 8], small0)
        wiT = at("wiT", [P, TB, IDX_HEADS], small0 + 96)
        rowmax = at("rowmax", [P, 2], small0 + 224)
        negmax = at("negmax", [P, 2], small0 + 256)
        rowsum = at("rowsum", [P, 2], small0 + 288)
        rowinv = at("rowinv", [P, 2], small0 + 320)
        g2g = at("g2g", [P, KB], small0 + 352)
        rtcol = at("rtcol", [P, TB], small0 + 448)
        gcols = at("gcols", [P, 2, TB, ML_HEADS], small0 + 2528)
        fcols = at("fcols", [P, TB, ML_HEADS], small0 + 2656)
        mcol = at("mcol", [P, 4, TB], small0 + 2720)
        ncol = at("ncol", [P, TB], small0 + 2784)
        spread = at("spread", [P, TB, P], TMP0 + 8192)
        mem_raw = at("mem_raw", [P, KB, M], G0)
        mem_sq = at("mem_sq", [P, KB, M], G0 + 8192)
        mem_hi = at("mem_hi", [P, KB, M], G0 + 16384, F32R)
        mem_lo = at("mem_lo", [P, KB, M], G0 + 24576, F32R)
        mem_rstd = at("mem_rstd", [P, M + MB], TMP0)
        x_sq = at("x_sq", [P, KB, T], C0)
        qi_parts = at("qi_parts", [P, IDX_HEADS, T], C0, F32R)
        ki_hi = at("ki_hi", [P, T], C0 + 16384, F32R)
        ki_lo = at("ki_lo", [P, T], C0 + 18432, F32R)
        wi_rows = at("wi_rows", [P, T], C0 + 26624)
        relu = at("relu", [P, 2, T], TMP0)
        score = bias
        ln_rstd = at("ln_rstd", [P, T], small0 + 480)
        ln_sq = at("ln_sq", [P, KB, T], B0)
        qxT = at("qxT", [P, XH, T], G0)
        xo_hi = at("xo_hi", [P, XH, T], C0, F32R)
        xo_lo = at("xo_lo", [P, XH, T], C0 + 16384, F32R)
        ff_t = at("ff_t", [P, 2, T], TMP0)
        ff_f = at("ff_f", [P, 2, T], TMP0 + 4096)
        ssq_g = at("ssq_g", [P, T], TMP0 + 8192)
        sq_g = at("sq_g", [P, T], TMP0 + 10240)
        cq_sq = at("cq_sq", [P, 3, T], TMP0)
        cq_rstd = at("cq_rstd", [P, 2, T], TMP0 + 6144)
        cq = at("cq", [P, 3, T], C0)
        cn_hi = at("cn_hi", [P, 3, T], TMP0, F32R)
        cn_lo = at("cn_lo", [P, 3, T], C0 + 24576, F32R)
        ogate = at("ogate", [P, ML_HEADS, T], C0 + 16384)
        qk_in = at("qk_in", [P, 4, ML_TAPS - 1 + T], G0)
        qk_ml = at("qk_ml", [P, 4, T], G0 + 8256)
        v_ml = at("v_ml", [P, TB, ML_HEADS * ML_V], G0 + 16448)
        v_mla = at("v_mla", [P, TB, MLA_HEADS * MLA_V], G0)
        qh = at("qh", [P, MLA_HEADS, T], BIAS0)
        kh = at("kh", [P, MLA_HEADS, T], C0)
        gt = at("gt", [P, 6, T], B0)
        ropet = at("ropet", [P, 2, T], G0 + 24640)
        angle = at("angle", [P, 2, T], G0)
        rot = at("rot", [P, 2, T], B0 + 22528)
        krT = at("krT", [P, T], B0 + 26624)
        sel = at("sel", [P, ML_HEADS * P], G0 + 28736)
        posi = at("posi", [P, T], G0 + 4096, I32)
        qrot = at("qrot", [P, 2, T], B0 + 28672)
        sT = at("sT", [P, 2, T], TMP0)
        decay = at("decay", [P, 2, T], B0 + 12288)
        negm_diag = at("negm_diag", [P, TB, P], B0 + 16384)
        mrow = at("mrow", [P, T], B0 + 18432)
        ml_square = at("ml_square", [P, T], B0 + 20480)
        ml_spread = at("ml_spread", [P, TB, P], C0 + 24576)
        hml = at("hml", [P, 2, T], QK0 + 4096)
        mixed = at("mixed", [P, KB, T], C0)
        ffy = at("ffy", [P, KB, T], C0 + 16384)
        y_out = at("y_out", [P, KB, T], G0)

        def col(name, i=0, n=1, p0=0, p1=P):
            return cols[p0:p1, COL[name] + i:COL[name] + i + n]

        def con(name, n, i=0, p0=0, p1=P):
            return consts[p0:p1, CON[name] + i:CON[name] + i + n]

        ident = con("ident", P)
        ones = con("ones", P)
        eps = con("misc", 1, EPS_COL)

        ps = [ctx.enter_context(nc.psum_tensor(f"bank{i}", [P, 512], F32)) for i in range(8)]
        STAT = 4

        raw_landed = [sem(f"raw_landed{i}") for i in range(RING)]
        w_hi_done = sem("w_hi_done")
        w_lo_done = sem("w_lo_done")
        chunk_done = sem("chunk_done")
        evac_act = sem("evac_act")
        evac_dve = sem("evac_dve")
        consts_landed = sem("consts_landed")
        mem_landed = sem("mem_landed")
        x_landed = sem("x_landed")
        x_again = sem("x_landed_again")
        out_landed = sem("out_landed")
        sems = {n: sem(n) for n in SEMAPHORES.split()}
        block = ctx.enter_context(nc.Block())

        def w_slot(t, slot, k, n=P):
            return t[:, slot, k * n:(k + 1) * n]

        DSA_G, X_G, MLA_G = 0, HEADS, HEADS + XH

        def keys_of(G, qb):
            return M if X_G <= G < MLA_G else (qb + 1) * P

        def scale_of(G):
            if G < MLA_G:
                return float(P) ** -0.5
            return float(NOPE + ROPE) ** -0.5

        def bias_of(G, qb):
            n = keys_of(G, qb)
            if G < X_G and qb > 0:
                return bias[:, qb, 0:n]
            if G < X_G or G >= MLA_G:
                return con("bias", n, T - n)
            return con("bias", n, 0)

        def out_of(G):
            if G < X_G:
                return ps[2][:, :], c_hi[:, G, :], c_lo[:, G, :]
            if G < MLA_G:
                return ps[2][:, :], xo_hi[:, G - X_G, :], xo_lo[:, G - X_G, :]
            h = G - MLA_G
            r = slice(MLA_V * (h % 2), MLA_V * (h % 2) + MLA_V)
            return ps[2][r, :], a_hi[r, ML_HEADS + h // 2, :], a_lo[r, ML_HEADS + h // 2, :]

        @block.sync
        def _(sp):
            for j in range(RING):
                sp.dma_start(w_raw[:, j, :], stream[j]).then_inc(raw_landed[j], 16)
                if j == 0:
                    sp.dma_start(mem_raw[:, :, :], memT).then_inc(mem_landed, 16)
            sp.dma_start(res[:, :, :], xT).then_inc(x_landed, 16)
            with sp.Fori(1, CHUNKS // RING) as i:
                for j in range(RING):
                    sp.wait_ge(chunk_done, RING * i + j - (RING - 1))
                    sp.dma_start(w_raw[:, j, :],
                                 stream[bass.ds(RING * i + j, 1), :, :].rearrange("o p n -> (o p) n")
                                 ).then_inc(raw_landed[j], 16)
            for i in range(KB):
                if i in POOL_ADDS:
                    sp.wait_ge(sems["y_pool"], POOL_ADDS.index(i) + 1)
                else:
                    sp.wait_ge(sems["y_written"], len([j for j in range(i + 1) if j not in POOL_ADDS]))
                sp.dma_start(out[:, i, :], y_out[:, i, :]).then_inc(out_landed, 16)
            sp.wait_ge(out_landed, 16 * KB)

        @block.gpsimd
        def _(pool):
            nc.gpsimd.memset(conv_in[:, :, 0:PAD], 0.0).then_inc(sems["pad_zeroed"], 1)

            def remainder(c, j):
                pool.wait_ge(w_hi_done, c + 1)
                nc.gpsimd.tensor_tensor(w_lo[:, j, :], w_raw[:, j, :], w_hi[:, j, :].bitcast(F32),
                                        ALU.subtract).then_inc(w_lo_done, 1)

            last = CH["FF2"] // RING
            mix = CH["WO"] // RING
            with pool.Fori(0, mix) as i:
                for j in range(RING):
                    remainder(RING * i + j, j)
            for j in range(AHEAD):
                remainder(CH["WO"] + j, j)
            pool.wait_ge(sems["rstd_ready"], 8)
            for j in range(KB):
                nc.gpsimd.tensor_tensor(res[:, j, :], res[:, j, :], col("norm_final_g", j).to_broadcast([P, T]),
                                        ALU.mult).then_inc(sems["x2_gained"], 1)
            for j in range(KB):
                pool.wait_ge(sems["x2_gained"], j + 1)
                nc.gpsimd.tensor_tensor(res[:, j, :], res[:, j, :], rstd[:, :], ALU.mult).then_inc(sems["x2_done"], 1)
            remainder(CH["WO"] + AHEAD, AHEAD)
            for h in range(ML_HEADS):
                pool.wait_ge(sems["ml_hi"], h + 1)
                nc.gpsimd.tensor_tensor(a_lo[:, h, :], hml[:, h % 2, :], a_hi[:, h, :].bitcast(F32), ALU.subtract
                                        ).then_inc(sems["ml_ready"], 1)
            with pool.Fori(mix + 1, last) as i:
                for j in range(RING):
                    remainder(RING * i + j, j)
            for j in range(AHEAD):
                remainder(CH["FF2"] + j, j)
            for j in range(1, KB):
                pool.wait_ge(sems["post_scaled"], j + 1)
                pool.wait_ge(sems["x2_done"], KB)
                nc.gpsimd.tensor_tensor(res[:, j, :], res[:, j, :], mixed[:, j, :], ALU.add
                                        ).then_inc(sems["post_added"], 1)
            remainder(CH["FF2"] + AHEAD, AHEAD)
            with pool.Fori(last + 1, CHUNKS // RING) as i:
                for j in range(RING):
                    remainder(RING * i + j, j)
            for j in POOL_ADDS:
                pool.wait_ge(sems["y_scaled"], j + 1)
                nc.gpsimd.tensor_tensor(y_out[:, j, :], ffy[:, j, :], res[:, j, :], ALU.add
                                        ).then_inc(sems["y_pool"], 1)

        @block.tensor
        def _(pe):
            def mm(o, l, r, start=True, stop=True):
                return nc.tensor.matmul(o, l, r, start=start, stop=stop)

            def three(o, wh, wl, xh, xl, start, stop):
                mm(o, wh, xh, start, False)
                mm(o, wh, xl, False, False)
                return mm(o, wl, xh, False, stop)

            def bank_free(o, first=None):
                if (o if first is None else first) >= DVE_FROM + RING:
                    pe.wait_ge(evac_dve, o - RING + 1 - DVE_FROM)
                elif first is not None or RING <= o <= DVE_FROM:
                    pe.wait_ge(evac_act, o - RING + 1)

            def chunk(c, slot, o, bank, hi, lo, width=T, ready=None, base=0, first=None, ks=range(KB)):
                if ks[0] == 0:
                    pe.wait_ge(w_lo_done, c + 1)
                    if o is not None:
                        bank_free(o, first)
                for k in ks:
                    if ready is not None:
                        pe.wait_ge(ready, base + k + 1)
                    m = three(ps[bank][:, 0:width], w_slot(w_hi, slot, k), w_slot(w_lo, slot, k),
                              hi[:, k, 0:width], lo[:, k, 0:width], k == 0, k == KB - 1)
                if ks[-1] == KB - 1:
                    m.then_inc(chunk_done, 1)

            def stage(name, n, hi, lo, width=T, ready=None, base=0):
                c0, o0 = CH[name], O[name]
                if n <= RING:
                    for j in range(n):
                        chunk(c0 + j, (c0 + j) % RING, o0 + j, (o0 + j) % RING, hi, lo, width,
                              ready if j == 0 else None, base)
                    return
                with pe.Fori(0, n // RING) as i:
                    for j in range(RING):
                        chunk(RING * i + c0 + j, (c0 + j) % RING, RING * i + (o0 + j), (o0 + j) % RING,
                              hi, lo, width, ready if j == 0 else None, base, first=o0 + j)

            def token_major(c0, o0, blocks, hi, lo, ready=None, base=0, beside=None):
                for t in range(RING):
                    slot = (c0 + t) % RING
                    if beside is not None:
                        beside(t)
                    pe.wait_ge(w_lo_done, c0 + t + 1)
                    for b in range(blocks):
                        if t == 0:
                            bank_free(o0 + b)
                        for kk in range(2):
                            k = 2 * t + kk
                            if ready is not None and b == 0:
                                pe.wait_ge(ready, base + k + 1)
                            o = ps[(o0 + b) % RING][:, :]
                            xh, xl = hi[:, k, b * P:(b + 1) * P], lo[:, k, b * P:(b + 1) * P]
                            wh, wl = w_slot(w_hi, slot, kk, T), w_slot(w_lo, slot, kk, T)
                            mm(o, xh, wh, k == 0, False)
                            mm(o, xh, wl, False, False)
                            m = mm(o, xl, wh, False, k == KB - 1)
                        if t == RING - 1 and b < blocks - 1:
                            m.then_inc(sems["rows_done"], 1)
                    m.then_inc(chunk_done, 1)

            def stat(n, bank, parts, width=T):
                for k, (s, v, part) in enumerate(parts):
                    if s is not None:
                        pe.wait_ge(s, v)
                    m = mm(ps[bank][:, 0:width], ones, part, k == 0, k == len(parts) - 1)
                m.then_inc(sems["stat_ready"], 1)

            def token_scales(squares, src, n, part=None, last=None):
                if part in (None, 0):
                    pe.wait_ge(*squares)
                    if last is not None:
                        pe.wait_ge(*last[0])
                    for tb in range(TB):
                        b = slice(tb * P, (tb + 1) * P)
                        m = mm(ps[STAT][:, tb:tb + 1], src[:, b], ones[:, 0:1], True, last is None)
                        if last is not None:
                            m = mm(ps[STAT][:, tb:tb + 1], last[1][:, b], ones[:, 0:1], False, True)
                    m.then_inc(sems["stat_ready"], 1)
                if part in (None, 1):
                    pe.wait_ge(sems["spread_done"], n)
                    for tb in range(TB):
                        m = mm(ps[5][:, tb * P:(tb + 1) * P], ones, spread[:, tb, :])
                    m.then_inc(sems["scales_ready"], 1)

            def attend(G0, n_heads, score, value, hook=None):
                n_units = 4 * n_heads

                def scores(n):
                    U, G, qb = 4 * G0 + n, G0 + n // 4, n % 4
                    if U >= 2:
                        pe.wait_ge(sems["p_ready"], U - 1)
                    score(G, qb, ps[4 + U % 2][:, 0:keys_of(G, qb)]).then_inc(sems["s_ready"], 1)

                def turn(n):
                    U, G, qb = 4 * G0 + n, G0 + n // 4, n % 4
                    pe.wait_ge(sems["p_scaled"], U + 1)
                    if U >= 2:
                        pe.wait_ge(sems["pT_copied"], U - 1)
                    for kb in range(keys_of(G, qb) // P):
                        r = slice(kb * P, (kb + 1) * P)
                        m = nc.tensor.transpose(ps[6 + U % 2][:, r], probs[:, U % 2, r], ident)
                    m.then_inc(sems["pT_ready"], 1)

                def values_out(n):
                    U, G, qb = 4 * G0 + n, G0 + n // 4, n % 4
                    pe.wait_ge(sems["pT_copied"], U + 1)
                    if qb == 0 and G > 0:
                        pe.wait_ge(sems["o_ready"], G)
                    nk = keys_of(G, qb) // P
                    for kb in range(nk):
                        m = mm(out_of(G)[0][:, qb * P:(qb + 1) * P], value(G, kb),
                               probsT[:, U % 2, kb * P:(kb + 1) * P], kb == 0, kb == nk - 1)
                    m.then_inc(sems["pv_done"], 1)

                scores(0)
                scores(1)
                for n in range(n_units):
                    if n + 2 < n_units:
                        scores(n + 2)
                    if hook is not None:
                        hook(n)
                    turn(n)
                    if n >= 1:
                        values_out(n - 1)
                values_out(n_units - 1)

            pe.wait_ge(consts_landed, 32)
            for j in range(4):
                chunk(CH["MK"] + j, j, O["MK"] + j, j, mem_hi, mem_lo, M, sems["start_ready"] if j == 0 else None)
            token_major(CH["MV"], O["MV"], MB, mem_hi, mem_lo,
                        beside=lambda t: token_scales((sems["squares_added"], KB - 1), x_sq[:, 0, :], 1, t - 1))
            stage("QI", 4, a_hi, a_lo, T, sems["start_ready"], KB)
            pe.wait_ge(sems["qi_split"], 2)
            stage("KI", 1, a_hi, a_lo)
            pe.wait_ge(sems["mem_added"], 3)
            mm(ps[4][:, 0:M], ones, mem_sq[:, 0, :])
            for b in range(MB):
                m = mm(ps[4][:, M + b:M + b + 1], mem_sq[:, 0, b * P:(b + 1) * P], ones[:, 0:1])
            m.then_inc(sems["stat_ready"], 1)
            pe.wait_ge(evac_act, O["KI"] + 1)
            pe.wait_ge(sems["stat_root"], 1)
            for tb in range(TB):
                m = nc.tensor.transpose(ps[5][:, tb * IDX_HEADS:(tb + 1) * IDX_HEADS],
                                        wi_rows[0:IDX_HEADS, tb * P:(tb + 1) * P],
                                        ident[0:IDX_HEADS, 0:IDX_HEADS])
            m.then_inc(sems["wi_turned"], 1)
            for n in range(3 * IDX_HEADS):
                qb, h = 1 + n // IDX_HEADS, n % IDX_HEADS
                r = slice(IDX_DIM * (h % 2), IDX_DIM * (h % 2) + IDX_DIM)
                if n >= 2:
                    pe.wait_ge(sems["relu_ready"], n - 1)
                o, keys, b = ps[6 + n % 2][:, 0:(qb + 1) * P], slice(0, (qb + 1) * P), slice(qb * P, (qb + 1) * P)
                if n == 0:
                    pe.wait_ge(sems["qi_split"], IDX_HEADS)
                    pe.wait_ge(sems["ki_split"], 2)
                mm(o, qi_parts[:, h, b], ki_hi[:, keys], True, False)
                mm(o, qi_parts[r, h, b], ki_lo[r, keys], False, True).then_inc(sems["logits_ready"], 1)
            stage("C", 16, a_hi, a_lo)
            stage("G", 16, a_hi, a_lo)
            for half in range(2):
                token_major(CH["V"] + 4 * half, O["V"] + 4 * half, TB, a_hi, a_lo)

            def qk_chunk(n, ks=range(KB)):
                c, o = CH["ATT"] + n, O["ATT"] + n
                if ks[0] == 0:
                    pe.wait_ge(evac_act, o - 1 if n >= 2 else O["ATT"])
                chunk(c, c % RING, None, n % 2, a_hi, a_lo, ks=ks)

            def conv_out_chunk(j, ks=range(KB)):
                c = CH["CO"] + j
                if ks[0] == 0 and j < 2:
                    pe.wait_ge(evac_act, DVE_FROM)
                elif ks[0] == 0:
                    pe.wait_ge(evac_dve, j - 1)
                chunk(c, c % RING, None, j % 2, b_hi, b_lo, ready=sems["convact_ready"] if j == 0 else None, ks=ks)

            def dsa_score(G, qb, o):
                pe.wait_ge(evac_act, O["ATT"] + 2 * G + 2)
                return mm(o, qT[:, G % 2, qb * P:(qb + 1) * P], kT[:, G % 2, 0:(qb + 1) * P])

            def dsa_hook(n):
                near = range(LN_SILU_AT - 1, LN_SILU_AT + 2)
                for u in (near if n == LN_SILU_AT else [] if n in near else [n]):
                    filler, ks = (u - 2) // 2, range(4 * (u % 2), 4 * (u % 2) + 4)
                    if 0 <= filler < 2 * (HEADS - 2):
                        qk_chunk(4 + filler, ks)
                    elif filler >= 0:
                        conv_out_chunk(filler - 2 * (HEADS - 2), ks)
                if n in (LN_MEAN_AT, LN_VAR_AT):
                    pe.wait_ge(sems["ln_added"], (KB - 1) * (1 if n == LN_MEAN_AT else 2))
                    mm(ps[3][:, :], ones, ln_rstd[:, :]).then_inc(sems["ln_sum"], 1)

            for n in range(4):
                qk_chunk(n)
            pe.wait_ge(sems["conv_done"], KB)
            attend(DSA_G, HEADS, dsa_score,
                   lambda G, kb: values[:, kb, G * P:(G + 1) * P], dsa_hook)
            for j in range(CO_BESIDE, KB):
                conv_out_chunk(j)
            pe.wait_ge(sems["ln_root"], 1)
            pe.wait_ge(evac_dve, KB)
            stage("AO", KB, c_hi, c_lo, ready=sems["o_ready"])
            stage("MX", KB, a_hi, a_lo, ready=sems["mix_ready"])
            def xq_chunk(h, ks=range(KB)):
                if ks[0] == 0:
                    last = O["QX"] + (h - RING if h < XH - 1 else 0)
                    pe.wait_ge(evac_dve, last + 1 - DVE_FROM)
                chunk(CH["QX"] + h, (CH["QX"] + h) % RING, None, (3, 0, 1, 3)[h], b_hi, b_lo,
                      ready=sems["hg_ready"] if h == 0 else None, ks=ks)

            def x_hook(n):
                if n in X_FILLED:
                    quarter = 2 * 4 + X_FILLED.index(n)
                    xq_chunk(quarter // 4, range(2 * (quarter % 4), 2 * (quarter % 4) + 2))

            xq_chunk(0)
            stat(2, STAT, [(sems["ssq_added"], KB, ssq[:, :])])
            xq_chunk(1)

            def x_score(G, qb, o):
                h = G - X_G
                pe.wait_ge(evac_dve, O["QX"] + h + 1 - DVE_FROM)
                if h == 0 and qb < 2:
                    pe.wait_ge(sems["stat_root"], 3)
                return mm(o, qxT[:, h, qb * P:(qb + 1) * P], kxT[:, h, :])

            attend(X_G, XH, x_score, lambda G, kb: vx[:, kb, (G - X_G) * P:(G - X_G + 1) * P], x_hook)
            for j in range(XH):
                c = CH["OX"] + j
                pe.wait_ge(w_lo_done, c + 1)
                for r in range(2):
                    o = O["OX"] + 2 * j + r
                    bank_free(o)
                    for k in range(XH):
                        if j == 0 and r == 0:
                            pe.wait_ge(sems["o_ready"], X_G + k + 1)
                        m = three(ps[o % RING][:, :], w_slot(w_hi, c % RING, r * XH + k),
                                  w_slot(w_lo, c % RING, r * XH + k), xo_hi[:, k, :], xo_lo[:, k, :],
                                  k == 0, k == XH - 1)
                    if r == 0:
                        m.then_inc(sems["ox_first"], 1)
                m.then_inc(chunk_done, 1)

            def feed_forward(name, s, hset, norm):
                c0, o0 = CH[name], O[name]

                def ff_chunk(g, j, ready=None, base=0, ks=range(KB)):
                    hi, lo = (a_hi, a_lo) if j < KB else (b_hi, b_lo)
                    chunk(g * 16 + (c0 + j), (c0 + j) % RING, g * 16 + (o0 + j), (o0 + j) % RING, hi, lo, T,
                          ready, base, first=o0 + j, ks=ks)

                for k in range(KB):
                    ff_chunk(0, 0, sems["hg_ready"], KB * hset, range(k, k + 1))
                    norm(k)
                for j in range(1, 2 * KB):
                    ff_chunk(0, j, sems["f_ready"] if j == KB else None, 32 * s)
                with pe.Fori(1, FF_GROUPS) as g:
                    for j in range(2 * KB):
                        ff_chunk(g, j, sems["f_ready"] if j == KB else None, g * KB + 32 * s)

            def norm_ffn(k):
                if k == KB - 1:
                    stat(3, STAT, [(sems["ssq_added"], 2 * KB, ssq[:, :])])

            feed_forward("FF1", 0, 1, norm_ffn)
            stage("CQ", 2, a_hi, a_lo, ready=sems["hg_ready"], base=2 * KB)
            stat(4, STAT, [(sems["ssq_added"], 3 * KB, ssq[:, :])])
            stat(5, 5, [(sems["ssqg_added"], KB, ssq_g[:, :])])
            stage("CKV", 1, a_hi, a_lo)
            stage("KR", 1, a_hi, a_lo)
            pe.wait_ge(sems["rt_done"], 1)
            for tb in range(TB):
                m = nc.tensor.transpose(ps[6][:, tb * P:(tb + 1) * P], ssq[:, tb * P:(tb + 1) * P], ident)
            m.then_inc(sems["rt_turned"], 1)
            stage("QK", 4, a_hi, a_lo)
            stat(6, STAT, [(sems["cq_squared"], k + 1, cq_sq[:, k, :]) for k in range(2)])
            stat(7, 5, [(sems["cq_squared"], 3, cq_sq[:, 2, :])])
            token_major(CH["VM"], O["VM"], TB, a_hi, a_lo)
            stage("OM", 4, a_hi, a_lo)
            for t in range(2):
                c = CH["UQ"] + t
                pe.wait_ge(w_lo_done, c + 1)
                for j in range(4):
                    o = O["UQ"] + 4 * t + j
                    bank_free(o)
                    for k in range(2):
                        if t == 0 and j == 0:
                            pe.wait_ge(sems["cn_ready"], k + 1)
                        m = three(ps[o % RING][:, :], w_slot(w_hi, c % RING, 2 * j + k),
                                  w_slot(w_lo, c % RING, 2 * j + k), cn_hi[:, k, :], cn_lo[:, k, :],
                                  k == 0, k == 1)
                    if j < 3:
                        m.then_inc(sems["uq_out"], 1)
                m.then_inc(chunk_done, 1)
            c = CH["UKV"]
            pe.wait_ge(w_lo_done, c + 1)
            pe.wait_ge(sems["cn_ready"], 3)
            for j in range(4):
                o = O["UKV"] + j
                bank_free(o)
                m = three(ps[o % RING][:, :], w_slot(w_hi, c % RING, j), w_slot(w_lo, c % RING, j),
                          cn_hi[:, 2, :], cn_lo[:, 2, :], True, True)
                m.then_inc(sems["kv_keys_done"], 1)
            for j in range(TB):
                o = O["UKV"] + 4 + j
                bank_free(o)
                xh, xl = cn_hi[:, 2, j * P:(j + 1) * P], cn_lo[:, 2, j * P:(j + 1) * P]
                wh, wl = w_slot(w_hi, c % RING, 1, T), w_slot(w_lo, c % RING, 1, T)
                m = three(ps[o % RING][:, :], xh, xl, wh, wl, True, True)
                m.then_inc(chunk_done if j == TB - 1 else sems["kv_values_done"], 1)
            pe.wait_ge(sems["gates_done"], 1)
            for tb in range(TB):
                for i, row in enumerate((0, 3)):
                    c = (i * TB + tb) * ML_HEADS
                    m = nc.tensor.transpose(ps[7][:, c:c + ML_HEADS], gt[0:ML_HEADS, row, tb * P:(tb + 1) * P],
                                            ident[0:ML_HEADS, 0:ML_HEADS])
            m.then_inc(sems["gates_turned"], 1)
            pe.wait_ge(evac_dve, O["WO"] - DVE_FROM)
            pe.wait_ge(sems["gcols_done"], 1)
            pe.wait_ge(sems["rstd_ready"], 8)
            pe.wait_ge(sems["late_landed"], 32)
            pe.wait_ge(sems["qk_silu"], 4)
            num, dn, shared = ps[0], ps[1], ps[3]

            def ml_step(h, st):
                r = slice(ML_QK * (h % 2), ML_QK * (h % 2) + ML_QK)
                if st == 0:
                    if h >= 1:
                        pe.wait_ge(sems["ml_sT"], 4 * h)
                    mm(shared[:, :], sel[0:ML_HEADS, h * P:(h + 1) * P], gt[0:ML_HEADS, 4, :]
                       ).then_inc(sems["ml_rows"], 1)
                if 3 <= st < 3 + TB:
                    jb = st - 3
                    if jb == 0:
                        pe.wait_ge(sems["ml_mrow"], h + 1)
                    else:
                        pe.wait_ge(sems["ml_sT"], 4 * h + jb)
                    mm(shared[:, 0:T - jb * P], qk_ml[r, 2 + h // 2, jb * P:(jb + 1) * P],
                       qk_ml[r, h // 2, jb * P:T]).then_inc(sems["ml_s"], 1)
                if 4 <= st < 4 + TB:
                    jb = st - 4
                    u = 4 * h + jb
                    pe.wait_ge(sems["ml_sT"], u + 1)
                    if jb == 0 and h >= 1:
                        pe.wait_ge(sems["ml_num"], h)
                        pe.wait_ge(sems["ml_gated"], h)
                    part = sT[:, u % 2, 0:T - jb * P]
                    mm(num[:, jb * P:T], v_ml[:, jb, h * ML_V:(h + 1) * ML_V], part, jb == 0, jb == TB - 1)
                    for qb in range(jb, TB):
                        m = mm(dn[:, qb:qb + 1], part[:, (qb - jb) * P:(qb - jb + 1) * P], ones[:, 0:1],
                               jb == 0 and qb == 0, jb == TB - 1)
                    m.then_inc(sems["ml_out"], 1)
                if st == 8:
                    pe.wait_ge(sems["ml_sq"], h + 1)
                    pe.wait_ge(sems["ml_den"], h + 1)
                    for tb in range(TB):
                        m = mm(dn[:, TB + tb:TB + tb + 1], ml_square[:, tb * P:(tb + 1) * P], ones[:, 0:1])
                    m.then_inc(sems["ml_sum"], 1)
                if st == 10:
                    pe.wait_ge(sems["ml_spread"], h + 1)
                    for tb in range(TB):
                        m = mm(dn[:, tb * P:(tb + 1) * P], ones, ml_spread[:, tb, :])
                    m.then_inc(sems["ml_scale"], 1)

            def ml_hook(n):
                for h in range(ML_HEADS):
                    ml_step(h, n + ML_LEAD - ML_EVERY * h)

            def mla_score(G, qb, o):
                h = G - MLA_G
                if qb == 0:
                    pe.wait_ge(sems["rope_done"], h + 1)
                    pe.wait_ge(sems["q_roped"], h + 1)
                return mm(o, qh[0:NOPE + ROPE, h, qb * P:(qb + 1) * P], kh[0:NOPE + ROPE, h, 0:(qb + 1) * P])

            for n in range(-ML_LEAD, 0):
                ml_hook(n)
            attend(MLA_G, MLA_HEADS, mla_score,
                   lambda G, kb: v_mla[:, kb, (G - MLA_G) * MLA_V:(G - MLA_G + 1) * MLA_V], ml_hook)
            for n in range(4 * MLA_HEADS, ML_END):
                ml_hook(n)
            for j in range(KB):
                c, o = CH["WO"] + j, O["WO"] + j
                pe.wait_ge(w_lo_done, c + 1)
                bank_free(o)
                order = [k for k in range(KB) if k not in (ML_HEADS - 1, KB - 1)] + [ML_HEADS - 1, KB - 1]
                for k in order:
                    if j == 0 and k < ML_HEADS:
                        pe.wait_ge(sems["ml_ready"], k + 1)
                    elif j == 0:
                        pe.wait_ge(sems["o_ready"], MLA_G + 2 * (k - ML_HEADS) + 2)
                    m = three(ps[o % RING][:, :], w_slot(w_hi, c % RING, k), w_slot(w_lo, c % RING, k),
                              a_hi[:, k, :], a_lo[:, k, :], k == order[0], k == order[-1])
                m.then_inc(chunk_done, 1)
            token_scales((sems["ssq_added"], 4 * KB - 1), ssq, 2, last=((sems["res_sq"], 4 * KB), sq[:, (KB - 1) % 2, :]))

            def norm_pre_mlp(k):
                pe.wait_ge(sems["res_sq"], 4 * KB + k + 1)
                mm(ps[STAT][:, :], ones, sq[:, k % 2, :], k == 0, k == KB - 1).then_inc(sems["post_summed"], 1)

            feed_forward("FF2", 1, 3, norm_pre_mlp)
            pe.wait_ge(sems["rstd_ready"], 10)
            token_scales((sems["ssq_added"], 5 * KB - 2), ssq, 3, last=((sems["res_sq"], 6 * KB), sq[:, (KB - 1) % 2, :]))

        @block.scalar
        def _(act):
            A = nc.scalar
            rounded = [0]

            def round_chunk(c, slot, turn):
                act.wait_ge(raw_landed[slot], 16 * turn)
                if not isinstance(c, int) or c >= RING:
                    act.wait_ge(chunk_done, c - (RING - 1))
                A.copy(w_hi[:, slot, :], w_raw[:, slot, :]).then_inc(w_hi_done, 1)

            def round_to(c):
                while rounded[0] <= min(c + AHEAD, CHUNKS - 1):
                    n = rounded[0]
                    round_chunk(n, n % RING, n // RING + 1)
                    rounded[0] += 1

            def root(n, dst, bank, scale, width=T, sums=None):
                if sums is None:
                    act.wait_ge(sems["stat_ready"], n + 1 if n < 9 else n)
                else:
                    act.wait_ge(*sums)
                A.activation(dst, ps[bank][:, 0:width], ACT.Sqrt, bias=eps, scale=scale).then_inc(sems["stat_root"], 1)

            def empty(c, o, dst, rows=slice(0, P), width=T, row_block=None):
                if row_block is None:
                    act.wait_ge(chunk_done, c + 1)
                else:
                    act.wait_ge(sems["rows_done"], row_block + 1)
                A.copy(dst, ps[o % RING][rows, 0:width]).then_inc(evac_act, 1)

            def attend(G0, n_heads, hook=None, after=None):
                n_units = 4 * n_heads

                def exps(n):
                    U, G, qb = 4 * G0 + n, G0 + n // 4, n % 4
                    act.wait_ge(sems["s_masked"], U + 1)
                    if U >= 2:
                        act.wait_ge(sems["pT_ready"], U - 1)
                    r = slice(0, keys_of(G, qb))
                    A.activation(probs[:, U % 2, r], ps[4 + U % 2][:, r], ACT.Exp, bias=negmax[:, U % 2:U % 2 + 1],
                                 scale=-1.0, accum_out=rowsum[:, U % 2:U % 2 + 1]).then_inc(sems["p_ready"], 1)

                def turned(n):
                    U, G, qb = 4 * G0 + n, G0 + n // 4, n % 4
                    act.wait_ge(sems["pT_ready"], U + 1)
                    if U >= 2:
                        act.wait_ge(sems["pv_done"], U - 1)
                    r = slice(0, keys_of(G, qb))
                    A.copy(probsT[:, U % 2, r], ps[6 + U % 2][:, r]).then_inc(sems["pT_copied"], 1)

                def out_hi(G):
                    o, hi, _ = out_of(G)
                    act.wait_ge(sems["pv_done"], 4 * (G + 1))
                    A.copy(hi, o).then_inc(sems["o_hi"], 1)

                exps(0)
                exps(1)
                for n in range(n_units):
                    if hook is not None:
                        hook(n)
                    turned(n)
                    if n + 2 < n_units:
                        exps(n + 2)
                    if n % 4 == 0 and n >= 4:
                        out_hi(G0 + n // 4 - 1)
                    if after is not None:
                        after(n)
                out_hi(G0 + n_heads - 1)

            act.dma_start(cols[:, :], cols_in).then_inc(consts_landed, 16)
            act.dma_start(consts[:, :], consts_in).then_inc(consts_landed, 16)
            round_to(-AHEAD)
            act.wait_ge(consts_landed, 32)
            act.wait_ge(mem_landed, 16)
            for k in range(KB):
                A.activation(mem_hi[:, k, :], mem_raw[:, k, :], ACT.Copy, scale=col("norm_mem_g", k)
                             ).then_inc(sems["start_hi"], 1)
                if k % 4 == 3:
                    round_to(1 + k // 4 - AHEAD)
            round_to(0)
            act.wait_ge(x_landed, 16)
            for k in range(KB):
                A.activation(x_sq[:, k, :], res[:, k, :], ACT.Square).then_inc(sems["squares"], 1)
                if k == 1:
                    empty(CH["MK"], O["MK"], kxT[:, 0, :], width=M)
                    round_to(CH["MK"] + 1)
            for j in range(1, XH):
                empty(CH["MK"] + j, O["MK"] + j, kxT[:, j, :], width=M)
                if j == 2:
                    root(0, ncol[:, :], STAT, 1.0 / D, TB)
                round_to(CH["MK"] + j + 1)
            for k in range(KB):
                act.wait_ge(sems["start_scaled"], k + 1)
                A.copy(a_hi[:, k, :], res[:, k, :]).then_inc(sems["start_hi"], 1)
                if k % 2 == 0:
                    round_to(CH["MV"] + 1 + k // 2)
            for b in range(MB):
                empty(CH["MV"] + 3, O["MV"] + b, vx[:, b, :], row_block=b if b < MB - 1 else None)
            low, high = slice(0, IDX_DIM), slice(IDX_DIM, 2 * IDX_DIM)
            for j in range(4):
                round_to(CH["QI"] + j)
                act.wait_ge(chunk_done, CH["QI"] + j + 1)
                bank = ps[(O["QI"] + j) % RING]
                A.copy(qi_parts[low, 2 * j, :], bank[low, :])
                A.copy(qi_parts[high, 2 * j + 1, :], bank[high, :]).then_inc(evac_act, 1)
            round_to(CH["KI"])
            act.wait_ge(chunk_done, CH["KI"] + 1)
            bank = ps[O["KI"] % RING]
            A.copy(ki_hi[low, :], bank[low, :])
            A.copy(ki_hi[high, :], bank[low, :])
            A.mul(wi_rows[0:IDX_HEADS, :], bank[IDX_DIM:IDX_DIM + IDX_HEADS, :],
                  float(IDX_HEADS) ** -0.5).then_inc(evac_act, 1)
            for n in range(3 * IDX_HEADS):
                qb = 1 + n // IDX_HEADS
                act.wait_ge(sems["logits_ready"], n + 1)
                if n >= 2:
                    act.wait_ge(sems["score_added"], n - 1)
                A.activation(relu[:, n % 2, 0:(qb + 1) * P], ps[6 + n % 2][:, 0:(qb + 1) * P], ACT.Relu,
                             scale=float(IDX_DIM) ** -0.5).then_inc(sems["relu_ready"], 1)
            act.wait_ge(sems["score_added"], 3 * IDX_HEADS)
            root(1, mem_rstd[:, :], 4, 1.0 / D, M + MB)
            for j in range(16):
                c, o = CH["C"] + j, O["C"] + j
                round_to(c)
                act.wait_ge(chunk_done, c + 1)
                if j % 2 == 0:
                    A.activation(conv_io[:, j // 2, :], ps[o % RING][:, :], ACT.Sigmoid).then_inc(evac_act, 1)
                else:
                    A.copy(conv_in[:, j // 2, PAD:PAD + T], ps[o % RING][:, :]).then_inc(evac_act, 1)
            for j in range(16):
                c, o = CH["G"] + j, O["G"] + j
                round_to(c)
                act.wait_ge(chunk_done, c + 1)
                gate = (gate_c if j < KB else gate_a)[:, j % KB, :]
                A.activation(gate, ps[o % RING][:, :], ACT.Sigmoid, bias=col("b_gate", j)).then_inc(evac_act, 1)
            for half in range(2):
                for t in range(4):
                    round_to(CH["V"] + 4 * half + t)
                for b in range(TB):
                    empty(CH["V"] + 4 * half + 3, O["V"] + 4 * half + b, values[:, b, half * T:(half + 1) * T],
                          row_block=MB - 1 + half * (TB - 1) + b if b < TB - 1 else None)

            def empty_qk(n):
                c = CH["ATT"] + n
                round_to(c)
                act.wait_ge(chunk_done, c + 1)
                dst = (qT if n % 2 == 0 else kT)[:, (n // 2) % 2, :]
                A.copy(dst, ps[n % 2][:, :]).then_inc(evac_act, 1)

            def dsa_hook(n):
                if n % 2 == 1 and n != LN_SILU_AT - 1:
                    for u in ((n - 2, n) if n == LN_SILU_AT + 1 else (n,)):
                        filler = (u - 2) // 2
                        if 0 <= filler < 2 * (HEADS - 2):
                            empty_qk(4 + filler)
                        elif filler >= 0:
                            round_to(CH["ATT"] + 4 + filler)
                if LN_MEAN_AT < n <= LN_MEAN_AT + KB // 2:
                    for k in range(2 * (n - LN_MEAN_AT) - 2, 2 * (n - LN_MEAN_AT)):
                        act.wait_ge(sems["centred"], k + 1)
                        A.activation(ln_sq[:, k, :], conv_io[:, k, :], ACT.Square).then_inc(sems["ln_squared"], 1)
                if n == LN_VAR_AT + 1:
                    act.wait_ge(sems["ln_sum"], 2)
                    A.activation(ln_rstd[:, :], ps[3][:, :], ACT.Sqrt, bias=eps, scale=1.0 / D
                                 ).then_inc(sems["ln_root"], 1)
                if n == LN_SILU_AT:
                    for k in range(KB):
                        act.wait_ge(sems["ln_scaled"], k + 1)
                        A.activation(conv_io[:, k, :], conv_io[:, k, :], ACT.Silu, bias=col("conv_ln_b", k)
                                     ).then_inc(sems["ln_silu"], 1)
                if 0 <= n - LN_SPLIT_AT < KB:
                    k = n - LN_SPLIT_AT
                    act.wait_ge(sems["ln_silu"], k + 1)
                    A.copy(b_hi[:, k, :], conv_io[:, k, :]).then_inc(sems["ln_hi"], 1)

            for n in range(4):
                empty_qk(n)
            attend(DSA_G, HEADS, dsa_hook)
            act.wait_ge(sems["pv_done"], 4 * X_G)
            act.dma_start(res[:, :, :], xT).then_inc(x_again, 16)

            for j in range(CO_BESIDE, KB):
                round_to(CH["CO"] + j)
            for j in range(KB):
                round_to(CH["AO"] + j)
                act.wait_ge(sems["mix_added"], j + 1)
                A.copy(a_hi[:, j, :], gate_c[:, j, :]).then_inc(sems["mix_hi"], 1)

            def residual(e, hset, i, gain, dst_hi, done, src=None, gain_g=None):
                src = res if src is None else src
                act.wait_ge(*done)
                if dst_hi is not None:
                    A.activation(dst_hi[:, i, :], src[:, i, :], ACT.Copy, scale=gain).then_inc(sems["hg_hi"], 1)
                if e == 4 and i >= 2:
                    act.wait_ge(sems["post_summed"], i - 1)
                elif e == 5 and i < 2:
                    act.wait_ge(sems["post_summed"], KB - 1 + i)
                elif KB * e + i >= 2:
                    act.wait_ge(sems["ssq_added"], KB * (e if e < 5 else 4) + i - 1 - (e == 5 or (e, i) == (4, 1)))
                A.activation(sq[:, i % 2, :], src[:, i, :], ACT.Square).then_inc(sems["res_sq"], 1)
                if gain_g is not None:
                    if i >= 1:
                        act.wait_ge(sems["ssqg_added"], i)
                    A.activation(sq_g[:, :], src[:, i, :], ACT.Square, scale=gain_g).then_inc(sems["res_sqg"], 1)

            for j in range(KB):
                round_to(CH["MX"] + j)
                residual(0, 0, j, col("norm_x_g", j), b_hi, (evac_dve, O["MX"] + j + 1 - DVE_FROM))
            round_to(CH["QX"])
            root(2, rstd[:, :], STAT, 1.0 / D)
            round_to(CH["QX"] + 1)

            def x_hook(n):
                if n in (4, 8):
                    round_to(CH["QX"] + 2 + (n - 4) // 4)

            attend(X_G, XH, x_hook)
            for j in range(KB):
                round_to(CH["OX"] + j // 2)
                residual(1, 1, j, col("norm_ffn_g", j), a_hi, (evac_dve, O["OX"] + j + 1 - DVE_FROM))
            root(3, rstd[:, :], STAT, 1.0 / D)

            def ff_group(name, s, g, last=None, beside=None):
                c0, o0 = CH[name], O[name]
                for j in range(2 * KB):
                    if beside is not None:
                        beside(j)
                    n = g * 16 + (c0 + j)
                    if not isinstance(n, int):
                        m = c0 + j + AHEAD
                        round_chunk(g * 16 + m, m % RING, g * 4 + (m // RING + 1))
                    else:
                        round_to(n)
                    if j < KB:
                        f = g * KB + (32 * s + j)
                        act.wait_ge(evac_dve, g * 16 + (o0 + j + 1 - DVE_FROM))
                        if not isinstance(f, int) or f >= 2:
                            if not (s == 0 and j < 2 and not isinstance(f, int)):
                                act.wait_ge(sems["f_ready"], f - 1)
                        A.activation(ff_f[:, j % 2, :], ff_t[:, j % 2, :], ACT.Square).then_inc(sems["f_sq"], 1)
                        act.wait_ge(sems["f_sq"], f + 1)
                        A.copy(b_hi[:, j, :], ff_f[:, j % 2, :]).then_inc(sems["f_hi"], 1)
                    elif last is not None:
                        last(j - KB, g * 16 + (o0 + j))

            def feed_forward(name, s, last, beside=None):
                ff_group(name, s, 0, beside=beside)
                with act.Fori(1, FF_GROUPS - 1) as g:
                    ff_group(name, s, g)
                rounded[0] = CH[name] + 16 * (FF_GROUPS - 1) + AHEAD
                ff_group(name, s, FF_GROUPS - 1, last)

            act.wait_ge(sems["pv_done"], 4 * MLA_G)
            act.dma_start(posi[:, :], pos_in.to_broadcast([P, T])).then_inc(sems["late_landed"], 16)
            act.dma_start(sel[0:ML_HEADS, :], sel_in).then_inc(sems["late_landed"], 16)
            rr = slice(NOPE, NOPE + ROPE)

            def rotary(j):
                if j == KB + 5:
                    act.wait_ge(sems["angles"], 2)
                    A.activation(ropet[:, 1, :], ropet[:, 1, :], ACT.Sin).then_inc(sems["sines"], 1)
                    A.activation(ropet[:, 0, :], ropet[:, 0, :], ACT.Sin).then_inc(sems["sines"], 1)

            feed_forward("FF1", 0, lambda i, o: residual(
                2, 2, i, g2g[:, i:i + 1], a_hi, (evac_dve, o + 1 - DVE_FROM), gain_g=col("norm_final_g", i)),
                rotary)
            round_to(CH["CQ"])
            root(4, rstd[:, :], STAT, 1.0 / D)
            round_to(CH["CQ"] + 1)
            act.wait_ge(sems["mean2"], 1)
            A.activation(sq[:, 0, :], sq[:, 0, :], ACT.Sqrt, bias=eps).then_inc(sems["stat_root"], 1)
            round_to(CH["CKV"])
            for i in range(3):
                act.wait_ge(evac_dve, O["CQ"] + i + 1 - DVE_FROM)
                A.activation(cq_sq[:, i, :], cq[:, i, :], ACT.Square).then_inc(sems["cq_squared"], 1)
                round_to(CH["CQ"] + 1 + i)
            act.wait_ge(evac_dve, O["KR"] + 1 - DVE_FROM)
            g4 = slice(0, ML_HEADS)
            A.activation(gt[g4, 0, :], krT[g4, :], ACT.Identity, bias=col("b_gates_2", 0, p1=ML_HEADS)
                         ).then_inc(sems["gate_step"], 1)
            A.copy(gt[g4, 1, :], krT[32:32 + ML_HEADS, :]).then_inc(sems["gate_step"], 1)
            act.wait_ge(sems["gate_step"], 2)
            A.activation(gt[g4, 2, :], gt[g4, 1, :], ACT.Abs, bias=col("b_gates_2", 1, p1=ML_HEADS)
                         ).then_inc(sems["gate_step"], 1)
            act.wait_ge(sems["gate_step"], 3)
            A.activation(gt[g4, 2, :], gt[g4, 2, :], ACT.Exp, scale=-1.0).then_inc(sems["gate_step"], 1)
            act.wait_ge(sems["gate_step"], 4)
            A.activation(gt[g4, 2, :], gt[g4, 2, :], ACT.Ln, bias=con("misc", 1, ONE_COL, p1=ML_HEADS)
                         ).then_inc(sems["gate_step"], 1)
            A.copy(rot[NOPE:NOPE + ROPE, 1, :], krT[96:128, :]).then_inc(sems["kr_moved"], 1)
            for j in range(4):
                round_to(CH["QK"] + j)
            root(6, cq_rstd[:, 0, :], STAT, 1.0 / (2 * P))
            root(7, cq_rstd[:, 1, :], 5, 1.0 / P)
            for i in range(3):
                act.wait_ge(sems["cn_scaled"], i + 1)
                A.copy(cn_hi[:, i, :], cq[:, i, :]).then_inc(sems["cn_hi_done"], 1)
            for j in range(4):
                round_to(CH["VM"] + j)
                act.wait_ge(sems["ml_conv"], ML_TAPS * (j + 1))
                A.activation(qk_ml[:, j, :], qk_ml[:, j, :], ACT.Silu).then_inc(sems["qk_silu"], 1)
            def open_gate(j):
                act.wait_ge(evac_dve, O["OM"] + j + 1 - DVE_FROM)
                A.activation(ogate[:, j, :], ogate[:, j, :], ACT.Sigmoid).then_inc(sems["o_gated"], 1)

            for j in range(4):
                round_to(CH["OM"] + j)
                if j >= 1:
                    open_gate(j - 1)
            round_to(CH["UQ"])
            open_gate(3)
            for t in range(2):
                c, o = CH["UQ"] + t, O["UQ"] + 4 * t
                round_to(c)
                act.wait_ge(sems["uq_out"], 3 * t + 3)
                A.copy(qh[0:NOPE, 4 * t + 1, :], ps[(o + 2) % RING][NOPE:2 * NOPE, :]).then_inc(sems["q_moved"], 1)
                act.wait_ge(chunk_done, c + 1)
                A.copy(qh[0:NOPE, 4 * t + 3, :], ps[(o + 3) % RING][NOPE:2 * NOPE, :]).then_inc(sems["q_moved"], 1)
                act.wait_ge(sems["rope_q"], t + 1)
                if t == 1:
                    for j in range(4):
                        act.wait_ge(sems["kv_keys_done"], j + 1)
                        A.copy(kh[0:NOPE, 2 * j + 1, :], ps[(O["UKV"] + j) % RING][NOPE:2 * NOPE, :]
                               ).then_inc(sems["kv_odd"], 1)
                for i in range(4):
                    A.copy(qh[rr, 4 * t + i, :], qrot[ROPE * i:ROPE * (i + 1), t, :]).then_inc(sems["q_roped"], 1)
            round_to(CH["UKV"])
            act.wait_ge(sems["gcols_done"], 1)
            A.activation(fcols[:, :, :], gcols[:, 1, :, :], ACT.Exp, scale=-1.0).then_inc(sems["floors_done"], 1)

            def ml_step(h, st):
                if st == 0:
                    act.wait_ge(sems["ml_rows"], h + 1)
                    if h >= 1:
                        act.wait_ge(sems["ml_diag"], TB * h)
                    A.copy(mrow[:, :], ps[3][:, :]).then_inc(sems["ml_mrow"], 1)
                if 2 <= st < 2 + TB:
                    jb = st - 2
                    u = 4 * h + jb
                    act.wait_ge(sems["ml_diag"], TB * (h + 1))
                    if u >= 2:
                        act.wait_ge(sems["ml_sT"], u - 1)
                    g = gcols[:, 0, jb, h:h + 1]
                    m = A.activation(decay[:, u % 2, 0:P], negm_diag[:, jb, :], ACT.Exp, bias=g)
                    if jb < TB - 1:
                        m = A.activation(decay[:, u % 2, P:T - jb * P], mrow[:, (jb + 1) * P:T], ACT.Exp,
                                         bias=g, scale=-1.0)
                    m.then_inc(sems["ml_decay"], 1)
                if st == 7:
                    act.wait_ge(sems["ml_out"], 4 * (h + 1))
                    if h >= 1:
                        act.wait_ge(sems["ml_sum"], h)
                    A.activation(ml_square[:, :], ps[0][:, :], ACT.Square).then_inc(sems["ml_sq"], 1)
                if st == 8:
                    act.wait_ge(sems["ml_var"], h + 1)
                    A.activation(mcol[:, 3, :], mcol[:, 2, :], ACT.Sqrt).then_inc(sems["ml_root"], 1)
                if st == 11:
                    act.wait_ge(sems["ml_gated"], h + 1)
                    A.copy(a_hi[:, h, :], hml[:, h % 2, :]).then_inc(sems["ml_hi"], 1)

            def ml_hook(n):
                for h in range(ML_HEADS):
                    ml_step(h, n + ML_LEAD - ML_EVERY * h)
                if n == 4:
                    round_to(CH["UKV"] + 1)

            for n in range(-ML_LEAD, 0):
                ml_hook(n)
            attend(MLA_G, MLA_HEADS, after=ml_hook)
            for n in range(4 * MLA_HEADS, ML_END):
                ml_hook(n)
            for j in range(KB):
                round_to(CH["WO"] + j)
                if j < KB - 1:
                    residual(3, None, j, None, None, (evac_dve, O["WO"] + j + 1 - DVE_FROM), src=mixed)
                else:
                    act.wait_ge(chunk_done, CH["WO"] + j + 1)
                    act.wait_ge(sems["ssq_added"], 4 * KB - 2)
                    A.activation(sq[:, j % 2, :], ps[(O["WO"] + j) % RING][:, :], ACT.Square).then_inc(sems["res_sq"], 1)
            root(8, ncol[:, :], STAT, 1.0 / D, TB)
            for j in range(KB):
                residual(4, 3, j, col("norm_pre_mlp_2", j), a_hi,
                         (sems["post_added"], j) if j else (sems["post_first"], 1))
            root(9, rstd[:, :], STAT, 1.0 / D, sums=(sems["post_summed"], KB))
            feed_forward("FF2", 1, lambda i, o: residual(
                5, None, i, None, None, (evac_dve, o + 1 - DVE_FROM), src=ffy))
            root(10, ncol[:, :], STAT, 1.0 / D, TB)

        @block.vector
        def _(dve):
            V = nc.vector

            def ps_of(o):
                return ps[o % RING][:, :]

            def inverse(n, t):
                dve.wait_ge(sems["stat_root"], n + 1)
                V.reciprocal(t, t).then_inc(sems["rstd_ready"], 1)
                dve.wait_ge(sems["rstd_ready"], n + 1)

            def spread_columns(c, dst, done):
                for tb in range(TB):
                    m = V.tensor_scalar(dst[:, tb, :], ident, c[:, tb:tb + 1], None, ALU.mult)
                m.then_inc(done, 1)

            def token_scales(n, count):
                inverse(n, ncol[:, :])
                spread_columns(ncol, spread, sems["spread_done"])
                dve.wait_ge(sems["scales_ready"], count)

            def out_lo(G):
                o, hi, lo = out_of(G)
                dve.wait_ge(sems["o_hi"], G + 1)
                V.tensor_tensor(lo, o, hi.bitcast(F32), ALU.subtract).then_inc(sems["o_ready"], 1)

            def attend(G0, n_heads, hook=None):
                n_units = 4 * n_heads

                def mask(n):
                    U, G, qb = 4 * G0 + n, G0 + n // 4, n % 4
                    b = U % 2
                    dve.wait_ge(sems["s_ready"], U + 1)
                    if U >= 2:
                        dve.wait_ge(sems["p_ready"], U - 1)
                    r = slice(0, keys_of(G, qb))
                    o = ps[4 + b][:, r]
                    V.tensor_tensor_reduce(o, o, bias_of(G, qb), -scale_of(G), -TAKEN,
                                           ALU.add, ALU.min, negmax[:, b:b + 1]).then_inc(sems["s_masked"], 1)

                def normalise(n):
                    U, G, qb = 4 * G0 + n, G0 + n // 4, n % 4
                    b = U % 2
                    dve.wait_ge(sems["p_ready"], U + 1)
                    p = probs[:, b, 0:keys_of(G, qb)]
                    V.reciprocal(rowinv[:, b:b + 1], rowsum[:, b:b + 1]).then_inc(sems["p_inv"], 1)
                    dve.wait_ge(sems["p_inv"], U + 1)
                    V.tensor_scalar(p, p, rowinv[:, b:b + 1], None, ALU.mult).then_inc(sems["p_scaled"], 1)

                mask(0)
                mask(1)
                for n in range(n_units):
                    normalise(n)
                    if n + 2 < n_units:
                        mask(n + 2)
                    if hook is not None:
                        hook(n)
                    if n % 4 == 0 and n >= 4:
                        out_lo(G0 + n // 4 - 1)
                out_lo(G0 + n_heads - 1)

            def split_x(k):
                dve.wait_ge(sems["start_hi"], KB + k + 1)
                V.tensor_tensor(a_lo[:, k, :], res[:, k, :], a_hi[:, k, :].bitcast(F32), ALU.subtract
                                ).then_inc(sems["start_ready"], 1)

            dve.wait_ge(consts_landed, 32)
            V.tensor_tensor(g2g[:, :], col("norm_final_g", 0, KB), col("norm_pre_mix_2", 0, KB), ALU.mult
                            ).then_inc(sems["gains_ready"], 1)
            for k in range(KB):
                dve.wait_ge(sems["start_hi"], k + 1)
                V.scalar_tensor_tensor(out=mem_lo[:, k, :], in0=mem_raw[:, k, :], scalar=col("norm_mem_g", k),
                                       in1=mem_hi[:, k, :].bitcast(F32), op0=ALU.mult, op1=ALU.subtract
                                       ).then_inc(sems["start_ready"], 1)
            for k in range(1, KB):
                dve.wait_ge(sems["squares"], k + 1)
                if k >= 2:
                    dve.wait_ge(sems["squares_added"], k - 1)
                V.tensor_tensor(x_sq[:, 0, :], x_sq[:, 0, :], x_sq[:, k, :], ALU.add).then_inc(sems["squares_added"], 1)
            token_scales(0, 1)
            for k in range(KB):
                V.scalar_tensor_tensor(out=res[:, k, :], in0=res[:, k, :], scalar=col("norm_mix_g", k),
                                       in1=ps[5][:, :], op0=ALU.mult, op1=ALU.mult).then_inc(sems["start_scaled"], 1)
                if k >= 1:
                    split_x(k - 1)
            split_x(KB - 1)
            low, high = slice(0, IDX_DIM), slice(IDX_DIM, 2 * IDX_DIM)

            def split_indexer(j):
                dve.wait_ge(evac_act, O["QI"] + j + 1)
                bank = ps_of(O["QI"] + j)
                for n, (own, other) in enumerate(((low, high), (high, low))):
                    if j < 4:
                        V.tensor_tensor(qi_parts[other, 2 * j + n, :], bank[own, :],
                                        qi_parts[own, 2 * j + n, :].bitcast(F32), ALU.subtract
                                        ).then_inc(sems["qi_split"], 1)
                    else:
                        V.tensor_tensor(ki_lo[own, :], bank[low, :], ki_hi[low, :].bitcast(F32), ALU.subtract
                                        ).then_inc(sems["ki_split"], 1)

            split_indexer(0)
            V.tensor_tensor(mem_sq[:, :, :], mem_raw[:, :, :], mem_raw[:, :, :], ALU.mult).then_inc(sems["mem_squared"], 1)
            dve.wait_ge(sems["mem_squared"], 1)
            for n, half in enumerate((4, 2, 1)):
                V.tensor_tensor(mem_sq[:, 0:half, :], mem_sq[:, 0:half, :], mem_sq[:, half:2 * half, :], ALU.add
                                ).then_inc(sems["mem_added"], 1)
                dve.wait_ge(sems["mem_added"], n + 1)
            for j in range(1, 5):
                split_indexer(j)
            dve.wait_ge(sems["wi_turned"], 1)
            V.tensor_copy(wiT[:, :, :], ps[5][:, 0:TB * IDX_HEADS].rearrange("p (t h) -> p t h", t=TB)
                          ).then_inc(sems["wi_copied"], 1)
            dve.wait_ge(sems["wi_copied"], 1)
            for n in range(3 * IDX_HEADS):
                qb, h = 1 + n // IDX_HEADS, n % IDX_HEADS
                s, r, w = score[:, qb, 0:(qb + 1) * P], relu[:, n % 2, 0:(qb + 1) * P], wiT[:, qb, h:h + 1]
                dve.wait_ge(sems["relu_ready"], n + 1)
                if h == 0:
                    V.tensor_scalar(s, r, w, None, ALU.mult).then_inc(sems["score_added"], 1)
                else:
                    dve.wait_ge(sems["score_added"], n)
                    V.scalar_tensor_tensor(out=s, in0=r, scalar=w, in1=s, op0=ALU.mult, op1=ALU.add
                                           ).then_inc(sems["score_added"], 1)
            for qb in range(1, TB):
                dve.wait_ge(sems["score_added"], 3 * IDX_HEADS)
                s = score[:, qb, qb * P:(qb + 1) * P]
                V.tensor_tensor(s, s, con("bias", P, T - P), ALU.add).then_inc(sems["score_masked"], 1)
            steps = 0
            dve.wait_ge(sems["score_masked"], TB - 1)
            for _ in range(TOPK // 8):
                for b in range(1, TB):
                    if steps >= 3:
                        dve.wait_ge(sems["topk_step"], steps - 2)
                    V.max(top8[:, b - 1, :], score[:, b, 0:(b + 1) * P]).then_inc(sems["topk_step"], 1)
                    steps += 1
                for b in range(1, TB):
                    dve.wait_ge(sems["topk_step"], steps - 2)
                    s = score[:, b, 0:(b + 1) * P]
                    V.match_replace(s, top8[:, b - 1, :], s, TAKEN).then_inc(sems["topk_step"], 1)
                    steps += 1
            dve.wait_ge(sems["topk_step"], steps)
            for b in range(1, TB):
                s = score[:, b, 0:(b + 1) * P]
                V.tensor_scalar(s, s, TAKEN_BELOW, MASKED, ALU.is_gt, ALU.mult).then_inc(sems["topk_done"], 1)
            dve.wait_ge(sems["pad_zeroed"], 1)
            dve.wait_ge(sems["stat_root"], 2)
            with dve.Fori(0, KB // 2) as r:
                def blk(t, e, a, b):
                    return t[:, bass.ds(2 * r + e, 1), a:b].rearrange("p o n -> p (o n)")

                for e in range(2):
                    dve.wait_ge(evac_act, 4 * r + (O["C"] + 2 * e + 2))
                    u = blk(conv_in, e, PAD, PAD + T)
                    V.tensor_tensor(u, u, blk(conv_io, e, 0, T), ALU.mult).then_inc(sems["gated"], 1)
                for k in range(TAPS):
                    for e in range(2):
                        acc = ps[4 + e][:, :]
                        u = blk(conv_in, e, k, k + T)
                        w = cols[:, bass.ds((2 * r + e) * TAPS + (COL["conv_w"] + k), 1)]
                        if k == 0:
                            dve.wait_ge(sems["gated"], 2 * r + (e + 1))
                            V.tensor_scalar(acc, u, w, cols[:, bass.ds(2 * r + (COL["conv_b"] + e), 1)],
                                            ALU.mult, ALU.add).then_inc(sems["tap_done"], 1)
                            continue
                        dve.wait_ge(sems["tap_done"], 2 * (TAPS - 1) * r + (2 * (k - 1) + e + 1))
                        last = k == TAPS - 1
                        V.scalar_tensor_tensor(out=blk(conv_io, e, 0, T) if last else acc, in0=u, scalar=w,
                                               in1=acc, op0=ALU.mult, op1=ALU.add
                                               ).then_inc(sems["conv_done"] if last else sems["tap_done"], 1)

            def gate_conv(j):
                dve.wait_ge(chunk_done, CH["CO"] + j + 1)
                V.tensor_tensor(gate_c[:, j, :], ps[j % 2][:, :], gate_c[:, j, :], ALU.mult).then_inc(evac_dve, 1)

            def dsa_hook(n):
                beside = (n - 2) // 2 - 2 * (HEADS - 2)
                if n % 2 == 1 and beside >= 0:
                    gate_conv(beside)
                if n == MEM_SCALE_AT:
                    inverse(1, mem_rstd[:, :])
                if n == MEM_SCALE_AT + 1:
                    for h in range(XH):
                        V.tensor_tensor(kxT[:, h, :], kxT[:, h, :], mem_rstd[:, 0:M], ALU.mult
                                        ).then_inc(sems["mem_scaled"], 1)
                if n == MEM_SCALE_AT + 2:
                    for b in range(MB):
                        V.tensor_scalar(vx[:, b, :], vx[:, b, :], mem_rstd[:, M + b:M + b + 1], None, ALU.mult
                                        ).then_inc(sems["mem_scaled"], 1)
                if n < LN_MEAN_AT:
                    for k in range(max(2 * n, 1), 2 * n + 2):
                        if k >= 2:
                            dve.wait_ge(sems["ln_added"], k - 1)
                        dve.wait_ge(sems["conv_done"], KB)
                        V.tensor_tensor(ln_rstd[:, :], conv_io[:, 0, :] if k == 1 else ln_rstd[:, :],
                                        conv_io[:, k, :], ALU.add).then_inc(sems["ln_added"], 1)
                if 0 <= n - LN_MEAN_AT < KB // 2:
                    dve.wait_ge(sems["ln_sum"], 1)
                    for k in range(2 * (n - LN_MEAN_AT), 2 * (n - LN_MEAN_AT) + 2):
                        V.scalar_tensor_tensor(out=conv_io[:, k, :], in0=ps[3][:, :], scalar=-1.0 / D,
                                               in1=conv_io[:, k, :], op0=ALU.mult, op1=ALU.add
                                               ).then_inc(sems["centred"], 1)
                if LN_MEAN_AT < n <= LN_MEAN_AT + KB // 2:
                    for k in range(max(2 * (n - LN_MEAN_AT) - 2, 1), 2 * (n - LN_MEAN_AT)):
                        dve.wait_ge(sems["ln_squared"], k + 1)
                        if k >= 2:
                            dve.wait_ge(sems["ln_added"], KB - 1 + k - 1)
                        V.tensor_tensor(ln_rstd[:, :], ln_sq[:, 0, :] if k == 1 else ln_rstd[:, :],
                                        ln_sq[:, k, :], ALU.add).then_inc(sems["ln_added"], 1)
                if n in (LN_VAR_AT + 1, LN_VAR_AT + 2):
                    dve.wait_ge(sems["ln_root"], 1)
                    half = ln_rstd[:, (n - LN_VAR_AT - 1) * (T // 2):(n - LN_VAR_AT) * (T // 2)]
                    V.reciprocal(half, half).then_inc(sems["ln_inv"], 1)
                if 0 <= n - LN_SCALE_AT < KB // 2:
                    dve.wait_ge(sems["ln_inv"], 2)
                    for k in range(2 * (n - LN_SCALE_AT), 2 * (n - LN_SCALE_AT) + 2):
                        V.scalar_tensor_tensor(out=conv_io[:, k, :], in0=conv_io[:, k, :],
                                               scalar=col("conv_ln_g", k), in1=ln_rstd[:, :],
                                               op0=ALU.mult, op1=ALU.mult).then_inc(sems["ln_scaled"], 1)
                if 0 <= n - LN_SPLIT_AT < KB:
                    k = n - LN_SPLIT_AT
                    dve.wait_ge(sems["ln_hi"], k + 1)
                    V.tensor_tensor(b_lo[:, k, :], conv_io[:, k, :], b_hi[:, k, :].bitcast(F32), ALU.subtract
                                    ).then_inc(sems["convact_ready"], 1)

            attend(DSA_G, HEADS, dsa_hook)
            for j in range(CO_BESIDE, KB):
                gate_conv(j)
            for j in range(KB):
                dve.wait_ge(chunk_done, CH["AO"] + j + 1)
                V.tensor_tensor(gate_a[:, j, :], ps[(O["AO"] + j) % RING][:, :], gate_a[:, j, :], ALU.mult
                                ).then_inc(evac_dve, 1)
                dve.wait_ge(evac_dve, O["AO"] + j + 1 - DVE_FROM)
                V.tensor_tensor(gate_c[:, j, :], gate_c[:, j, :], gate_a[:, j, :], ALU.add).then_inc(sems["mix_added"], 1)
                dve.wait_ge(sems["mix_hi"], j + 1)
                V.tensor_tensor(a_lo[:, j, :], gate_c[:, j, :], a_hi[:, j, :].bitcast(F32), ALU.subtract
                                ).then_inc(sems["mix_ready"], 1)

            def add_square(e, i):
                if e >= 3 and i == KB - 1:
                    return
                n = KB * (e if e < 5 else 4) + i - (e == 5)
                dve.wait_ge(sems["res_sq"], KB * e + i + 1)
                if i == 0:
                    V.tensor_copy(ssq[:, :], sq[:, 0, :]).then_inc(sems["ssq_added"], 1)
                else:
                    dve.wait_ge(sems["ssq_added"], n)
                    V.tensor_tensor(ssq[:, :], ssq[:, :], sq[:, i % 2, :], ALU.add).then_inc(sems["ssq_added"], 1)

            def split_residual(hset, i, gain, hi, lo):
                dve.wait_ge(sems["hg_hi"], KB * (min(hset, 3)) + i + 1)
                V.scalar_tensor_tensor(out=lo[:, i, :], in0=res[:, i, :], scalar=gain,
                                       in1=hi[:, i, :].bitcast(F32), op0=ALU.mult, op1=ALU.subtract
                                       ).then_inc(sems["hg_ready"], 1)

            def accumulate(o, t, i, own=True):
                if own:
                    dve.wait_ge(evac_dve, o - DVE_FROM)
                V.tensor_tensor(t[:, i, :], ps_of(o), t[:, i, :], ALU.add).then_inc(evac_dve, 1)

            dve.wait_ge(x_again, 16)
            for j in range(KB):
                dve.wait_ge(chunk_done, CH["MX"] + j + 1)
                accumulate(O["MX"] + j, res, j, False)
                split_residual(0, j, col("norm_x_g", j), b_hi, b_lo)
                add_square(0, j)
            inverse(2, rstd[:, :])

            def x_queries(h):
                dve.wait_ge(chunk_done, CH["QX"] + h + 1)
                V.tensor_tensor(qxT[:, h, :], ps[(3, 0, 1, 3)[h]][:, :], rstd[:, :], ALU.mult).then_inc(evac_dve, 1)

            def x_hook(n):
                if n % 4 == 1 and n // 4 + 1 < XH:
                    x_queries(n // 4 + 1)

            x_queries(0)
            attend(X_G, XH, x_hook)
            for j in range(KB):
                if j % 2 == 0:
                    dve.wait_ge(sems["ox_first"], j // 2 + 1)
                else:
                    dve.wait_ge(chunk_done, CH["OX"] + j // 2 + 1)
                accumulate(O["OX"] + j, res, j)
                split_residual(1, j, col("norm_ffn_g", j), a_hi, a_lo)
                add_square(1, j)
            inverse(3, rstd[:, :])

            def ff_group(name, s, g, dst, last=None, beside=None):
                c0, o0 = CH[name], O[name]
                for j in range(2 * KB):
                    if beside is not None:
                        beside(j)
                    dve.wait_ge(chunk_done, g * 16 + (c0 + j + 1))
                    o = g * 16 + (o0 + j)
                    bank = ps[(o0 + j) % RING][:, :]
                    if j < KB:
                        f = g * KB + (32 * s + j)
                        if not isinstance(f, int) or f >= 2:
                            if not (s == 0 and j < 2 and not isinstance(f, int)):
                                dve.wait_ge(sems["f_sq"], f - 1)
                        V.scalar_tensor_tensor(out=ff_t[:, j % 2, :], in0=bank, scalar=0.0, in1=rstd[:, :],
                                               op0=ALU.max, op1=ALU.mult).then_inc(evac_dve, 1)
                        dve.wait_ge(sems["f_hi"], f + 1)
                        V.tensor_tensor(b_lo[:, j, :], ff_f[:, j % 2, :], b_hi[:, j, :].bitcast(F32), ALU.subtract
                                        ).then_inc(sems["f_ready"], 1)
                    else:
                        i = j - KB
                        if s == 1 and isinstance(g, int) and g == 0:
                            V.tensor_copy(dst[:, i, :], bank).then_inc(evac_dve, 1)
                        else:
                            dve.wait_ge(evac_dve, g * 16 + (o0 + j - DVE_FROM))
                            V.tensor_tensor(dst[:, i, :], bank, dst[:, i, :], ALU.add).then_inc(evac_dve, 1)
                        if last is not None:
                            last(i)

            def feed_forward(name, s, dst, last, beside=None):
                ff_group(name, s, 0, dst, beside=beside)
                with dve.Fori(1, FF_GROUPS - 1) as g:
                    ff_group(name, s, g, dst)
                ff_group(name, s, FF_GROUPS - 1, dst, last)

            def last_ff1(i):
                split_residual(2, i, g2g[:, i:i + 1], a_hi, a_lo)
                add_square(2, i)
                dve.wait_ge(sems["res_sqg"], i + 1)
                if i == 0:
                    V.tensor_copy(ssq_g[:, :], sq_g[:, :]).then_inc(sems["ssqg_added"], 1)
                else:
                    dve.wait_ge(sems["ssqg_added"], i)
                    V.tensor_tensor(ssq_g[:, :], ssq_g[:, :], sq_g[:, :], ALU.add).then_inc(sems["ssqg_added"], 1)

            rr = slice(NOPE, NOPE + ROPE)
            ang, kq = angle[:, 0, :], angle[:, 1, :]
            cosT, sinT = ropet[:, 0, :], ropet[:, 1, :]

            def stepwise(ins, n):
                ins.then_inc(sems["rope_step"], 1)
                dve.wait_ge(sems["rope_step"], n)

            def rotary(j):
                if j == KB:
                    dve.wait_ge(sems["late_landed"], 32)
                    stepwise(V.tensor_copy(ang, posi[:, :]), 1)
                    stepwise(V.tensor_scalar(ang, ang, con("misc", 1, INV_COL), None, ALU.mult), 2)
                if KB < j < KB + 3:
                    dst, turn_off, off = ((sinT, 0.0, 0.0), (cosT, 0.25, float(np.pi / 2)))[j - KB - 1]
                    n = 2 + 6 * (j - KB - 1)
                    stepwise(V.tensor_scalar(kq, ang, 1.0 / TWO_PI, turn_off, ALU.mult, ALU.add), n + 1)
                    stepwise(V.tensor_scalar(kq, kq, ROUND, ROUND, ALU.add, ALU.subtract), n + 2)
                    src = ang
                    for i, part in enumerate((PI_HI, PI_MID, PI_LO)):
                        stepwise(V.scalar_tensor_tensor(out=dst, in0=kq, scalar=-part, in1=src, op0=ALU.mult,
                                                        op1=ALU.add), n + 3 + i)
                        src = dst
                    stepwise(V.tensor_scalar(dst, dst, off, PI_SAFE, ALU.add, ALU.min), n + 6)
                    V.tensor_scalar(dst, dst, -PI_SAFE, None, ALU.max).then_inc(sems["angles"], 1)
                if j == 2 * KB - 1:
                    dve.wait_ge(sems["sines"], 2)
                    V.tensor_scalar(sinT, sinT, con("misc", 1, SIGN_COL), None, ALU.mult
                                    ).then_inc(sems["rope_step"], 1)

            dve.wait_ge(sems["gains_ready"], 1)
            feed_forward("FF1", 0, res, last_ff1, rotary)
            rt = ssq
            inverse(4, rstd[:, :])
            V.tensor_tensor(sq[:, 0, :], rstd[:, :], rstd[:, :], ALU.mult).then_inc(sems["norm2"], 1)
            dve.wait_ge(sems["norm2"], 1)
            dve.wait_ge(sems["stat_ready"], 6)
            V.scalar_tensor_tensor(out=sq[:, 0, :], in0=ps[5][:, :], scalar=1.0 / D, in1=sq[:, 0, :],
                                   op0=ALU.mult, op1=ALU.mult).then_inc(sems["mean2"], 1)
            inverse(5, sq[:, 0, :])
            V.tensor_tensor(rt[:, :], sq[:, 0, :], rstd[:, :], ALU.mult).then_inc(sems["rt_done"], 1)
            dve.wait_ge(sems["rt_done"], 1)
            for i in range(2):
                dve.wait_ge(chunk_done, CH["CQ"] + i + 1)
                V.tensor_tensor(cq[:, i, :], ps_of(O["CQ"] + i), rt[:, :], ALU.mult).then_inc(evac_dve, 1)
            dve.wait_ge(chunk_done, CH["CKV"] + 1)
            V.tensor_tensor(cq[:, 2, :], ps_of(O["CKV"]), rt[:, :], ALU.mult).then_inc(evac_dve, 1)
            dve.wait_ge(chunk_done, CH["KR"] + 1)
            V.tensor_tensor(krT[:, :], ps_of(O["KR"]), rt[:, :], ALU.mult).then_inc(evac_dve, 1)
            dve.wait_ge(sems["rt_turned"], 1)
            V.tensor_copy(rtcol[:, :], ps[6][:, 0:T:P]).then_inc(sems["rt_cols"], 1)
            V.memset(qk_in[:, :, 0:ML_TAPS - 1], 0.0).then_inc(sems["qk_pad"], 1)
            dve.wait_ge(sems["qk_pad"], 1)
            taps = 0
            for j in range(4):
                dve.wait_ge(chunk_done, CH["QK"] + j + 1)
                V.tensor_tensor(qk_in[:, j, ML_TAPS - 1:], ps_of(O["QK"] + j), rt[:, :], ALU.mult
                                ).then_inc(evac_dve, 1)
                dve.wait_ge(evac_dve, O["QK"] + j + 1 - DVE_FROM)
                for k in range(ML_TAPS):
                    x, w = qk_in[:, j, k:k + T], col("conv_w_2", j * ML_TAPS + k)
                    if k == 0:
                        V.tensor_scalar(qk_ml[:, j, :], x, w, col("conv_b_2", j), ALU.mult, ALU.add
                                        ).then_inc(sems["ml_conv"], 1)
                    else:
                        dve.wait_ge(sems["ml_conv"], taps)
                        V.scalar_tensor_tensor(out=qk_ml[:, j, :], in0=x, scalar=w, in1=qk_ml[:, j, :],
                                               op0=ALU.mult, op1=ALU.add).then_inc(sems["ml_conv"], 1)
                    taps += 1
            inverse(6, cq_rstd[:, 0, :])
            inverse(7, cq_rstd[:, 1, :])
            for i in range(3):
                g = col("q_norm_2", i) if i < 2 else col("kv_norm_2")
                V.scalar_tensor_tensor(out=cq[:, i, :], in0=cq[:, i, :], scalar=g, in1=cq_rstd[:, i // 2, :],
                                       op0=ALU.mult, op1=ALU.mult).then_inc(sems["cn_scaled"], 1)
            g4 = slice(0, ML_HEADS)

            def chained(ins, n):
                ins.then_inc(sems["row_step"], 1)
                dve.wait_ge(sems["row_step"], n)

            chained(V.memset(gt[g4, 5, :], 0.0), 1)
            dve.wait_ge(sems["gate_step"], 5)
            chained(V.tensor_scalar(gt[g4, 1, :], gt[g4, 1, :], col("b_gates_2", 1, p1=ML_HEADS), 0.0,
                                    ALU.add, ALU.min), 2)
            chained(V.tensor_tensor(gt[g4, 1, :], gt[g4, 1, :], gt[g4, 2, :], ALU.subtract), 3)
            chained(V.tensor_tensor_scan(gt[g4, 3, :], gt[g4, 1, :], gt[g4, 5, :], 0.0, ALU.add, ALU.add), 4)
            chained(V.tensor_tensor(gt[g4, 0, :], gt[g4, 0, :], gt[g4, 3, :], ALU.subtract), 5)
            chained(V.tensor_tensor_scan(gt[g4, 4, :], gt[g4, 5, :], gt[g4, 0, :], 0.0, ALU.add, ALU.max), 6)
            V.tensor_tensor(gt[g4, 3, :], gt[g4, 3, :], gt[g4, 4, :], ALU.add).then_inc(sems["gates_done"], 1)
            for i in range(3):
                dve.wait_ge(sems["cn_hi_done"], i + 1)
                V.tensor_tensor(cn_lo[:, i, :], cq[:, i, :], cn_hi[:, i, :].bitcast(F32), ALU.subtract
                                ).then_inc(sems["cn_ready"], 1)
            dve.wait_ge(sems["rt_cols"], 1)
            for b in range(TB):
                dve.wait_ge(chunk_done, CH["VM"] + 4)
                V.tensor_scalar(v_ml[:, b, :], ps_of(O["VM"] + b), rtcol[:, b:b + 1], None, ALU.mult
                                ).then_inc(evac_dve, 1)
            dve.wait_ge(sems["kr_moved"], 1)
            dve.wait_ge(sems["rope_step"], 15)
            chained(V.tensor_tensor(rot[rr, 0, :], krT[rr, :], cosT[rr, :], ALU.mult), 7)
            chained(V.tensor_tensor(rot[rr, 1, :], rot[rr, 1, :], sinT[rr, :], ALU.mult), 8)
            chained(V.tensor_tensor(krT[rr, :], rot[rr, 0, :], rot[rr, 1, :], ALU.add), 9)
            for j in range(4):
                dve.wait_ge(chunk_done, CH["OM"] + j + 1)
                V.tensor_tensor(ogate[:, j, :], ps_of(O["OM"] + j), rt[:, :], ALU.mult).then_inc(evac_dve, 1)
            for t in range(2):
                o = O["UQ"] + 4 * t
                for i, table in enumerate((cosT, sinT)):
                    dve.wait_ge(sems["uq_out"], 3 * t + i + 1)
                    if t == 1:
                        dve.wait_ge(sems["rope_q"], 1)
                    V.tensor_tensor(rot[:, i, :], ps_of(o + i), table, ALU.mult).then_inc(evac_dve, 1)
                dve.wait_ge(evac_dve, o + 2 - DVE_FROM)
                V.tensor_tensor(qrot[:, t, :], rot[:, 0, :], rot[:, 1, :], ALU.add).then_inc(sems["rope_q"], 1)
                for i in range(2):
                    dve.wait_ge(sems["q_moved"], 2 * t + i + 1)
                    V.tensor_copy(qh[0:NOPE, 4 * t + 2 * i, :], ps_of(o + 2 + i)[0:NOPE, :]).then_inc(evac_dve, 1)
            V.tensor_copy(kh[rr, 0, :], krT[rr, :]).then_inc(sems["rope_done"], 1)
            for j in range(4):
                dve.wait_ge(sems["kv_odd"], j + 1)
                V.tensor_copy(kh[0:NOPE, 2 * j, :], ps_of(O["UKV"] + j)[0:NOPE, :]).then_inc(evac_dve, 1)
            for j in range(TB):
                if j < TB - 1:
                    dve.wait_ge(sems["kv_values_done"], j + 1)
                else:
                    dve.wait_ge(chunk_done, CH["UKV"] + 1)
                V.tensor_copy(v_mla[:, j, :], ps_of(O["UKV"] + 4 + j)).then_inc(evac_dve, 1)
            dve.wait_ge(sems["gates_turned"], 1)
            V.tensor_copy(gcols[:, :, :, :], ps[7][:, 0:2 * TB * ML_HEADS].rearrange("p (i t h) -> p i t h", i=2, t=TB)
                          ).then_inc(sems["gcols_done"], 1)

            def ml_step(h, st):
                hm = hml[:, h % 2, :]
                if st == 1:
                    dve.wait_ge(sems["ml_mrow"], h + 1)
                    if h >= 1:
                        dve.wait_ge(sems["ml_decay"], TB * h)
                    for b in range(TB):
                        V.scalar_tensor_tensor(out=negm_diag[:, b, :], in0=mrow[:, b * P:(b + 1) * P], scalar=-1.0,
                                               in1=con("maskT", P), op0=ALU.mult, op1=ALU.add
                                               ).then_inc(sems["ml_diag"], 1)
                if 3 <= st < 3 + TB:
                    jb = st - 3
                    u = 4 * h + jb
                    dve.wait_ge(sems["ml_s"], u + 1)
                    dve.wait_ge(sems["ml_decay"], u + 1)
                    if u >= 2:
                        dve.wait_ge(sems["ml_out"], u - 1)
                    w = slice(0, T - jb * P)
                    V.scalar_tensor_tensor(out=sT[:, u % 2, w], in0=ps[3][:, w], scalar=float(ML_QK) ** -0.5,
                                           in1=decay[:, u % 2, w], op0=ALU.mult, op1=ALU.mult
                                           ).then_inc(sems["ml_sT"], 1)
                if st == 7:
                    dve.wait_ge(sems["ml_out"], 4 * (h + 1))
                    dve.wait_ge(sems["floors_done"], 1)
                    for i, sign in enumerate((-1.0, 1.0)):
                        V.scalar_tensor_tensor(out=mcol[:, 0, :], in0=ps[1][:, 0:TB], scalar=sign,
                                               in1=mcol[:, 0, :] if i else fcols[:, :, h],
                                               op0=ALU.mult, op1=ALU.max).then_inc(sems["ml_floor"], 1)
                        dve.wait_ge(sems["ml_floor"], 2 * h + i + 1)
                    V.scalar_tensor_tensor(out=mcol[:, 1, :], in0=mcol[:, 0, :], scalar=EPS, in1=mcol[:, 0, :],
                                           op0=ALU.mult, op1=ALU.mult).then_inc(sems["ml_den"], 1)
                if st == 8:
                    dve.wait_ge(sems["ml_sq"], h + 1)
                    dve.wait_ge(sems["o_gated"], h + 1)
                    if h >= 2:
                        dve.wait_ge(sems["ml_ready"], h - 1)
                    V.scalar_tensor_tensor(out=hm, in0=ps[0][:, :], scalar=col("ml_head_norm_2", h),
                                           in1=ogate[:, h, :], op0=ALU.mult, op1=ALU.mult).then_inc(sems["ml_num"], 1)
                    dve.wait_ge(sems["ml_sum"], h + 1)
                    dve.wait_ge(sems["ml_den"], h + 1)
                    V.scalar_tensor_tensor(out=mcol[:, 2, :], in0=ps[1][:, TB:2 * TB], scalar=1.0 / ML_V,
                                           in1=mcol[:, 1, :], op0=ALU.mult, op1=ALU.add).then_inc(sems["ml_var"], 1)
                if st == 9:
                    dve.wait_ge(sems["ml_root"], h + 1)
                    V.reciprocal(mcol[:, 3, :], mcol[:, 3, :]).then_inc(sems["ml_inv"], 1)
                    dve.wait_ge(sems["ml_inv"], h + 1)
                    spread_columns(mcol[:, 3, :], ml_spread, sems["ml_spread"])
                if st == 10:
                    dve.wait_ge(sems["ml_scale"], h + 1)
                    dve.wait_ge(sems["ml_num"], h + 1)
                    V.tensor_tensor(hm, hm, ps[1][:, :], ALU.mult).then_inc(sems["ml_gated"], 1)

            def ml_hook(n):
                for h in range(ML_HEADS):
                    ml_step(h, n + ML_LEAD - ML_EVERY * h)
                if n >= 0 and n % 4 == 0 and n // 4 + 1 < MLA_HEADS:
                    V.tensor_copy(kh[rr, n // 4 + 1, :], krT[rr, :]).then_inc(sems["rope_done"], 1)

            for n in range(-ML_LEAD, 0):
                ml_hook(n)
            attend(MLA_G, MLA_HEADS, ml_hook)
            for n in range(4 * MLA_HEADS, ML_END):
                ml_hook(n)
            for j in range(KB):
                dve.wait_ge(chunk_done, CH["WO"] + j + 1)
                if j == KB - 1:
                    dve.wait_ge(sems["res_sq"], 4 * KB)
                V.tensor_copy(mixed[:, j, :], ps_of(O["WO"] + j)).then_inc(evac_dve, 1)
                add_square(3, j)
            token_scales(8, 2)
            for j in range(KB):
                V.scalar_tensor_tensor(out=mixed[:, j, :], in0=mixed[:, j, :], scalar=col("norm_post_mix_2", j),
                                       in1=ps[5][:, :], op0=ALU.mult, op1=ALU.mult).then_inc(sems["post_scaled"], 1)
                if j == 0:
                    dve.wait_ge(sems["x2_done"], KB)
                    dve.wait_ge(sems["post_scaled"], 1)
                    V.tensor_tensor(res[:, 0, :], res[:, 0, :], mixed[:, 0, :], ALU.add).then_inc(sems["post_first"], 1)
                if j >= 2:
                    split_residual(3, j - 2, col("norm_pre_mlp_2", j - 2), a_hi, a_lo)
            for j in range(KB - 2, KB):
                split_residual(3, j, col("norm_pre_mlp_2", j), a_hi, a_lo)
            inverse(9, rstd[:, :])
            feed_forward("FF2", 1, ffy, lambda i: add_square(5, i))
            def add_last(j):
                if j not in POOL_ADDS:
                    dve.wait_ge(sems["y_scaled"], j + 1)
                    V.tensor_tensor(y_out[:, j, :], ffy[:, j, :], res[:, j, :], ALU.add).then_inc(sems["y_written"], 1)

            token_scales(10, 3)
            for j in range(KB):
                V.scalar_tensor_tensor(out=ffy[:, j, :], in0=ffy[:, j, :], scalar=col("norm_post_mlp_2", j),
                                       in1=ps[5][:, :], op0=ALU.mult, op1=ALU.mult).then_inc(sems["y_scaled"], 1)
                if j >= 1:
                    add_last(j - 1)
            add_last(KB - 1)


def _columns(v, n):
    return np.ascontiguousarray(np.reshape(v, (n, P)).T)


def _block(w, cols):
    s = w[:, cols]
    return s.reshape(-1, P, s.shape[1]).transpose(1, 0, 2).reshape(P, -1)


def _stream(i):
    w1, w2 = i["w_in"][0], i["w_in_2"][0]
    kv, chunks = i["wx_kv"][0], []

    def blocks(w, n, c0=0):
        chunks.extend(_block(w, slice(c0 + P * j, c0 + P * (j + 1))) for j in range(n))

    def rows(w, c0):
        chunks.extend(_block(w[2 * P * t:2 * P * (t + 1)], slice(c0, c0 + T)) for t in range(4))

    ca, cg, q0, k0, v0 = 0, D, 2 * D, 3 * D, 4 * D
    qi0 = 5 * D
    ki0 = qi0 + IDX_HEADS * IDX_DIM
    wi0 = ki0 + IDX_DIM
    g0 = wi0 + IDX_HEADS
    blocks(kv, 4)
    rows(kv, T)
    blocks(w1, 4, qi0)
    ki = np.zeros((D, P), w1.dtype)
    ki[:, 0:IDX_DIM + IDX_HEADS] = w1[:, ki0:g0]
    blocks(ki, 1)
    for j in range(KB):
        blocks(w1, 1, cg + P * j)
        blocks(w1, 1, ca + P * j)
    blocks(w1, 16, g0)
    rows(w1, v0)
    rows(w1, v0 + T)
    for h in range(HEADS):
        blocks(w1, 1, q0 + P * h)
        blocks(w1, 1, k0 + P * h)
    blocks(i["w_conv_out"][0], KB)
    blocks(i["w_attn_out"][0], KB)
    blocks(i["w_mix_out"][0], KB)
    blocks(i["wx_q"][0], XH)
    wo = i["wx_o"][0]
    for j in range(XH):
        chunks.append(np.concatenate([_block(wo, slice(P * (2 * j + r), P * (2 * j + r + 1))) for r in range(2)], 1))

    def feed_forward(up, down):
        for g in range(FF_GROUPS):
            blocks(up, KB, D * g)
            blocks(down[D * g:D * (g + 1)], KB)

    feed_forward(i["w_ff1"][0], i["w_ff2"][0])
    o0 = 2 * ML_HEADS * ML_QK
    o1 = o0 + ML_HEADS * ML_V
    o2 = o1 + ML_HEADS * ML_V
    o3 = o2 + 2 * ML_HEADS
    o4 = o3 + 2 * P
    o5 = o4 + P
    blocks(w2, 2, o3)
    blocks(w2, 1, o4)
    kr = np.zeros((D, P), w2.dtype)
    kr[:, 0:ML_HEADS] = w2[:, o2:o2 + ML_HEADS]
    kr[:, 32:32 + ML_HEADS] = w2[:, o2 + ML_HEADS:o3]
    kr[:, 64:96] = w2[:, o5:]
    kr[:, 96:112] = w2[:, o5 + ROPE // 2:]
    kr[:, 112:128] = w2[:, o5:o5 + ROPE // 2]
    blocks(kr, 1)
    blocks(w2, 4)
    rows(w2, o0)
    blocks(w2, 4, o1)
    uq = i["w_uq_2"][0]
    per = NOPE + ROPE
    uq = uq.reshape(2 * P, MLA_HEADS, per)
    for h in range(0, MLA_HEADS, 4):
        rotated = uq[:, h:h + 4, NOPE:]
        swapped = np.concatenate([rotated[:, :, ROPE // 2:], rotated[:, :, 0:ROPE // 2]], 2)
        plain = uq[:, h:h + 4, 0:NOPE].reshape(2 * P, 4 * NOPE)
        parts = [rotated.reshape(2 * P, P), swapped.reshape(2 * P, P), plain[:, 0:P], plain[:, P:]]
        chunks.append(np.concatenate([_block(w, slice(0, P)) for w in parts], 1))
    ukv = i["w_ukv_2"][0].reshape(P, MLA_HEADS, NOPE + MLA_V)
    chunks.append(np.concatenate([ukv[:, :, 0:NOPE].reshape(P, -1), ukv[:, :, NOPE:].reshape(P, -1)], 1))
    blocks(i["w_out_2"][0], KB)
    feed_forward(i["w_up_2"][0], i["w_down_2"][0])
    assert len(chunks) == CHUNKS
    return np.stack(chunks)


def _packed(i):
    c = np.zeros((P, NCOLS), np.float32)
    for name, n in COLS:
        if name == "conv_w":
            c[:, COL[name]:COL[name] + n] = i[name][0].reshape(TAPS, KB, P).transpose(2, 1, 0).reshape(P, n)
        elif name == "conv_w_2":
            c[:, COL[name]:COL[name] + n] = i[name][0].reshape(ML_TAPS, 4, P).transpose(2, 1, 0).reshape(P, n)
        elif name == "b_gates_2":
            c[0:ML_HEADS, COL[name]:COL[name] + 2] = i[name][0].reshape(2, ML_HEADS).T
        else:
            c[:, COL[name]:COL[name] + n] = _columns(i[name], n)
    return c


def _constants():
    c = np.zeros((P, NCONST), np.float32)
    c[:, CON["ident"]:CON["ident"] + P] = np.eye(P, dtype=np.float32)
    c[:, CON["ones"]:CON["ones"] + P] = 1.0
    r = np.arange(P)
    later = np.where(r[None, :] > r[:, None], np.float32(MASKED), np.float32(0))
    c[:, CON["bias"] + T - P:CON["bias"] + T] = later
    c[:, CON["maskT"]:CON["maskT"] + P] = later.T
    misc = CON["misc"]
    c[:, misc + EPS_COL] = EPS
    inv = (1.0 / (np.float32(10000.0) ** (np.arange(0, ROPE, 2, dtype=np.float32) / ROPE))).astype(np.float32)
    c[:, misc + INV_COL] = np.tile(inv, P // (ROPE // 2))
    c[:, misc + SIGN_COL] = np.tile(np.repeat([-1.0, 1.0], ROPE // 2), P // ROPE)
    c[:, misc + ONE_COL] = 1.0
    s = np.zeros((ML_HEADS, ML_HEADS * P), np.float32)
    for h in range(ML_HEADS):
        s[h, h * P:(h + 1) * P] = 1.0
    return c, s


def _feature_major(a, n):
    return np.ascontiguousarray(a.reshape(n, KB, P).transpose(2, 1, 0))


def kernel(**inputs):
    import concourse.bacc as bacc
    from concourse.bass_utils import run_bass_kernel_spmd as run

    i = {k: np.asarray(v) for k, v in inputs.items()}
    consts, sel = _constants()
    arrays = {
        "in_stream": _stream(i),
        "in_xT": _feature_major(i["x"], T),
        "in_memT": _feature_major(i["mem"], M),
        "in_cols": _packed(i),
        "in_consts": consts,
        "in_sel": sel,
        "in_positions": np.ascontiguousarray(i["positions_2"].reshape(1, T)),
    }
    nc = bacc.Bacc("TRN2", target_bir_lowering=False, num_devices=1, dynamic_dma_scratch_size=1024)
    args = [nc.dram_tensor(n, a.shape, mybir.dt.from_np(a.dtype), kind="ExternalInput").ap()
            for n, a in arrays.items()]
    out = nc.dram_tensor("out_y", (P, KB, T), F32, kind="ExternalOutput").ap()
    program(nc, *args, out)
    r = run(nc, [arrays], core_ids=[0])
    y = r.results[0]["out_y"]
    return np.ascontiguousarray(y.transpose(2, 1, 0)).reshape(1, T, D)
```
